# Optimizing a Trainium2 kernel written in Bass

```python
import math
import jax, jax.numpy as jnp
from jax import lax
import numpy as np

D_MODEL = 1024
BATCH = 1
SEQ = 256
DEPTH = 1

HEAD_DIM = 64
N_MOBA_HEADS = 8
N_FOX_HEADS = 8
MOBA_WIDTH = N_MOBA_HEADS * HEAD_DIM
FOX_WIDTH = N_FOX_HEADS * HEAD_DIM
MOBA_BLOCK = 256
MOBA_TOPK = 3
Q_CHUNK = 128
ROPE_THETA = 500000.0
ROPE_DIM = HEAD_DIM // 4
D_FF = 11 * D_MODEL // 4
CONV_WIDTH = 3
NORM_EPS = 1e-6
N_BRANCH = 2
NEG_INF = -1e30
IN_SPLITS = (MOBA_WIDTH, MOBA_WIDTH, MOBA_WIDTH, FOX_WIDTH, FOX_WIDTH, FOX_WIDTH, N_FOX_HEADS, N_BRANCH * D_MODEL)
IN_COLS = sum(IN_SPLITS)


def rms_norm(x, g):
    xf = x.astype(jnp.float32)
    y = xf * lax.rsqrt(jnp.mean(xf * xf, axis=-1, keepdims=True) + NORM_EPS)
    return (y * g.astype(jnp.float32)).astype(x.dtype)

def split_heads(t, n_heads):
    b, s, _ = t.shape
    return t.reshape(b, s, n_heads, HEAD_DIM).transpose(0, 2, 1, 3)

def merge_heads(t):
    b, h, s, d = t.shape
    return t.transpose(0, 2, 1, 3).reshape(b, s, h * d)

def partial_rope(x, pos):
    half = ROPE_DIM // 2
    inv_freq = jnp.power(ROPE_THETA, -jnp.arange(half, dtype=jnp.float32) * 2.0 / ROPE_DIM)
    ang = pos.astype(jnp.float32)[:, None] * inv_freq[None, :]
    cos, sin = jnp.cos(ang), jnp.sin(ang)
    xr = x[..., :ROPE_DIM].astype(jnp.float32)
    x1, x2 = xr[..., :half], xr[..., half:]
    rot = jnp.concatenate([x1 * cos - x2 * sin, x2 * cos + x1 * sin], axis=-1).astype(x.dtype)
    return jnp.concatenate([rot, x[..., ROPE_DIM:]], axis=-1)

def moba_attention(q, k, v):
    B, H, S, Dh = q.shape
    nb = -(-S // MOBA_BLOCK)
    pad = nb * MOBA_BLOCK - S
    nqc = S // Q_CHUNK
    scale = Dh ** -0.5
    kp = jnp.pad(k, ((0, 0), (0, 0), (0, pad), (0, 0)))
    vp = jnp.pad(v, ((0, 0), (0, 0), (0, pad), (0, 0)))
    kb = kp.reshape(B, H, nb, MOBA_BLOCK, Dh)
    vb = vp.reshape(B, H, nb, MOBA_BLOCK, Dh)
    k_mean = jnp.mean(kb, axis=3, dtype=jnp.float32)
    gate = jnp.einsum('bhsd,bhnd->bhsn', q.astype(jnp.float32), k_mean)
    pos = jnp.arange(S)
    q_blk = pos // MOBA_BLOCK
    fully_past = jnp.arange(nb)[None, :] < q_blk[:, None]
    gate = jnp.where(fully_past, gate, -jnp.inf)
    k_sel = min(MOBA_TOPK, nb)
    top_val, top_idx = lax.top_k(gate, k_sel)
    top_ok = jnp.isfinite(top_val)
    own = jnp.broadcast_to(q_blk[None, None, :, None], (B, H, S, 1)).astype(top_idx.dtype)
    sel_idx = jnp.concatenate([top_idx, own], axis=-1)
    sel_ok = jnp.concatenate([top_ok, jnp.ones((B, H, S, 1), dtype=bool)], axis=-1)
    ns = k_sel + 1

    def to_chunks(t):
        tail = t.shape[3:]
        t = t.reshape((B, H, nqc, Q_CHUNK) + tail)
        t = jnp.moveaxis(t, 2, 1)
        return t.reshape((B * nqc, H, Q_CHUNK) + tail)

    q_c = to_chunks(q)
    idx_c = to_chunks(sel_idx)
    ok_c = to_chunks(sel_ok)
    b_ids = jnp.repeat(jnp.arange(B), nqc)
    qpos_c = jnp.tile(pos.reshape(nqc, Q_CHUNK), (B, 1))
    head_ix = jnp.arange(H)[:, None, None]
    key_off = jnp.arange(MOBA_BLOCK)

    def step(args):
        b, qi, idx, ok, qp = args
        k_g = kb[b][head_ix, idx]
        v_g = vb[b][head_ix, idx]
        s = jnp.einsum('hcd,hcnld->hcnl', qi, k_g, preferred_element_type=jnp.float32) * scale
        kpos = idx[..., None] * MOBA_BLOCK + key_off
        mask = ok[..., None] & (kpos <= qp[None, :, None, None])
        s = jnp.where(mask, s, NEG_INF)
        p = jax.nn.softmax(s.reshape(H, Q_CHUNK, ns * MOBA_BLOCK), axis=-1)
        p = p.reshape(H, Q_CHUNK, ns, MOBA_BLOCK).astype(v_g.dtype)
        o = jnp.einsum('hcnl,hcnld->hcd', p, v_g, preferred_element_type=jnp.float32)
        return o.astype(qi.dtype)

    out = lax.map(step, (b_ids, q_c, idx_c, ok_c, qpos_c))
    out = out.reshape(B, nqc, H, Q_CHUNK, Dh)
    return jnp.moveaxis(out, 1, 2).reshape(B, H, S, Dh)

def forgetting_attention(q, k, v, log_f):
    B, H, S, Dh = q.shape
    nqc = S // Q_CHUNK
    scale = Dh ** -0.5
    c = jnp.cumsum(log_f, axis=-1)
    pos = jnp.arange(S)
    q_c = jnp.moveaxis(q.reshape(B, H, nqc, Q_CHUNK, Dh), 2, 0)
    c_c = jnp.moveaxis(c.reshape(B, H, nqc, Q_CHUNK), 2, 0)
    qpos_c = pos.reshape(nqc, Q_CHUNK)

    def step(args):
        qi, ci, qp = args
        s = jnp.einsum('bhcd,bhsd->bhcs', qi, k, preferred_element_type=jnp.float32) * scale
        s = s + ci[..., None] - c[:, :, None, :]
        s = jnp.where(pos[None, :] <= qp[:, None], s, NEG_INF)
        p = jax.nn.softmax(s, axis=-1).astype(v.dtype)
        o = jnp.einsum('bhcs,bhsd->bhcd', p, v, preferred_element_type=jnp.float32)
        return o.astype(qi.dtype)

    out = lax.map(step, (q_c, c_c, qpos_c))
    return jnp.moveaxis(out, 0, 2).reshape(B, H, S, Dh)

def causal_depthwise_conv(t, w, bias):
    kern = w.reshape(CONV_WIDTH, 1, w.shape[-1]).astype(t.dtype)
    y = lax.conv_general_dilated(t, kern, window_strides=(1,), padding=[(CONV_WIDTH - 1, 0)],
                                 dimension_numbers=('NWC', 'WIO', 'NWC'),
                                 feature_group_count=t.shape[-1])
    return y + bias.astype(t.dtype)

def first_inputs(seed: int = 0) -> dict:
    key = jax.random.key(seed)
    ks = jax.random.split(key, 18)
    f32 = jnp.float32

    def nrm(k, shape, scale):
        return jax.random.normal(k, shape, f32) * scale

    def gain(k, shape):
        return 1.0 + 0.02 * jax.random.normal(k, shape, f32)

    return {
        "x": nrm(ks[0], (BATCH, SEQ, D_MODEL), 1.0),
        "attn_norm_g": gain(ks[1], (DEPTH, D_MODEL)),
        "w_in": nrm(ks[2], (DEPTH, D_MODEL, IN_COLS), D_MODEL ** -0.5),
        "b_forget": nrm(ks[3], (DEPTH, N_FOX_HEADS), 0.1),
        "b_gate": nrm(ks[4], (DEPTH, N_BRANCH, D_MODEL), 0.1),
        "moba_q_norm_g": gain(ks[5], (DEPTH, HEAD_DIM)),
        "moba_k_norm_g": gain(ks[6], (DEPTH, HEAD_DIM)),
        "fox_q_norm_g": gain(ks[7], (DEPTH, HEAD_DIM)),
        "fox_k_norm_g": gain(ks[8], (DEPTH, HEAD_DIM)),
        "w_branch_moba": nrm(ks[9], (DEPTH, MOBA_WIDTH, D_MODEL), MOBA_WIDTH ** -0.5),
        "w_branch_fox": nrm(ks[10], (DEPTH, FOX_WIDTH, D_MODEL), FOX_WIDTH ** -0.5),
        "w_out": nrm(ks[11], (DEPTH, D_MODEL, D_MODEL), D_MODEL ** -0.5),
        "ffn_norm_g": gain(ks[12], (DEPTH, D_MODEL)),
        "w_ffn_up": nrm(ks[13], (DEPTH, D_MODEL, 2 * D_FF), D_MODEL ** -0.5),
        "ffn_conv_w": nrm(ks[14], (DEPTH, CONV_WIDTH, D_FF), CONV_WIDTH ** -0.5),
        "ffn_conv_b": nrm(ks[15], (DEPTH, D_FF), 0.02),
        "w_ffn_down": nrm(ks[16], (DEPTH, D_FF, D_MODEL), D_FF ** -0.5),
    }

def first_block(x, attn_norm_g, w_in, b_forget, b_gate, moba_q_norm_g, moba_k_norm_g,
              fox_q_norm_g, fox_k_norm_g, w_branch_moba, w_branch_fox, w_out,
              ffn_norm_g, w_ffn_up, ffn_conv_w, ffn_conv_b, w_ffn_down):
    B, S, D = x.shape
    pos = jnp.arange(S)
    bounds = []
    acc = 0
    for w in IN_SPLITS[:-1]:
        acc += w
        bounds.append(acc)
    for l in range(DEPTH):
        h = rms_norm(x, attn_norm_g[l])
        proj = jnp.einsum('bsd,de->bse', h, w_in[l])
        qa, ka, va, qb, kb, vb, f_logit, g_logit = jnp.split(proj, bounds, axis=-1)
        qa = partial_rope(rms_norm(split_heads(qa, N_MOBA_HEADS), moba_q_norm_g[l]), pos)
        ka = partial_rope(rms_norm(split_heads(ka, N_MOBA_HEADS), moba_k_norm_g[l]), pos)
        va = split_heads(va, N_MOBA_HEADS)
        o_a = merge_heads(moba_attention(qa, ka, va))
        qb = rms_norm(split_heads(qb, N_FOX_HEADS), fox_q_norm_g[l])
        kb = rms_norm(split_heads(kb, N_FOX_HEADS), fox_k_norm_g[l])
        vb = split_heads(vb, N_FOX_HEADS)
        log_f = jax.nn.log_sigmoid(f_logit.astype(jnp.float32) + b_forget[l].astype(jnp.float32))
        log_f = log_f.transpose(0, 2, 1)
        o_b = merge_heads(forgetting_attention(qb, kb, vb, log_f))
        br_a = jnp.einsum('bse,ed->bsd', o_a, w_branch_moba[l])
        br_b = jnp.einsum('bse,ed->bsd', o_b, w_branch_fox[l])
        gates = jax.nn.sigmoid(g_logit.astype(jnp.float32).reshape(B, S, N_BRANCH, D)
                               + b_gate[l].astype(jnp.float32)).astype(x.dtype)
        merged = gates[:, :, 0] * br_a + gates[:, :, 1] * br_b
        x = x + jnp.einsum('bsd,de->bse', merged, w_out[l])
        h2 = rms_norm(x, ffn_norm_g[l])
        up = jnp.einsum('bsd,df->bsf', h2, w_ffn_up[l])
        u, g = jnp.split(up, 2, axis=-1)
        g = causal_depthwise_conv(g, ffn_conv_w[l], ffn_conv_b[l])
        x = x + jnp.einsum('bsf,fd->bsd', jax.nn.silu(g) * u, w_ffn_down[l])
    return x


HG_HEADS = 4
HG_DK = 128
HG_DV = 128
HG_WIDTH = HG_HEADS * HG_DV
SA_HEADS = 4
SA_DH = 64
SA_WIDTH = SA_HEADS * SA_DH
MEM_HEADS = 4
MEM_DH = 64
MEM_WIDTH = MEM_HEADS * MEM_DH
MIX_WIDTH = HG_WIDTH + SA_WIDTH + MEM_WIDTH
IDX_HEADS = 8
IDX_DH = 64
TOPK_MAX = 256
N_MEM = 256
D_FF_2 = -(-8 * D_MODEL // (3 * 256)) * 256
CHUNK = 64
Q_BLOCK = 128
EPS = 1e-6
IN_SIZES = (HG_HEADS * HG_DK, HG_HEADS * HG_DK, HG_WIDTH, HG_WIDTH,
            SA_WIDTH, SA_WIDTH, SA_WIDTH,
            IDX_HEADS * IDX_DH, IDX_DH, IDX_HEADS,
            MEM_WIDTH)
IN_WIDTH = sum(IN_SIZES)


f32 = jnp.float32

def rmsnorm(x, gain):
    x32 = x.astype(f32)
    y = x32 * lax.rsqrt(jnp.mean(x32 * x32, axis=-1, keepdims=True) + EPS)
    return (y * gain.astype(f32)).astype(x.dtype)

def split_in(p):
    offs, acc = [], 0
    for s in IN_SIZES[:-1]:
        acc += s
        offs.append(acc)
    return jnp.split(p, offs, axis=-1)

def to_chunks(a, B, N):
    return a.reshape(B, N, CHUNK, a.shape[2], a.shape[3]).transpose(1, 0, 3, 2, 4)

def hgrn2_mix(q, f_logit, i, g, lb, out_gain):
    B, L = q.shape[:2]
    N = L // CHUNK
    lb = lb.reshape(HG_HEADS, HG_DK)
    z = f_logit.astype(f32)
    log_f = jnp.logaddexp(jnp.log(lb), jnp.log1p(-lb) + jax.nn.log_sigmoid(z))
    k = (1.0 - lb) * jax.nn.sigmoid(-z)
    qf = jax.nn.silu(q.astype(f32))
    xs = (to_chunks(qf, B, N), to_chunks(k, B, N),
          to_chunks(i.astype(f32), B, N), to_chunks(log_f, B, N))
    causal = jnp.tril(jnp.ones((CHUNK, CHUNK), dtype=bool))

    def step(S, inp):
        qc, kc, vc, gc = inp
        b = jnp.cumsum(gc, axis=2)
        o_inter = jnp.einsum('bhck,bhkv->bhcv', qc * jnp.exp(b), S)
        diff = b[:, :, :, None, :] - b[:, :, None, :, :]
        decay = jnp.exp(jnp.where(causal[:, :, None], diff, -jnp.inf))
        A = jnp.einsum('bhtk,bhtsk,bhsk->bhts', qc, decay, kc)
        o = o_inter + jnp.einsum('bhts,bhsv->bhtv', A, vc)
        b_last = b[:, :, -1:, :]
        S = jnp.exp(b_last[:, :, 0, :])[..., None] * S + \
            jnp.einsum('bhck,bhcv->bhkv', kc * jnp.exp(b_last - b), vc)
        return S, o

    S0 = jnp.zeros((B, HG_HEADS, HG_DK, HG_DV), f32)
    _, o = lax.scan(step, S0, xs)
    o = o.transpose(1, 0, 3, 2, 4).reshape(B, L, HG_HEADS, HG_DV)
    o = rmsnorm(o, out_gain) * jax.nn.silu(g.astype(f32))
    return o.reshape(B, L, HG_WIDTH).astype(q.dtype)

def dsa_mix(q, k, v, iq, ik, iw, q_gain, k_gain):
    B, L = q.shape[:2]
    topk = min(TOPK_MAX, L // 4)
    nb = L // Q_BLOCK
    q = rmsnorm(q, q_gain).astype(f32)
    k = rmsnorm(k, k_gain).astype(f32)
    v32 = v.astype(f32)
    ik32 = ik.astype(f32)
    iw32 = iw.astype(f32) * (IDX_HEADS ** -0.5 * IDX_DH ** -0.5)
    key_pos = jnp.arange(L)
    bidx = jnp.arange(B)[:, None, None]

    def blockify(a):
        return a.reshape(B, nb, Q_BLOCK, *a.shape[2:]).swapaxes(0, 1)

    def one_block(args):
        blk, qb, iqb, iwb = args
        qpos = blk * Q_BLOCK + jnp.arange(Q_BLOCK)
        s = jnp.einsum('bqhd,bsd->bqhs', iqb.astype(f32), ik32)
        score = jnp.einsum('bqh,bqhs->bqs', iwb, jax.nn.relu(s))
        visible = key_pos[None, :] <= qpos[:, None]
        score = jnp.where(visible[None], score, -jnp.inf)
        _, idx = lax.top_k(score, topk)
        valid = idx <= qpos[None, :, None]
        kg = k[bidx, idx]
        vg = v32[bidx, idx]
        logits = jnp.einsum('bqhd,bqkhd->bhqk', qb, kg) * (SA_DH ** -0.5)
        logits = jnp.where(valid[:, None], logits, -jnp.inf)
        p = jax.nn.softmax(logits, axis=-1)
        return jnp.einsum('bhqk,bqkhd->bqhd', p, vg)

    out = lax.map(one_block, (jnp.arange(nb), blockify(q), blockify(iq), blockify(iw32)))
    return out.swapaxes(0, 1).reshape(B, L, SA_WIDTH).astype(v.dtype)

def mem_mix(qm, mem_n, w_kv, q_gain, k_gain):
    B, L = qm.shape[:2]
    km, vm = jnp.split(mem_n @ w_kv, 2, axis=-1)
    M = mem_n.shape[1]
    km = km.reshape(B, M, MEM_HEADS, MEM_DH)
    vm = vm.reshape(B, M, MEM_HEADS, MEM_DH)
    qm = rmsnorm(qm, q_gain).astype(f32)
    km = rmsnorm(km, k_gain).astype(f32)
    logits = jnp.einsum('bqhd,bmhd->bhqm', qm, km) * (MEM_DH ** -0.5)
    p = jax.nn.softmax(logits, axis=-1)
    out = jnp.einsum('bhqm,bmhd->bqhd', p, vm.astype(f32))
    return out.reshape(B, L, MEM_WIDTH).astype(mem_n.dtype)

def second_inputs(seed: int = 0) -> dict:
    key = jax.random.key(seed)
    ks = jax.random.split(key, 16)
    nrm = jax.random.normal

    def gain(k, n):
        return 1.0 + 0.02 * nrm(k, (DEPTH, n), f32)

    return {
        "x": nrm(ks[0], (BATCH, SEQ, D_MODEL), f32),
        "mem": nrm(ks[1], (BATCH, N_MEM, D_MODEL), f32),
        "w_in": nrm(ks[2], (DEPTH, D_MODEL, IN_WIDTH), f32) * D_MODEL ** -0.5,
        "w_out": nrm(ks[3], (DEPTH, MIX_WIDTH, D_MODEL), f32) * MIX_WIDTH ** -0.5,
        "w_mem_kv": nrm(ks[4], (DEPTH, D_MODEL, 2 * MEM_WIDTH), f32) * D_MODEL ** -0.5,
        "lb_logits": nrm(ks[5], (DEPTH, HG_HEADS * HG_DK), f32),
        "norm_mix": gain(ks[6], D_MODEL),
        "norm_mem": gain(ks[7], D_MODEL),
        "norm_ffn": gain(ks[8], D_MODEL),
        "hg_out_gain": gain(ks[9], HG_DV),
        "sa_q_gain": gain(ks[10], SA_DH),
        "sa_k_gain": gain(ks[11], SA_DH),
        "mem_q_gain": gain(ks[12], MEM_DH),
        "mem_k_gain": gain(ks[13], MEM_DH),
        "w_ffn_in": nrm(ks[14], (DEPTH, D_MODEL, 2 * D_FF_2), f32) * D_MODEL ** -0.5,
        "w_ffn_out": nrm(ks[15], (DEPTH, D_FF_2, D_MODEL), f32) * D_FF_2 ** -0.5,
    }

def second_block(x, mem, w_in, w_out, w_mem_kv, lb_logits, norm_mix, norm_mem, norm_ffn,
              hg_out_gain, sa_q_gain, sa_k_gain, mem_q_gain, mem_k_gain,
              w_ffn_in, w_ffn_out):
    B, L, _ = x.shape
    lb = jnp.cumsum(jax.nn.softmax(lb_logits.astype(f32), axis=0), axis=0)
    lb = lb - lb[0:1]
    for layer in range(DEPTH):
        h = rmsnorm(x, norm_mix[layer])
        hq, hf, hi, hg, sq, sk, sv, iq, ik, iw, mq = split_in(h @ w_in[layer])
        o_hg = hgrn2_mix(hq.reshape(B, L, HG_HEADS, HG_DK), hf.reshape(B, L, HG_HEADS, HG_DK),
                         hi.reshape(B, L, HG_HEADS, HG_DV), hg.reshape(B, L, HG_HEADS, HG_DV),
                         lb[layer], hg_out_gain[layer])
        o_sa = dsa_mix(sq.reshape(B, L, SA_HEADS, SA_DH), sk.reshape(B, L, SA_HEADS, SA_DH),
                       sv.reshape(B, L, SA_HEADS, SA_DH), iq.reshape(B, L, IDX_HEADS, IDX_DH),
                       ik, iw, sa_q_gain[layer], sa_k_gain[layer])
        mem_n = rmsnorm(mem, norm_mem[layer])
        o_mem = mem_mix(mq.reshape(B, L, MEM_HEADS, MEM_DH), mem_n, w_mem_kv[layer],
                        mem_q_gain[layer], mem_k_gain[layer])
        mixed = jnp.concatenate([o_hg, o_sa, o_mem], axis=-1)
        x = x + (mixed @ w_out[layer]).astype(x.dtype)
        h = rmsnorm(x, norm_ffn[layer])
        a, b = jnp.split(h @ w_ffn_in[layer], 2, axis=-1)
        x = x + ((jax.nn.silu(a) * b) @ w_ffn_out[layer]).astype(x.dtype)
    return x


def setup_inputs(seed=0):
    out = dict(first_inputs(seed))
    for name, value in second_inputs(seed + 1).items():
        if name != "x":
            out[name + "_2"] = value
    return out


def reference(
    x, attn_norm_g, w_in, b_forget, b_gate, moba_q_norm_g, moba_k_norm_g, fox_q_norm_g,
    fox_k_norm_g, w_branch_moba, w_branch_fox, w_out, ffn_norm_g, w_ffn_up, ffn_conv_w,
    ffn_conv_b, w_ffn_down, mem_2, w_in_2, w_out_2, w_mem_kv_2, lb_logits_2, norm_mix_2,
    norm_mem_2, norm_ffn_2, hg_out_gain_2, sa_q_gain_2, sa_k_gain_2, mem_q_gain_2, mem_k_gain_2,
    w_ffn_in_2, w_ffn_out_2,
):
    x = first_block(
        x, attn_norm_g, w_in, b_forget, b_gate, moba_q_norm_g, moba_k_norm_g, fox_q_norm_g,
        fox_k_norm_g, w_branch_moba, w_branch_fox, w_out, ffn_norm_g, w_ffn_up, ffn_conv_w,
        ffn_conv_b, w_ffn_down,
    )
    return second_block(
        x, mem_2, w_in_2, w_out_2, w_mem_kv_2, lb_logits_2, norm_mix_2, norm_mem_2, norm_ffn_2,
        hg_out_gain_2, sa_q_gain_2, sa_k_gain_2, mem_q_gain_2, mem_k_gain_2, w_ffn_in_2,
        w_ffn_out_2,
    )


_drawn_inputs = setup_inputs


def setup_inputs(seed=0):
    import zlib

    import numpy as np

    out = dict(_drawn_inputs(seed))
    spreads = {}
    factors = {'attn_norm_g': 3.549,
     'b_gate': 2.778,
     'moba_q_norm_g': 8.0,
     'moba_k_norm_g': 8.0,
     'fox_q_norm_g': 7.358,
     'fox_k_norm_g': 8.0,
     'ffn_norm_g': 3.018,
     'ffn_conv_b': 3.978,
     'norm_mix_2': 3.853,
     'norm_mem_2': 26.456,
     'norm_ffn_2': 13.374,
     'hg_out_gain_2': 24.698,
     'sa_q_gain_2': 193.725,
     'sa_k_gain_2': 182.107,
     'mem_q_gain_2': 27.622,
     'mem_k_gain_2': 34.664}
    for name, (base, spread) in spreads.items():
        noise = np.random.default_rng([zlib.crc32(name.encode()), seed]).standard_normal(out[name].shape)
        drawn = base * np.exp(spread * noise) if base else spread * noise
        out[name] = __import__('jax').numpy.asarray(drawn.astype(out[name].dtype))
    for name, factor in factors.items():
        out[name] = (out[name] * factor).astype(out[name].dtype)
    return out
```

```python
import numpy as np
from contextlib import ExitStack

import concourse.bass as bass
from concourse import mybir
from concourse.alu_op_type import AluOpType as ALU

ACT = mybir.ActivationFunctionType
AX = mybir.AxisListType
F32 = mybir.dt.float32
F32R = mybir.dt.float32r

P = 128
D = 1024
S = 256
T = S // P
DH = 64
DFF = 2816
KT = D // P
FT = DFF // P
CK = 4
CN = 512
RAW, SPLIT = 2, 4
PAIRS = DFF // CN
REST = DFF - PAIRS * CN
LEVELS = 7
EPS = 1e-6
BIG = 1e30
FLOOR = -3e38
TOPK = min(256, S // 4)
IDX_SCALE = float(8 ** -0.5 * 64 ** -0.5)

C_ID = 0
C_CM = C_ID + P
C_T8 = C_CM + 3 * P
C_E8 = C_T8 + P
C_OR = C_E8 + P
C_HC = C_OR + 2 * P
C_HM = C_HC + 9 * P
C_CS = C_HM + 8 * P
C_END = C_CS + T * 16


def constants():
    c = np.zeros((P, C_END), np.float32)
    s, t = np.arange(P)[:, None], np.arange(P)[None, :]
    c[:, C_ID:C_ID + P] = s == t
    c[:, C_CM + P:C_CM + 2 * P] = np.where(t <= s, 0, -BIG)
    c[:, C_CM + 2 * P:C_CM + 3 * P] = np.where(t <= s, 0, -BIG)
    c[:, C_T8:C_T8 + P] = 8.0 * (s <= t)
    c[:, C_E8:C_E8 + P] = 8.0
    c[:, C_OR:C_OR + P] = 1.0
    c[:, C_OR + P:C_OR + 2 * P] = s > t
    c[:, C_HC:C_HC + P] = s > t
    for n in range(LEVELS):
        half = 64 >> n
        mid = t // (2 * half) * (2 * half) + half - 1
        late = t > mid
        c[:, C_HC + (n + 1) * P:C_HC + (n + 2) * P] = np.where(late, (s > mid) & (s <= t), (s > t) & (s <= mid))
        same = s // (2 * half) == t // (2 * half)
        c[:, C_HM + n * P:C_HM + (n + 1) * P] = same & late & (s <= mid)
    c[:, C_HC + 8 * P:C_HC + 9 * P] = s <= t
    c[:, C_HM + 7 * P:C_HM + 8 * P] = s == t
    freq = (500000.0 ** (-np.arange(8) * 2.0 / 16)).astype(np.float32)
    angle = (np.arange(S, dtype=np.float32)[:, None] * freq[None, :]).astype(np.float64)
    for i in range(T):
        c[:, C_CS + 16 * i:C_CS + 16 * i + 8] = np.cos(angle[i * P:(i + 1) * P])
        c[:, C_CS + 16 * i + 8:C_CS + 16 * i + 16] = np.sin(angle[i * P:(i + 1) * P])
    return c


def plan():
    groups, chunks = {}, []

    def add(name, w, col, n, kt, lhs, k0=0):
        g = dict(name=name, w=w, n=n, kt=kt, lhs=lhs, k0=k0, idx=len(groups), first=len(chunks))
        for a in range(0, kt, CK):
            chunks.append(dict(w=w, row=a * P, nk=min(CK, kt - a), col=col, n=n))
        g["last"] = len(chunks) - 1
        groups[name] = g

    add("mkv", "w_mem_kv_2", 0, CN, KT, "o")
    for n, c in (("qa", 0), ("ka", 512), ("va", 1024), ("qb", 1536), ("kb", 2048)):
        add(n, "w_in", c, CN, KT, "h")
    add("f", "w_in", 3072, 8, KT, "h")
    add("vb", "w_in", 2560, CN, KT, "h")
    for n in range(4):
        add(f"gate{n}", "w_in", 3080 + CN * n, CN, KT, "h")
    for c in range(2):
        add(f"bra{c}", "w_branch_moba", CN * c, CN, 4, "o")
        add(f"brb{c}", "w_branch_fox", CN * c, CN, 4, "o", 4)
    for c in range(2):
        add(f"wo1_{c}", "w_out", CN * c, CN, KT, "h")

    def ffn(m, up, down, gcol, ucol):
        add(f"g{m}s", up, gcol + PAIRS * CN, REST, KT, "h")
        add(f"u{m}s", up, ucol + PAIRS * CN, REST, KT, "h")
        for j in range(PAIRS):
            add(f"g{m}_{j}", up, gcol + CN * j, CN, KT, "h")
            add(f"u{m}_{j}", up, ucol + CN * j, CN, KT, "h")
        for c in range(2):
            add(f"d{m}_{c}", down, CN * c, CN, FT, "act")

    ffn(1, "w_ffn_up", "w_ffn_down", DFF, 0)
    for n, c, w in (("iqb", 3072, 328), ("sviq", 2560, 512), ("hf", 512, 512), ("hq", 0, 512), ("sqk", 2048, 512),
                    ("mq", 3400, 256), ("hi", 1024, 512), ("hg", 1536, 512)):
        add(n, "w_in_2", c, w, KT, "h")
    for c in range(2):
        add(f"wo2_{c}", "w_out_2", CN * c, CN, KT, "o2")
    ffn(2, "w_ffn_in_2", "w_ffn_out_2", 0, DFF)
    return groups, chunks


class Count:

    def __init__(self, known, sem):
        self.known, self.now, self.seen, self.sem, self.loop = known, {}, {}, sem, None

    def mark(self, ins, family, step, i=0):
        ins.then_inc(self.sem(family), 1)
        if family.endswith("free"):
            return
        n = self.now[family] = self.now.get(family, 0) + 1
        if (family, step) not in self.seen:
            self.seen[family, step] = [n, 0]
            if self.loop:
                self.loop[1].append((family, step))
        else:
            base, per = self.seen[family, step]
            assert isinstance(i, int) and n == base + per * i, (family, step, n, base, per, i)

    def value(self, family, step, i=0):
        family = family.replace("free", "full")
        if self.known and (family, step) not in self.known:
            raise KeyError((family, step))
        base, per = self.known.get((family, step), (1, 0))
        return base + i * per if per else base

    def at(self, family, step, i=0):
        return self.sem(family), self.value(family, step, i)

    def enter(self):
        self.loop = (dict(self.now), [])

    def leave(self, times):
        was, steps = self.loop
        per = {f: n - was.get(f, 0) for f, n in self.now.items()}
        for f, s in steps:
            self.seen[f, s][1] = per[f]
        for f in self.now:
            self.now[f] = was.get(f, 0) + per[f] * times
        self.loop = None


def program(nc, dram, out, known):
    groups, chunks = plan()
    ctx = ExitStack()
    sems = {}

    def sem(name):
        if name not in sems:
            sems[name] = ctx.enter_context(nc.semaphore("s_" + name.replace(" ", "_")))
        return sems[name]

    cnt = Count(known, sem)
    done, at = cnt.mark, cnt.at

    with ctx:
        def sb(name, shape, dt=F32, where=ctx):
            return where.enter_context(nc.sbuf_tensor("b_" + name, shape, dt))

        raw = sb("raw", [P, RAW, CK, CN])
        whi = sb("whi", [P, SPLIT, CK, CN], F32R)
        wlo = sb("wlo", [P, SPLIT, CK, CN], F32R)
        x = sb("x", [P, T, D])
        hhi = sb("hhi", [P, KT, S], F32R)
        hlo = sb("hlo", [P, KT, S], F32R)
        cst = sb("cst", [P, C_END])
        gain = sb("gain", [P, D])
        xn = sb("xn", [P, T, D])
        mkT = sb("mkT", [P, 2, S])
        mv = sb("mv", [P, T, 256])
        hgain = sb("hgain", [P, 8, DH])
        vec = sb("vec", [4 * FT, P])
        vT = sb("vT", [P, 4 * FT])
        bf = sb("bf", [P, 8])
        ss = sb("ss", [P, 16])
        ms = sb("ms", [P, 16])
        rs = sb("rs", [P, 16])
        nt = sb("nt", [P, 16])
        mx = sb("mx", [P, 24, T])
        nm = sb("nm", [P, 24, T])
        sm = sb("sm", [P, 24, T])
        rc = sb("rc", [P, 24, T])
        lf = sb("lf", [P, T, 8])
        lt = sb("lt", [P, 2, T, 8])
        rp = sb("rp", [P, 4, T, 8, 8])
        og = sb("og", [P, P])

        a1 = ExitStack()
        qT = [sb(f"qT{n}", [P, 4, S], where=a1) for n in range(2)]
        kT = [sb(f"kT{n}", [P, 4, S], where=a1) for n in range(2)]
        va = [sb(f"v{n}", [P, T, 512], where=a1) for n in range(2)]
        gates = sb("gates", [P, T, 2 * D], where=a1)
        ohi = sb("ohi", [P, KT, S], F32R, where=a1)
        olo = sb("olo", [P, KT, S], F32R, where=a1)
        qraw = sb("qraw", [P, T, 512], where=a1)
        sq = sb("sq", [P, T, 512], where=a1)
        L = sb("L", [P, 3, P], where=a1)
        Sm = [sb(f"Sm{n}", [P, 384], where=a1) for n in range(2)]
        PT = sq[:, 0, :]
        memx = gates[:, :, 0:D]
        memg = gates[:, 0, D:2 * D]
        a1.close()

        a2 = ExitStack()
        ahi = sb("ahi", [P, FT, S], F32R, where=a2)
        alo = sb("alo", [P, FT, S], F32R, where=a2)
        y = sb("y", [P, 4, S], where=a2)
        e = sb("e", [P, 4, S], where=a2)
        gtok, utok = xn[:, :, 0:CN], xn[:, :, CN:2 * CN]
        a2.close()

        a3 = ExitStack()
        logf = sb("logf", [P, T, 512], where=a3)
        vh = sb("vh", [P, T, 512], where=a3)
        hqT = sb("hqT", [P, 4, S], where=a3)
        hkT = sb("hkT", [P, 4, S], where=a3)
        big = sb("big", [P, 3 * 1024], where=a3)
        dec = big[:, 0:1024].rearrange("p (l t) -> p l t", t=P)
        qd = big[:, 1024:1920].rearrange("p (l t) -> p l t", t=P)
        kd = big[:, 2048:2944].rearrange("p (l t) -> p l t", t=P)
        iqT = big[:, 0:1024].rearrange("p (l t) -> p l t", t=S)
        sco, work = big[:, 1024:1408], big[:, 1408:1792]
        rel = [big[:, 2048:2432], big[:, 2432:2816]]
        kx, qx = sb("kx", [P, P], where=a3), sb("qx", [P, P], where=a3)
        AT = sb("AT", [P, 3, P], where=a3)
        ikT = sb("ikT", [P, S], where=a3)
        sqkT = sb("sqkT", [P, 4, S], where=a3)
        sv = sb("sv", [P, T, 256], where=a3)
        mqT = sb("mqT", [P, 2, S], where=a3)
        madd = sb("madd", [P, 384], where=a3)
        iw = sb("iw", [P, T, 8], where=a3)
        mx8 = sb("mx8", [P, T, 8], where=a3)
        ikk = sb("ikk", [P, T, P], where=a3)
        tok = [sb("tokA", [P, T, 512], where=a3), sb("tokB", [P, T, 512], where=a3)]
        o2hi = sb("o2hi", [P, KT, S], F32R, where=a3)
        o2lo = sb("o2lo", [P, KT, S], F32R, where=a3)
        Sn, PTn = [big[:, 1024:1536], big[:, 1536:2048]], big[:, 0:512]
        a3.close()

        acc = [[ctx.enter_context(nc.psum_tensor(f"acc{p}{t}", [P, 512], F32)) for t in range(T)] for p in range(2)]
        XX = ctx.enter_context(nc.psum_tensor("banks", [P, 4, 512], F32))
        X = [XX[:, n, :] for n in range(4)]
        ident = cst[:, C_ID:C_ID + P]
        lhs_of = {"h": (hhi, hlo), "o": (ohi, olo), "act": (ahi, alo), "o2": (o2hi, o2lo)}

        def head(j):
            r = slice(64 * (j % 2), 64 * (j % 2) + 64)
            if j < 16:
                n, h = j // 8, j % 8
                return qT[n][r, h // 2, :], kT[n][r, h // 2, :], va[n][:, :, h * DH:h * DH + DH], j * DH, False
            h = (j - 16) % 4
            if j < 20:
                return sqkT[r, h // 2, :], sqkT[r, 2 + h // 2, :], sv[:, :, h * DH:h * DH + DH], 512 + h * DH, False
            return mqT[r, h // 2, :], mkT[r, h // 2, :], mv[:, :, h * DH:h * DH + DH], 768 + h * DH, True

        def probs(j):
            return (Sm if j < 16 else Sn)[j % 2]

        def probsT(j):
            return PT if j < 16 else PTn

        T_BANKS = {"mk": [0], "qa": [2, 3], "ka": [0, 1], "qb": [2, 3], "kb": [0, 1], "sqk": [2, 3], "mq": [0]}
        FIRST_GROUPS = (("qa", "mk"), ("ka", "qa"), ("va", "ka"), ("qb", None), ("kb", "qb"), ("f", "kb"), ("vb", None))

        def unit_with(j):
            return j - 3 if 3 <= j < 16 else None

        def moved(name, t, i=0):
            return sem(f"acc{groups[name]['idx'] % 2}{t} free"), groups[name]["idx"] // 2 + 1 + i

        def leave(ins, name, t, i=0):
            done(ins, f"acc{groups[name]['idx'] % 2}{t} free", name, i)

        def sums(eng, name, t, i=0):
            g = groups[name]
            if t == 0:
                eng.wait_ge(sem("tile 0 summed"), g["idx"] + 1 + 2 * i)
            else:
                eng.wait_ge(sem("chunk used"), g["last"] + 1 + 4 * i)
            return acc[g["idx"] % 2][t]

        STEPS1 = range(20)
        STEPS2 = range(16, 26)

        block = ctx.enter_context(nc.Block())

        @block.tensor
        def _(pe):
            def claim(bank, step, i=0):
                v = cnt.value(f"bank{bank} full", step, i) - 1
                if not isinstance(v, int) or v > 0:
                    pe.wait_ge(sem(f"bank{bank} free"), v)

            def full(ins, bank, step, i=0):
                done(ins, f"bank{bank} full", step, i)

            def gemm(name, c=None, i=0):
                g = groups[name]
                hi, lo = lhs_of[g["lhs"]]
                p, turn, cols = g["idx"] % 2, g["idx"] // 2, g["n"]
                lastc = (g["kt"] - 1) // CK
                for c in range(lastc + 1) if c is None else [c]:
                    n = g["first"] + c
                    nk = min(CK, g["kt"] - c * CK)
                    pe.wait_ge(sem("lo ready"), n + 1 + 4 * i)
                    for t in range(T):
                        if c == 0 and turn > 0:
                            pe.wait_ge(sem(f"acc{p}{t} free"), turn + i)
                        for k in range(nk):
                            kk = g["k0"] + c * CK + k
                            a, b = hi[:, kk, t * P:(t + 1) * P], lo[:, kk, t * P:(t + 1) * P]
                            wh, wl = whi[:, n % SPLIT, k, 0:cols], wlo[:, n % SPLIT, k, 0:cols]
                            o = acc[p][t][:, 0:cols]
                            first, last = c == 0 and k == 0, c == lastc and k == nk - 1
                            nc.tensor.matmul(o, a, wh, start=first, stop=False)
                            nc.tensor.matmul(o, b, wh, start=False, stop=False)
                            mm = nc.tensor.matmul(o, a, wl, start=False, stop=last)
                        if t == T - 1:
                            mm.then_inc(sem("chunk used"), 1)
                        elif c == lastc:
                            mm.then_inc(sem("tile 0 summed"), 1)

            def norm_T(k):
                for t in range(T):
                    pe.wait_ge(*at("tokens scaled", f"{k} {t}"))
                    for b in range(2):
                        claim(2 * t + b, f"{k}T")
                        for c in range(4):
                            mm = nc.tensor.transpose(X[2 * t + b][:, c * P:(c + 1) * P],
                                                     xn[:, t, (4 * b + c) * P:(4 * b + c + 1) * P], ident)
                        full(mm, 2 * t + b, f"{k}T")
                pe.wait_ge(*at("bank3 free", f"{k}T"))

            def tok_T(src, step, ready, banks, blocks=4, first=0):
                pe.wait_ge(*ready)
                for b in range(0, blocks, 2):
                    bank = banks[b // 2]
                    claim(bank, step)
                    for c in range(2):
                        for t in range(T):
                            cols = slice((first + b + c) * P, (first + b + c + 1) * P)
                            mm = nc.tensor.transpose(X[bank][:, c * S + t * P:c * S + (t + 1) * P], src[:, t, cols],
                                                     ident)
                    full(mm, bank, step)

            def attn_scores(j):
                q, k, _, _, whole = head(j)
                b = j % 2
                claim(b, f"scores {j}")
                for start, steps in ((0, ("qa", "ka")), (8, ("qb", "kb")), (16, ("sqk",)), (20, ("mq", "mk"))):
                    if j == start:
                        for step in steps:
                            pe.wait_ge(*at(f"bank{T_BANKS[step][-1]} free", f"{step}T"))
                fox = 8 <= j < 16
                mm = nc.tensor.matmul(X[b][:, 0:S], q[:, P:S], k, start=True, stop=not fox)
                if fox:
                    pe.wait_ge(*at("decay rows", f"{j}"))
                    nc.tensor.matmul(X[b][:, 0:P], L[:, 1, :], cst[:, C_OR + P:C_OR + 2 * P], start=False, stop=False)
                    nc.tensor.matmul(X[b][:, 0:S], L[:, 2, :], cst[:, C_OR:C_OR + 2 * P], start=False, stop=True)
                n = S if whole else P
                mm = nc.tensor.matmul(X[b][:, S:S + n], q[:, 0:P], k[:, 0:n], start=True, stop=not fox)
                if fox:
                    mm = nc.tensor.matmul(X[b][:, S:S + P], L[:, 0, :], cst[:, C_OR + P:C_OR + 2 * P],
                                          start=False, stop=True)
                full(mm, b, f"scores {j}")

            def attn_T(j, unit=None):
                step = f"probs {j} {unit}"
                claim(2, step)
                if j is not None:
                    pe.wait_ge(*(at(f"bank{j % 2} free", f"scores {j}") if head(j)[4] else at("probs ready", f"{j}")))
                    for c in range(4 if head(j)[4] else 3):
                        mm = nc.tensor.transpose(X[2][:, c * P:(c + 1) * P], probs(j)[:, c * P:(c + 1) * P], ident)
                if unit is not None:
                    blk, t = unit // 2, unit % 2
                    pe.wait_ge(*at("bank3 free", f"pv {2 * blk + 1}"))
                    mm = nc.tensor.transpose(X[2][:, 3 * P:4 * P], xn[:, t, blk * P:(blk + 1) * P], ident)
                full(mm, 2, step)

            def attn_pv(j):
                _, _, v, _, whole = head(j)
                pe.wait_ge(*at("bank2 free", f"probs {j} {unit_with(j)}"))
                for start, step in ((0, "va"), (8, "vb"), (16, "sviq"), (20, "mkv")):
                    if j == start:
                        pe.wait_ge(*moved(step, 1))
                claim(3, f"pv {j}")
                pt = probsT(j)
                nc.tensor.matmul(X[3][:, DH:2 * DH], pt[:, 0:P], v[:, 0, :], start=True, stop=False)
                nc.tensor.matmul(X[3][:, DH:2 * DH], pt[:, P:2 * P], v[:, 1, :], start=False, stop=True)
                mm = nc.tensor.matmul(X[3][:, 0:DH], pt[:, 2 * P:3 * P], v[:, 0, :], start=True, stop=not whole)
                if whole:
                    mm = nc.tensor.matmul(X[3][:, 0:DH], pt[:, 3 * P:4 * P], v[:, 1, :], start=False, stop=True)
                full(mm, 3, f"pv {j}")

            def ffn_T(m, which, i=0, short=""):
                src, base = (gtok, 0) if which == "g" else (utok, 2)
                for t in range(T):
                    pe.wait_ge(*moved(f"{which}{m}{short or '_0'}", t, i))
                for b in range(1 if short else 2):
                    step = f"{which}{m}{short}T"
                    claim(base + b, step, i)
                    for c in range(2):
                        for t in range(T):
                            mm = nc.tensor.transpose(X[base + b][:, c * S + t * P:c * S + (t + 1) * P],
                                                     src[:, t, (2 * b + c) * P:(2 * b + c + 1) * P], ident)
                    full(mm, base + b, step, i)

            def ffn(m):
                gemm(f"g{m}s")
                gemm(f"u{m}s", 0)
                ffn_T(m, "g", short="s")
                gemm(f"u{m}s", 1)
                gemm(f"g{m}_0", 0)
                ffn_T(m, "u", short="s")
                gemm(f"g{m}_0", 1)

                def pair(i, last):
                    gemm(f"u{m}_0", 0, i)
                    ffn_T(m, "g", i)
                    gemm(f"u{m}_0", 1, i)
                    if not last:
                        gemm(f"g{m}_0", 0, i + 1)
                    ffn_T(m, "u", i)
                    if not last:
                        gemm(f"g{m}_0", 1, i + 1)

                with pe.Fori(0, PAIRS - 1) as i:
                    cnt.enter()
                    pair(i, False)
                cnt.leave(PAIRS - 1)
                pair(PAIRS - 1, True)
                for c in range((FT + CK - 1) // CK):
                    if c < PAIRS:
                        pe.wait_ge(*at("act split", f"{m}", c))
                    gemm(f"d{m}_0", c)
                gemm(f"d{m}_1")

            pe.wait_ge(sem("consts in"), 16)
            pe.wait_ge(sem("vec in"), 32)
            full(nc.tensor.transpose(X[0][:, 0:4 * FT], vec[:, :], ident[0:4 * FT, 0:4 * FT]), 0, "vecT")

            norm_T("mem")
            gemm("mkv")
            norm_T("x1")
            for name, last in FIRST_GROUPS:
                gemm(name)
                if last:
                    tok_T(qraw, f"{last}T", at("heads roped" if last in ("qa", "ka") else "heads ready", last), T_BANKS[last], 2 if last == "mk" else 4)

            for s in STEPS1:
                if s < 16:
                    attn_scores(s)
                if s % 2 == 0 and s < 16:
                    gemm(f"gate{s // 4}", s // 2 % 2)
                if s >= 1:
                    attn_T(s - 1 if s <= 16 else None, s - 4 if s >= 4 else None)
                if 2 <= s <= 17:
                    attn_pv(s - 2)
            pe.wait_ge(*at("out split", "15"))
            for c in range(2):
                gemm(f"bra{c}")
                gemm(f"brb{c}")
            for c in range(2):
                for t in range(T):
                    bank = 2 * c + t
                    pe.wait_ge(*at("merged", f"{c} {t}"))
                    claim(bank, "mergedT")
                    for b in range(4):
                        mm = nc.tensor.transpose(X[bank][:, b * P:(b + 1) * P],
                                                 xn[:, t, c * CN + b * P:c * CN + (b + 1) * P], ident)
                    full(mm, bank, "mergedT")
            pe.wait_ge(*at("bank3 free", "mergedT"))
            gemm("wo1_0")
            gemm("wo1_1")
            norm_T("ffn1")
            ffn(1)

            norm_T("x2")
            gemm("iqb")
            gemm("sviq")
            gemm("hf")
            tok_T(tok[0], "iqT", moved("sviq", 1), [0, 1])
            claim(2, "ikT")
            for t in range(T):
                mm = nc.tensor.transpose(X[2][:, t * P:(t + 1) * P], ikk[:, t, :], ident)
            full(mm, 2, "ikT")
            pe.wait_ge(*at("bank2 free", "ikT"))
            for h in range(8):
                r = slice(64 * (h % 2), 64 * (h % 2) + 64)
                claim(h % 2, f"index {h}")
                q = iqT[r, h // 2, :]
                nc.tensor.matmul(X[h % 2][:, 0:S], q[:, P:S], ikT[r, :], start=True, stop=True)
                mm = nc.tensor.matmul(X[h % 2][:, S:S + P], q[:, 0:P], ikT[r, 0:P], start=True, stop=True)
                full(mm, h % 2, f"index {h}")
            gemm("hq")
            tok_T(tok[1], "hkT", at("hgrn k", "0"), [2, 3])
            gemm("sqk")
            tok_T(tok[0], "hqT", at("hgrn q", "0"), [0, 1])
            gemm("mq")
            tok_T(tok[0], "sqkT", at("heads ready", "sqk"), T_BANKS["sqk"])
            gemm("hi")
            tok_T(tok[0], "mqT", at("heads ready", "mq"), T_BANKS["mq"], 2)

            def hgrn_decay(u):
                h, t = u // 2, u % 2
                pe.wait_ge(*at("log f", "0"))
                for b in range(2):
                    claim(b, f"decay {u}")
                    c = C_HC + t * P + b * 512
                    full(nc.tensor.matmul(X[b][:, :], logf[:, t, h * P:(h + 1) * P], cst[:, c:c + 512],
                                          start=True, stop=True), b, f"decay {u}")

            def hgrn_pairs(u):
                h, t = u // 2, u % 2
                pe.wait_ge(*at("q decayed", f"{u}"))
                pe.wait_ge(*at("k decayed", f"{u}"))
                for b in range(2):
                    claim(2 + b, f"pairs {u}")
                    for c in range(4):
                        n, ts = 4 * b + c, slice(t * P, (t + 1) * P)
                        k, q = (kd[:, n, :], qd[:, n, :]) if n < LEVELS else (hkT[:, h, ts], hqT[:, h, ts])
                        mm = nc.tensor.matmul(X[2 + b][:, c * P:(c + 1) * P], k, q, start=True, stop=True)
                    full(mm, 2 + b, f"pairs {u}")
                if t == 1:
                    claim(0, f"cross {h}")
                    full(nc.tensor.matmul(X[0][:, 0:P], kx[:, :], qx[:, :], start=True, stop=True), 0, f"cross {h}")

            def hgrn_out(h):
                pe.wait_ge(*moved("hi", 1))
                pe.wait_ge(*at("weights summed", f"{2 * h + 1}"))
                pe.wait_ge(*at("bank0 free", f"cross {h}"))
                claim(1, f"hout {h}")
                v = vh[:, :, h * P:(h + 1) * P]
                nc.tensor.matmul(X[1][:, 0:P], AT[:, 0, :], v[:, 0, :], start=True, stop=True)
                nc.tensor.matmul(X[1][:, P:2 * P], AT[:, 1, :], v[:, 1, :], start=True, stop=False)
                full(nc.tensor.matmul(X[1][:, P:2 * P], AT[:, 2, :], v[:, 0, :], start=False, stop=True), 1, f"hout {h}")

            for s in STEPS2:
                if s < 24:
                    attn_scores(s)
                if s in (17, 20):
                    gemm("hg", (s - 17) // 3)
                if 17 <= s <= 24:
                    attn_T(s - 1)
                if 18 <= s:
                    attn_pv(s - 2)
            hgrn_decay(0)
            for u in range(8):
                hgrn_pairs(u)
                if u < 7:
                    hgrn_decay(u + 1)
                if u % 2 == 1:
                    hgrn_out(u // 2)
            for b, blk in enumerate((4, 6, 0, 2)):
                ready = at("bank3 free", "pv 23") if b < 2 else at("hgrn normed", "0")
                tok_T(xn, f"out {blk}T", ready, [b], 2, blk)
            pe.wait_ge(*at("bank3 free", "out 2T"))
            gemm("wo2_0")
            gemm("wo2_1")
            norm_T("ffn2")
            ffn(2)

        @block.sync
        def _(sp):
            for t in range(T):
                sp.dma_start(memx[:, t, :], dram["mem_2"][0, t * P:(t + 1) * P, :]).then_inc(sem(f"mem {t} in"), 16)
            for t in range(T):
                sp.dma_start(x[:, t, :], dram["x"][0, t * P:(t + 1) * P, :]).then_inc(sem(f"x {t} in"), 16)

            for n, c in enumerate(chunks):
                if n >= RAW:
                    sp.wait_ge(sem("lo ready"), n - RAW + 1)
                src = dram[c["w"]][0, c["row"]:c["row"] + c["nk"] * P, c["col"]:c["col"] + c["n"]]
                sp.dma_start(raw[:, n % RAW, 0:c["nk"], 0:c["n"]], src.rearrange("(k p) n -> p k n", p=P))\
                  .then_inc(sem(f"raw {n % RAW} in"), 16)
            for c in range(2):
                for t in range(T):
                    sp.wait_ge(*moved(f"d2_{c}", t))
                    sp.dma_start(out[0, t * P:(t + 1) * P, c * CN:(c + 1) * CN], x[:, t, c * CN:(c + 1) * CN])\
                      .then_inc(sem("out written"), 16)
            sp.wait_ge(sem("out written"), 16 * 2 * T)

        @block.scalar
        def _(act):
            A = nc.scalar.activation
            nc.scalar.preload_act_table_set("natural_log_exp_and_others")

            def row(dst, name, family):
                act.dma_start(dst, dram[name][0, :].partition_broadcast(P)).then_inc(sem(family), 16)

            act.dma_start(cst[:, :], dram["consts"]).then_inc(sem("consts in"), 16)
            row(memg, "norm_mem_2", "memory gain in")
            row(gain[:, :], "attn_norm_g", "gain in")
            act.dma_start(vec[0:3 * FT, :], dram["ffn_conv_w"][0].rearrange("a (b p) -> (a b) p", p=P))\
               .then_inc(sem("vec in"), 16)
            act.dma_start(vec[3 * FT:4 * FT, :], dram["ffn_conv_b"][0].rearrange("(b p) -> b p", p=P))\
               .then_inc(sem("vec in"), 16)
            row(bf[:, :], "b_forget", "small in")
            row(og[:, :], "hg_out_gain_2", "small in")
            for n, name in enumerate(("moba_q_norm_g", "moba_k_norm_g", "fox_q_norm_g", "fox_k_norm_g",
                                      "sa_q_gain_2", "sa_k_gain_2", "mem_q_gain_2", "mem_k_gain_2")):
                row(hgain[:, n, :], name, "small in")

            nxt = [0]

            def hi_one(n, i=0):
                c = chunks[n]
                act.wait_ge(sem(f"raw {n % RAW} in"), 16 * (n // RAW + 1) + 16 * (4 // RAW) * i)
                if n >= SPLIT:
                    act.wait_ge(sem("chunk used"), n - SPLIT + 1 + 4 * i)
                A(whi[:, n % SPLIT, 0:c["nk"], 0:c["n"]], raw[:, n % RAW, 0:c["nk"], 0:c["n"]], ACT.Copy)\
                    .then_inc(sem("hi ready"), 1)

            def hi_to(n):
                while nxt[0] <= min(n, len(chunks) - 1):
                    hi_one(nxt[0])
                    nxt[0] += 1

            def guess(step, cols):
                act.wait_ge(*at("mean square", step))
                done(A(rs[:, cols], ms[:, cols], ACT.Ln), "log", step)
                act.wait_ge(*at("log", step))
                done(A(rs[:, cols], rs[:, cols], ACT.Exp, scale=-0.5), "guess", step)

            def norm_squares(k, src, ready, last=None):
                for t in range(T):
                    act.wait_ge(*ready(t))
                    if last:
                        act.wait_ge(*last)
                    done(A(xn[:, t, :], src[:, t, :], ACT.Square, accum_out=ss[:, t:t + 1]), "squares", f"{k} {t}")
                    guess(f"{k} {t}", slice(t, t + 1))

            def norm_hi(k, hi):
                for t in range(T):
                    for b in range(2):
                        act.wait_ge(*at(f"bank{2 * t + b} full", f"{k}T"))
                        done(A(hi[:, 4 * b:4 * b + 4, t * P:(t + 1) * P],
                               X[2 * t + b].rearrange("p (c t) -> p c t", t=P), ACT.Copy),
                             "feature hi", f"{k} {2 * t + b}")

            def next_gain(k, name):
                act.wait_ge(*at("tokens scaled", f"{k} 1"))
                row(gain[:, :], name, "gain in")

            def heads_in(name, src, sqs, n=512):
                for t in range(T):
                    a = sums(act, name, t)
                    A(src[:, t, 0:n], a[:, 0:n], ACT.Copy)
                    if name == "mkv":
                        A(mv[:, t, :], a[:, 256:512], ACT.Copy)
                    leave(A(sqs[:, t, 0:n], a[:, 0:n], ACT.Square), name, t)

            def turned(dst, step, banks):
                for n, b in enumerate(banks):
                    act.wait_ge(*at(f"bank{b} full", f"{step}T"))
                    done(A(dst[:, 2 * n:2 * n + 2, :], X[b].rearrange("p (c t) -> p c t", t=S), ACT.Copy),
                         f"bank{b} free", f"{step}T")

            def exps(j):
                act.wait_ge(*at("max ready", f"{j}"))
                whole, pr, b = head(j)[4], probs(j), j % 2
                if whole and j >= 18:
                    act.wait_ge(*at("bank2 full", f"probs {j - 2} None"))
                for t, c0, n in ((1, 0, S), (0, S, S if whole else P)):
                    src = X[b][:, c0:c0 + n] if whole else pr[:, c0:c0 + n]
                    ins = A(pr[:, c0:c0 + n], src, ACT.Exp, bias=nm[:, j, t:t + 1], scale=DH ** -0.5,
                            accum_out=sm[:, j, t:t + 1])
                if whole:
                    done(ins, f"bank{b} free", f"scores {j}")
                else:
                    done(ins, "probs ready", f"{j}")

            def probs_out(j, unit):
                step = f"probs {j} {unit}"
                act.wait_ge(*at("bank2 full", step))
                c0 = 0 if j is not None else 3 * P
                c1 = 4 * P if unit is not None or head(j)[4] else 3 * P
                pt = probsT(j or 0)
                if j is not None and j not in (0, 16):
                    act.wait_ge(*at("bank3 full", f"pv {j - 1}"))
                if unit:
                    act.wait_ge(*at("out split", f"{unit - 1}"))
                done(A(pt[:, c0:c1], X[2][:, c0:c1], ACT.Copy), "bank2 free", step)
                if unit is not None:
                    act.wait_ge(*at("bank2 free", step))
                    blk, t = unit // 2, unit % 2
                    done(A(ohi[:, blk, t * P:(t + 1) * P], pt[:, 3 * P:4 * P], ACT.Copy), "out hi", f"{unit}")

            def ffn(m):
                first = groups[f"g{m}_0"]["first"]

                def move(which, i=0, short=""):
                    name, n = f"{which}{m}{short or '_0'}", REST if short else CN
                    dst, base = (gtok, 0) if which == "g" else (utok, 2)
                    for t in range(T):
                        a = sums(act, name, t, i)
                        if not short and t == 0:
                            for b in range(base, base + 2):
                                act.wait_ge(sem(f"bank{b} full"), cnt.value(f"bank{b} full", f"{which}{m}T", i) - 1
                                            if (f"bank{b} full", f"{which}{m}T") in known else 1)
                        leave(A(dst[:, t, 0:n], a[:, 0:n], ACT.Copy), name, t, i)

                def gate_in(i=0, short=""):
                    v = cnt.value("act split", f"{m}{short}", i) - 1
                    if not isinstance(v, int) or v > 0:
                        act.wait_ge(sem("act split"), v)
                    for b in range(1 if short else 2):
                        act.wait_ge(*at(f"bank{b} full", f"g{m}{short}T", i))
                        blk = FT - 2 if short else 4 * i + 2 * b
                        if m == 1:
                            for c in range(2):
                                ins = A(y[:, 2 * b + c, :], X[b][:, c * S:(c + 1) * S], ACT.Identity,
                                        bias=vT[:, bass.ds(blk + c + 3 * FT, 1)],
                                        scale=vT[:, bass.ds(blk + c + 2 * FT, 1)])
                            done(ins, "gate in", f"{m}{short} {b}", i)
                        else:
                            done(A(y[:, 2 * b:2 * b + 2, :], X[b].rearrange("p (c t) -> p c t", t=S), ACT.Copy),
                                 f"bank{b} free", f"g{m}{short}T", i)

                def finish(i=0, short=""):
                    n = 2 if short else 4
                    act.wait_ge(*at(f"bank{0 if short else 1} free", f"g{m}{short}T", i))
                    done(A(e[:, 0:n, :], y[:, 0:n, :], ACT.Exp, scale=-1.0), "gate exp", f"{m}{short}", i)
                    act.wait_ge(*at("gate exp", f"{m}{short}", i))
                    done(A(e[:, 0:n, :], e[:, 0:n, :], ACT.Identity, bias=1.0), "gate plus", f"{m}{short}", i)
                    act.wait_ge(*at("act ready", f"{m}{short}", i))
                    dst = ahi[:, FT - 2:FT, :] if short else ahi[:, bass.ds(4 * i, 4), :]
                    done(A(dst, y[:, 0:n, :], ACT.Copy), "act hi", f"{m}{short}", i)

                hi_to(first)
                move("g", short="s")
                hi_to(first + 1)
                gate_in(short="s")
                hi_to(first + 3)
                move("u", short="s")
                finish(short="s")
                with act.Fori(0, PAIRS) as i:
                    cnt.enter()
                    move("g", i)
                    hi_one(first + 4, i)
                    hi_one(first + 5, i)
                    gate_in(i)
                    hi_one(first + 6, i)
                    hi_one(first + 7, i)
                    move("u", i)
                    finish(i)
                cnt.leave(PAIRS)
                nxt[0] = first + 4 + 4 * PAIRS
                for c in range(2):
                    hi_to(groups[f"d{m}_{c}"]["last"] + 3)

            act.wait_ge(*at("bank0 full", "vecT"))
            done(A(vT[:, :], X[0][:, 0:4 * FT], ACT.Copy), "bank0 free", "vecT")
            norm_squares("mem", memx, lambda t: (sem(f"mem {t} in"), 16))
            norm_hi("mem", ohi)
            hi_to(1)
            for t in range(T):
                act.wait_ge(*at("tokens scaled", "mem 1"))
                act.dma_start(gates[:, t, :], dram["b_gate"][0].rearrange("a d -> (a d)").partition_broadcast(P))\
                   .then_inc(sem("gate bias in"), 16)
            norm_squares("x1", x, lambda t: (sem(f"x {t} in"), 16), at("bank3 full", "memT"))
            norm_hi("x1", hhi)
            next_gain("x1", "ffn_norm_g")
            hi_to(groups["mkv"]["last"] + 3)
            heads_in("mkv", qraw, sq, 256)
            guess("mk", slice(0, T * 4))
            where = {"mk": mkT, "qa": qT[0], "ka": kT[0], "qb": qT[1], "kb": kT[1]}
            for name, last in FIRST_GROUPS:
                hi_to(groups[name]["last"] + 3)
                if last:
                    turned(where[last], last, T_BANKS[last])
                if name in where:
                    heads_in(name, qraw, sq)
                    guess(name, slice(0, T * 8))
                elif name != "f":
                    for t in range(T):
                        a = sums(act, name, t)
                        leave(A(va[name == "vb"][:, t, :], a[:, :], ACT.Copy), name, t)
                else:
                    act.wait_ge(*at("forget", "-|z|"))
                    done(A(lt[:, 0], lt[:, 0], ACT.Exp), "forget exp", "0")
                    act.wait_ge(*at("forget exp", "0"))
                    done(A(lt[:, 1], lt[:, 0], ACT.Ln, bias=1.0), "forget ln", "0")

            for s in STEPS1:
                if s % 2 == 0 and s < 16:
                    hi_to(groups["gate0"]["first"] + s // 2 + 3)
                if s < 16:
                    exps(s)
                if s % 4 == 3 and s < 16:
                    n = s // 4
                    act.wait_ge(*moved(f"gate{n}", 1))
                    cols = gates[:, :, n * CN:(n + 1) * CN]
                    done(A(cols, cols, ACT.Exp, scale=-1.0), "mix exp", f"{n}")
                if s >= 1:
                    probs_out(s - 1 if s <= 16 else None, s - 4 if s >= 4 else None)
            for c in range(2):
                hi_to(groups[f"brb{c}"]["last"] + 3)
            for b in range(4):
                act.wait_ge(*at(f"bank{b} full", "mergedT"))
                done(A(hhi[:, 4 * (b // 2):4 * (b // 2) + 4, b % 2 * P:(b % 2 + 1) * P],
                       X[b].rearrange("p (c t) -> p c t", t=P), ACT.Copy), "merged hi", f"{b}")
            hi_to(groups["wo1_1"]["last"] + 3)
            norm_squares("ffn1", x, lambda t: moved("wo1_1", t), at("bank3 full", "mergedT"))
            norm_hi("ffn1", hhi)
            next_gain("ffn1", "norm_mix_2")
            ffn(1)

            norm_squares("x2", x, lambda t: moved("d1_1", t), at("bank3 full", "u1T", PAIRS - 1))
            norm_hi("x2", hhi)
            next_gain("x2", "norm_ffn_2")
            hi_to(groups["iqb"]["last"] + 3)
            for t in range(T):
                a = sums(act, "iqb", t)
                A(tok[0][:, t, 256:512], a[:, 0:256], ACT.Copy)
                A(ikk[:, t, 0:DH], a[:, 256:320], ACT.Copy)
                A(ikk[:, t, DH:P], a[:, 256:320], ACT.Copy)
                leave(A(iw[:, t, :], a[:, 320:328], ACT.Copy, scale=IDX_SCALE), "iqb", t)
            hi_to(groups["sviq"]["last"] + 3)
            for t in range(T):
                a = sums(act, "sviq", t)
                A(sv[:, t, :], a[:, 0:256], ACT.Copy)
                leave(A(tok[0][:, t, 0:256], a[:, 256:512], ACT.Copy), "sviq", t)
            hi_to(groups["hf"]["last"] + 3)
            for t in range(T):
                a = sums(act, "hf", t)
                A(tok[1][:, t, :], a[:, :], ACT.Copy)
                leave(A(vh[:, t, :], a[:, :], ACT.Abs), "hf", t)
            act.wait_ge(*moved("hf", 1))
            done(A(vh[:, :, :], vh[:, :, :], ACT.Exp, scale=-1.0), "hgrn exp", "f")
            act.wait_ge(*at("hgrn exp", "f"))
            done(A(vh[:, :, :], vh[:, :, :], ACT.Ln, bias=1.0), "hgrn ln", "f")
            turned(iqT, "iq", [0, 1])
            act.wait_ge(*at("bank2 full", "ikT"))
            done(A(ikT[:, :], X[2][:, 0:S], ACT.Copy), "bank2 free", "ikT")
            act.wait_ge(*at("hgrn k arg", "0"))
            done(A(tok[1][:, :, :], tok[1][:, :, :], ACT.Exp), "hgrn k", "0")
            for h in range(8):
                act.wait_ge(*at(f"bank{h % 2} full", f"index {h}"))
                if h >= 2:
                    act.wait_ge(*at("index summed", f"{h - 2}"))
                done(A(rel[h % 2], X[h % 2][:, 0:384], ACT.Relu), f"bank{h % 2} free", f"index {h}")
            hi_to(groups["hq"]["last"] + 3)
            act.wait_ge(*at("log f", "0"))
            for t in range(T):
                a = sums(act, "hq", t)
                A(tok[0][:, t, :], a[:, :], ACT.Copy)
                leave(A(vh[:, t, :], a[:, :], ACT.Exp, scale=-1.0), "hq", t)
            hi_to(groups["sqk"]["last"] + 3)
            turned(hkT, "hk", [2, 3])
            turned(hqT, "hq", [0, 1])
            heads_in("sqk", tok[0], tok[1])
            guess("sqk", slice(0, T * 8))
            hi_to(groups["mq"]["last"] + 3)
            turned(sqkT, "sqk", T_BANKS["sqk"])
            heads_in("mq", tok[0], tok[1], 256)
            guess("mq", slice(0, T * 4))
            hi_to(groups["hi"]["last"] + 3)
            turned(mqT, "mq", T_BANKS["mq"])
            act.wait_ge(*at("hgrn q", "0"))
            for t in range(T):
                a = sums(act, "hi", t)
                leave(A(vh[:, t, :], a[:, :], ACT.Copy), "hi", t)
            for s in STEPS2:
                if s in (17, 20):
                    hi_to(groups["hg"]["first"] + (s - 17) // 3 + 3)
                if s < 24:
                    exps(s)
                if s == 21:
                    for t in range(T):
                        a = sums(act, "hg", t)
                        A(tok[0][:, t, :], a[:, :], ACT.Copy)
                        leave(A(tok[1][:, t, :], a[:, :], ACT.Exp, scale=-1.0), "hg", t)
                if 17 <= s <= 24:
                    probs_out(s - 1, None)

            def decays(u):
                if u > 0:
                    act.wait_ge(*at("q decayed", f"{u - 1}"))
                    act.wait_ge(*at("k decayed", f"{u - 1}"))
                for b in range(2):
                    act.wait_ge(*at(f"bank{b} full", f"decay {u}"))
                    done(A(dec[:, 4 * b:4 * b + 4, :], X[b].rearrange("p (c t) -> p c t", t=P), ACT.Exp),
                         f"bank{b} free", f"decay {u}")

            decays(0)
            for u in range(8):
                if u % 2 == 1:
                    h = u // 2
                    act.wait_ge(*at("bank0 full", f"cross {h}"))
                    if h:
                        act.wait_ge(*at("bank1 full", f"hout {h - 1}"))
                    done(A(AT[:, 2, :], X[0][:, 0:P], ACT.Copy), "bank0 free", f"cross {h}")
                if u < 7:
                    decays(u + 1)
            act.wait_ge(*at("bank1 free", "hout 3"))
            act.wait_ge(*at("weights summed", "7"))
            act.wait_ge(*at("hgrn gate", "0"))
            done(A(tok[1][:, :, :], xn[:, :, 0:512], ACT.Square), "hgrn squares", "0")
            guess("hgrn", slice(0, T * 4))
            for b, blk in enumerate((4, 6, 0, 2)):
                act.wait_ge(*at(f"bank{b} full", f"out {blk}T"))
                done(A(o2hi[:, blk:blk + 2, :], X[b].rearrange("p (c t) -> p c t", t=S), ACT.Copy), "out2 hi", f"{b}")
            hi_to(groups["wo2_1"]["last"] + 3)
            norm_squares("ffn2", x, lambda t: moved("wo2_1", t), at("bank3 full", "out 2T"))
            norm_hi("ffn2", hhi)
            ffn(2)

        @block.vector
        def _(dve):
            V = nc.vector
            nxt = [0]

            def lo_one(n, i=0):
                c = chunks[n]
                dve.wait_ge(sem("hi ready"), n + 1 + 4 * i)
                V.tensor_tensor(wlo[:, n % SPLIT, 0:c["nk"], 0:c["n"]], raw[:, n % RAW, 0:c["nk"], 0:c["n"]],
                                whi[:, n % SPLIT, 0:c["nk"], 0:c["n"]].bitcast(F32), ALU.subtract)\
                    .then_inc(sem("lo ready"), 1)

            def lo_to(n):
                while nxt[0] <= min(n, len(chunks) - 1):
                    lo_one(nxt[0])
                    nxt[0] += 1

            def root(step, cols):
                dve.wait_ge(*at("guess", step))
                done(V.tensor_tensor(nt[:, cols], rs[:, cols], rs[:, cols], ALU.mult), "newton", f"{step} a")
                dve.wait_ge(*at("newton", f"{step} a"))
                done(V.scalar_tensor_tensor(nt[:, cols], nt[:, cols], -0.5, ms[:, cols], ALU.mult, ALU.mult),
                     "newton", f"{step} b")
                dve.wait_ge(*at("newton", f"{step} b"))
                done(V.scalar_tensor_tensor(rs[:, cols], nt[:, cols], 1.5, rs[:, cols], ALU.add, ALU.mult),
                     "newton", f"{step} c")
                dve.wait_ge(*at("newton", f"{step} c"))

            def norm(k, src, g, hi, lo, gain_in):
                for t in range(T):
                    dve.wait_ge(*at("squares", f"{k} {t}"))
                    done(V.tensor_scalar(ms[:, t:t + 1], ss[:, t:t + 1], 1.0 / D, EPS, ALU.mult, ALU.add),
                         "mean square", f"{k} {t}")
                    root(f"{k} {t}", slice(t, t + 1))
                    dve.wait_ge(*gain_in)
                    done(V.scalar_tensor_tensor(xn[:, t, :], src[:, t, :], rs[:, t:t + 1], g, ALU.mult, ALU.mult),
                         "tokens scaled", f"{k} {t}")
                for t in range(T):
                    for b in range(2):
                        n = 2 * t + b
                        dve.wait_ge(*at("feature hi", f"{k} {n}"))
                        h = (slice(None), slice(4 * b, 4 * b + 4), slice(t * P, (t + 1) * P))
                        done(V.tensor_tensor(lo[h], X[n].rearrange("p (c t) -> p c t", t=P), hi[h].bitcast(F32),
                                             ALU.subtract), f"bank{n} free", f"{k}T")

            def head_norm(step, src, sqs, heads, gains, width=DH, rope=False, name=None):
                dve.wait_ge(*moved(name or step, 1))
                n = T * heads
                shape = [P, T, heads, width]
                view = src[:, :, 0:heads * width].rearrange("p t (h d) -> p t h d", d=width)
                done(V.tensor_reduce(ss[:, 0:n].rearrange("p (t h) -> p t h", t=T),
                                     sqs[:, :, 0:heads * width].rearrange("p t (h d) -> p t h d", d=width),
                                     AX.X, ALU.add), "head squares", step)
                dve.wait_ge(*at("head squares", step))
                done(V.tensor_scalar(ms[:, 0:n], ss[:, 0:n], 1.0 / width, EPS, ALU.mult, ALU.add), "mean square", step)
                root(step, slice(0, n))
                r = rs[:, 0:n].rearrange("p (t h) -> p t h", t=T).unsqueeze(3).to_broadcast(shape)
                done(V.tensor_tensor(view, view, r, ALU.mult), "heads scaled", step)
                dve.wait_ge(*at("heads scaled", step))
                if step == "mk":
                    dve.wait_ge(sem("small in"), 16 * 10)
                for n, (h0, h1, g) in enumerate(gains):
                    part = view[:, :, h0:h1, :]
                    b = g.unsqueeze(1).unsqueeze(1).to_broadcast([P, T, h1 - h0, width])
                    ins = V.tensor_tensor(part, part, b, ALU.mult)
                done(ins, "heads gained" if rope else "heads ready", step)

            def attn_max(j):
                whole, pr, b = head(j)[4], probs(j), j % 2
                dve.wait_ge(*at(f"bank{b} full", f"scores {j}"))
                if whole:
                    for t, c0 in ((1, 0), (0, S)):
                        ins = V.tensor_reduce(mx[:, j, t:t + 1], X[b][:, c0:c0 + S], AX.X, ALU.max)
                    done(ins, "row max", f"{j}")
                    dve.wait_ge(*at("row max", f"{j}"))
                else:
                    if j >= 2 and j not in (16, 17):
                        dve.wait_ge(*at("bank2 full", f"probs {j - 2} {unit_with(j - 2)}"))
                    mask = cst[:, C_CM:C_CM + 3 * P] if j < 16 else madd[:, :]
                    for t, c0, n in ((1, 0, S), (0, S, P)):
                        ins = V.tensor_tensor_reduce(out=pr[:, c0:c0 + n], in0=X[b][:, c0:c0 + n],
                                                     in1=mask[:, c0:c0 + n], scale=1.0, scalar=FLOOR, op0=ALU.add,
                                                     op1=ALU.max, accum_out=mx[:, j, t:t + 1])
                    done(ins, f"bank{b} free", f"scores {j}")
                    dve.wait_ge(*at(f"bank{b} free", f"scores {j}"))
                done(V.tensor_scalar(nm[:, j, :], mx[:, j, :], -DH ** -0.5, None, ALU.mult), "max ready", f"{j}")

            def attn_out(j):
                done(V.reciprocal(rc[:, j, :], sm[:, j, :]), "sum inverted", f"{j}")
                dve.wait_ge(*at("sum inverted", f"{j}"))
                dve.wait_ge(*at("bank3 full", f"pv {j}"))
                c = head(j)[3]
                done(V.tensor_tensor(xn[:, :, c:c + DH], X[3][:, 0:2 * DH].rearrange("p (t d) -> p t d", d=DH),
                                     rc[:, j, :].unsqueeze(2).to_broadcast([P, T, DH]), ALU.mult),
                     "bank3 free", f"pv {j}")

            def residual(name):
                c = int(name[-1])
                for t in range(T):
                    a = sums(dve, name, t)
                    cols = x[:, t, c * CN:(c + 1) * CN]
                    leave(V.tensor_tensor(cols, a[:, :], cols, ALU.add), name, t)

            def ffn(m):
                first = groups[f"g{m}_0"]["first"]

                def conv(i=0, short=""):
                    for b in range(1 if short else 2):
                        dve.wait_ge(*at("gate in", f"{m}{short} {b}", i))
                        blk = FT - 2 if short else 4 * i + 2 * b
                        for lag in (1, 2):
                            for c in range(2):
                                step = f"{m}{short} {b} {c}"
                                if lag == 2:
                                    dve.wait_ge(*at("tap added", step, i))
                                ins = V.scalar_tensor_tensor(
                                    y[:, 2 * b + c, lag:S], X[b][:, c * S:(c + 1) * S - lag],
                                    vT[:, bass.ds(blk + c + (2 - lag) * FT, 1)], y[:, 2 * b + c, lag:S],
                                    ALU.mult, ALU.add)
                                if lag == 1:
                                    done(ins, "tap added", step, i)
                        done(ins, f"bank{b} free", f"g{m}{short}T", i)

                def finish(i=0, short=""):
                    n = 2 if short else 4
                    step = f"{m}{short}"
                    dve.wait_ge(*at("gate plus", step, i))
                    done(V.reciprocal(e[:, 0:n, :], e[:, 0:n, :]), "gate inverted", step, i)
                    for b in range(n // 2):
                        dve.wait_ge(*at(f"bank{2 + b} full", f"u{m}{short}T", i))
                        done(V.tensor_tensor(y[:, 2 * b:2 * b + 2, :], y[:, 2 * b:2 * b + 2, :],
                                             X[2 + b].rearrange("p (c t) -> p c t", t=S), ALU.mult),
                             f"bank{2 + b} free", f"u{m}{short}T", i)
                    dve.wait_ge(*at(f"bank{1 + n // 2} free", f"u{m}{short}T", i))
                    dve.wait_ge(*at("gate inverted", step, i))
                    done(V.tensor_tensor(y[:, 0:n, :], y[:, 0:n, :], e[:, 0:n, :], ALU.mult), "act ready", step, i)
                    dve.wait_ge(*at("act hi", step, i))
                    blks = slice(FT - 2, FT) if short else bass.ds(4 * i, 4)
                    done(V.tensor_tensor(alo[:, blks, :], y[:, 0:n, :], ahi[:, blks, :].bitcast(F32), ALU.subtract),
                         "act split", step, i)

                lo_to(first + 1)
                if m == 1:
                    conv(short="s")
                lo_to(first + 3)
                finish(short="s")
                with dve.Fori(0, PAIRS) as i:
                    cnt.enter()
                    lo_one(first + 4, i)
                    lo_one(first + 5, i)
                    if m == 1:
                        conv(i)
                    lo_one(first + 6, i)
                    lo_one(first + 7, i)
                    finish(i)
                cnt.leave(PAIRS)
                nxt[0] = first + 4 + 4 * PAIRS
                for c in range(2):
                    lo_to(groups[f"d{m}_{c}"]["last"] + 3)
                    residual(f"d{m}_{c}")

            def gain_at(n):
                return sem("gain in"), 16 * n

            norm("mem", memx, memg, ohi, olo, (sem("memory gain in"), 16))
            lo_to(1)
            norm("x1", x, gain[:, :], hhi, hlo, gain_at(1))
            lo_to(groups["mkv"]["last"] + 3)
            head_norm("mk", qraw, sq, 4, [(0, 4, hgain[:, 7, :])], name="mkv")
            for name, last in FIRST_GROUPS:
                lo_to(groups[name]["last"] + 3)
                if name[0] in "qk":
                    g = hgain[:, 2 * (name[1] == "b") + (name[0] == "k"), :]
                    head_norm(name, qraw, sq, 8, [(0, 8, g)], rope=name[1] == "a")
                if name == "f":
                    for t in range(T):
                        a = sums(dve, name, t)
                        leave(V.tensor_tensor(lf[:, t, :], a[:, 0:8], bf[:, :], ALU.add), name, t)
                    dve.wait_ge(*moved("f", 1))
                    done(V.tensor_scalar(lt[:, 0], lf[:, :, :], -1.0, None, ALU.mult), "forget neg", "0")
                    dve.wait_ge(*at("forget neg", "0"))
                    done(V.tensor_tensor(lt[:, 0], lt[:, 0], lf[:, :, :], ALU.min), "forget", "-|z|")
                    dve.wait_ge(*at("forget ln", "0"))
                    done(V.scalar_tensor_tensor(lf[:, :, :], lf[:, :, :], 0.0, lt[:, 1], ALU.min, ALU.subtract),
                         "log forget", "0")

            for s in STEPS1:
                if s % 2 == 0 and s < 16:
                    lo_to(groups["gate0"]["first"] + s // 2 + 3)
                if s < 16:
                    attn_max(s)
                if s % 4 == 3 and s < 16:
                    n = s // 4
                    for t in range(T):
                        a = sums(dve, f"gate{n}", t)
                        if n == 0 and t == 0:
                            dve.wait_ge(sem("gate bias in"), 32)
                        cols = gates[:, t, n * CN:(n + 1) * CN]
                        leave(V.tensor_tensor(cols, a[:, :], cols, ALU.add), f"gate{n}", t)
                if 2 <= s <= 17:
                    attn_out(s - 2)
                if s >= 4:
                    u = s - 4
                    dve.wait_ge(*at("out hi", f"{u}"))
                    h = (slice(None), u // 2, slice(u % 2 * P, (u % 2 + 1) * P))
                    done(V.tensor_tensor(olo[h], PT[:, 3 * P:4 * P], ohi[h].bitcast(F32), ALU.subtract),
                         "out split", f"{u}")
                if s % 4 == 1 and s >= 5:
                    n = s // 4 - 1
                    cols = gates[:, :, n * CN:(n + 1) * CN]
                    dve.wait_ge(*at("mix plus", f"{n}"))
                    done(V.reciprocal(cols, cols), "mix ready", f"{n}")

            for c in range(2):
                lo_to(groups[f"bra{c}"]["last"] + 3)
                if c == 0:
                    dve.wait_ge(*at("mix ready", "3"))
                for t in range(T):
                    a = sums(dve, f"bra{c}", t)
                    leave(V.tensor_tensor(xn[:, t, c * CN:(c + 1) * CN], a[:, :], gates[:, t, c * CN:(c + 1) * CN],
                                          ALU.mult), f"bra{c}", t)
                lo_to(groups[f"brb{c}"]["last"] + 3)
                for t in range(T):
                    a = sums(dve, f"brb{c}", t)
                    g = gates[:, t, D + c * CN:D + (c + 1) * CN]
                    leave(V.tensor_tensor(g, a[:, :], g, ALU.mult), f"brb{c}", t)
                    dve.wait_ge(*moved(f"brb{c}", t))
                    cols = xn[:, t, c * CN:(c + 1) * CN]
                    done(V.tensor_tensor(cols, cols, g, ALU.add), "merged", f"{c} {t}")
            for b in range(4):
                dve.wait_ge(*at("merged hi", f"{b}"))
                h = (slice(None), slice(4 * (b // 2), 4 * (b // 2) + 4), slice(b % 2 * P, (b % 2 + 1) * P))
                done(V.tensor_tensor(hlo[h], X[b].rearrange("p (c t) -> p c t", t=P), hhi[h].bitcast(F32),
                                     ALU.subtract), f"bank{b} free", "mergedT")
            for c in range(2):
                lo_to(groups[f"wo1_{c}"]["last"] + 3)
                residual(f"wo1_{c}")
            norm("ffn1", x, gain[:, :], hhi, hlo, gain_at(2))
            ffn(1)

            norm("x2", x, gain[:, :], hhi, hlo, gain_at(3))
            lo_to(groups["hf"]["last"] + 3)
            dve.wait_ge(*at("hgrn ln", "f"))
            done(V.scalar_tensor_tensor(logf[:, :, :], tok[1][:, :, :], 0.0, vh[:, :, :], ALU.min, ALU.subtract),
                 "log f", "0")
            dve.wait_ge(*at("log f", "0"))
            done(V.tensor_tensor(tok[1][:, :, :], logf[:, :, :], tok[1][:, :, :], ALU.subtract), "hgrn k arg", "0")
            halves = ((1, slice(0, S)), (0, slice(S, S + P)))
            for h in range(8):
                dve.wait_ge(*at(f"bank{h % 2} free", f"index {h}"))
                for t, c in halves:
                    if h == 0:
                        ins = V.tensor_scalar(sco[:, c], rel[0][:, c], iw[:, t, h:h + 1], None, ALU.mult)
                    else:
                        if t == 1:
                            dve.wait_ge(*at("index summed", f"{h - 1}"))
                        ins = V.scalar_tensor_tensor(sco[:, c], rel[h % 2][:, c], iw[:, t, h:h + 1], sco[:, c],
                                                     ALU.mult, ALU.add)
                done(ins, "index summed", f"{h}")
            dve.wait_ge(*at("index summed", "7"))
            done(V.tensor_tensor(sco, sco, cst[:, C_CM:C_CM + 3 * P], ALU.add), "index masked", "0")
            dve.wait_ge(*at("index masked", "0"))
            for r in range(TOPK // 8):
                for t, c in halves:
                    src = sco if r == 0 else work
                    if r:
                        dve.wait_ge(*at("struck out", f"{r - 1} {t}"))
                    done(V.max(mx8[:, t, :], src[:, c]), "eight found", f"{r} {t}")
                for t, c in halves:
                    src = sco if r == 0 else work
                    dve.wait_ge(*at("eight found", f"{r} {t}"))
                    done(V.match_replace(work[:, c], mx8[:, t, :], src[:, c], FLOOR), "struck out", f"{r} {t}")
            for t, c in halves:
                dve.wait_ge(*at("struck out", f"{TOPK // 8 - 1} {t}"))
            done(V.tensor_scalar(madd[:, :], work, -2e38, BIG, ALU.is_lt, ALU.mult), "chosen", "0")
            dve.wait_ge(*at("chosen", "0"))
            done(V.scalar_tensor_tensor(madd[:, :], madd[:, :], -BIG, cst[:, C_CM:C_CM + 3 * P], ALU.add, ALU.add),
                 "chosen", "1")
            lo_to(groups["hq"]["last"] + 3)
            dve.wait_ge(*at("silu plus", "q"))
            done(V.reciprocal(vh[:, :, :], vh[:, :, :]), "silu inverted", "q")
            dve.wait_ge(*at("silu inverted", "q"))
            done(V.tensor_tensor(tok[0][:, :, :], tok[0][:, :, :], vh[:, :, :], ALU.mult), "hgrn q", "0")
            lo_to(groups["sqk"]["last"] + 3)
            head_norm("sqk", tok[0], tok[1], 8, [(0, 4, hgain[:, 4, :]), (4, 8, hgain[:, 5, :])])
            lo_to(groups["mq"]["last"] + 3)
            head_norm("mq", tok[0], tok[1], 4, [(0, 4, hgain[:, 6, :])])
            lo_to(groups["hi"]["last"] + 3)
            dve.wait_ge(*at("chosen", "1"))
            for s in STEPS2:
                if s in (17, 20):
                    lo_to(groups["hg"]["first"] + (s - 17) // 3 + 3)
                if s < 24:
                    attn_max(s)
                if 18 <= s:
                    attn_out(s - 2)
            dve.wait_ge(*at("silu plus", "g"))
            done(V.reciprocal(tok[1][:, :, :], tok[1][:, :, :]), "silu inverted", "g")
            dve.wait_ge(*at("silu inverted", "g"))
            done(V.tensor_tensor(tok[0][:, :, :], tok[0][:, :, :], tok[1][:, :, :], ALU.mult), "hgrn gate", "0")

            def q_decayed(u):
                h, t = u // 2, u % 2
                dve.wait_ge(*at("bank1 free", f"decay {u}"))
                if u:
                    dve.wait_ge(*at("bank3 full", f"pairs {u - 1}"))
                q = hqT[:, h, t * P:(t + 1) * P]
                ins = V.tensor_tensor(qd[:, :, :], dec[:, 1 - t:8 - t, :],
                                      q.unsqueeze(1).to_broadcast([P, LEVELS, P]), ALU.mult)
                if t == 1:
                    if h:
                        dve.wait_ge(*at("bank0 full", f"cross {h - 1}"))
                    ins = V.tensor_tensor(qx[:, :], dec[:, 7, :], q, ALU.mult)
                done(ins, "q decayed", f"{u}")

            q_decayed(0)
            for u in range(8):
                h, t = u // 2, u % 2
                masked = tok[1].rearrange("p t (l s) -> p (t l) s", s=P)
                if u:
                    dve.wait_ge(*at("weights summed", f"{u - 1}"))
                else:
                    dve.wait_ge(*at("hgrn gate", "0"))
                for b in range(2):
                    dve.wait_ge(*at(f"bank{2 + b} full", f"pairs {u}"))
                    done(V.tensor_tensor(masked[:, 4 * b:4 * b + 4, :], X[2 + b].rearrange("p (l s) -> p l s", s=P),
                                         cst[:, C_HM + b * 512:C_HM + (b + 1) * 512].rearrange("p (l s) -> p l s", s=P),
                                         ALU.mult), f"bank{2 + b} free", f"pairs {u}")
                dve.wait_ge(*at("bank3 free", f"pairs {u}"))
                if h:
                    dve.wait_ge(*at("bank1 full", f"hout {h - 1}"))
                done(V.tensor_reduce(AT[:, t, :], masked.rearrange("p l s -> p s l"), AX.X, ALU.add),
                     "weights summed", f"{u}")
                if u < 7:
                    q_decayed(u + 1)
                if t == 1:
                    dve.wait_ge(*at("bank1 full", f"hout {h}"))
                    done(V.tensor_copy(xn[:, :, h * P:(h + 1) * P], X[1][:, 0:2 * P].rearrange("p (t d) -> p t d", d=P)),
                         "bank1 free", f"hout {h}")
            dve.wait_ge(*at("hgrn squares", "0"))
            view = xn[:, :, 0:512].rearrange("p t (h d) -> p t h d", d=P)
            done(V.tensor_reduce(ss[:, 0:8].rearrange("p (t h) -> p t h", t=T),
                                 tok[1].rearrange("p t (h d) -> p t h d", d=P), AX.X, ALU.add), "head squares", "hgrn")
            dve.wait_ge(*at("head squares", "hgrn"))
            done(V.tensor_scalar(ms[:, 0:8], ss[:, 0:8], 1.0 / P, EPS, ALU.mult, ALU.add), "mean square", "hgrn")
            root("hgrn", slice(0, 8))
            r = rs[:, 0:8].rearrange("p (t h) -> p t h", t=T).unsqueeze(3).to_broadcast([P, T, 4, P])
            done(V.tensor_tensor(view, view, r, ALU.mult), "heads scaled", "hgrn")
            dve.wait_ge(*at("heads scaled", "hgrn"))
            b = og[:, :].unsqueeze(1).unsqueeze(1).to_broadcast([P, T, 4, P])
            done(V.tensor_tensor(view, view, b, ALU.mult), "heads gained", "hgrn")
            dve.wait_ge(*at("heads gained", "hgrn"))
            done(V.tensor_tensor(xn[:, :, 0:512], xn[:, :, 0:512], tok[0][:, :, :], ALU.mult), "hgrn normed", "0")
            for b, blk in enumerate((4, 6, 0, 2)):
                dve.wait_ge(*at("out2 hi", f"{b}"))
                h = (slice(None), slice(blk, blk + 2), slice(None))
                done(V.tensor_tensor(o2lo[h], X[b].rearrange("p (c t) -> p c t", t=S), o2hi[h].bitcast(F32),
                                     ALU.subtract), f"bank{b} free", f"out {blk}T")
            for c in range(2):
                lo_to(groups[f"wo2_{c}"]["last"] + 3)
                residual(f"wo2_{c}")
            norm("ffn2", x, gain[:, :], hhi, hlo, gain_at(4))
            ffn(2)

        @block.gpsimd
        def _(pool):
            G = nc.gpsimd

            def rope(name):
                pool.wait_ge(*at("heads gained", name))
                v = qraw[:, :, :].rearrange("p t (h d) -> p t h d", d=DH)
                x1, x2 = v[:, :, :, 0:8], v[:, :, :, 8:16]
                cs = cst[:, C_CS:C_CS + 16 * T].rearrange("p (t a d) -> p t a d", t=T, a=2)
                cos = cs[:, :, 0, :].unsqueeze(2).to_broadcast([P, T, 8, 8])
                sin = cs[:, :, 1, :].unsqueeze(2).to_broadcast([P, T, 8, 8])
                for n, (a, b) in enumerate(((x1, cos), (x2, sin), (x2, cos), (x1, sin))):
                    ins = G.tensor_tensor(rp[:, n], a, b, ALU.mult)
                done(ins, "rope products", name)
                pool.wait_ge(*at("rope products", name))
                G.tensor_tensor(x1, rp[:, 0], rp[:, 1], ALU.subtract)
                done(G.tensor_tensor(x2, rp[:, 2], rp[:, 3], ALU.add), "heads roped", name)

            def decay_rows(j):
                h = j - 8
                pool.wait_ge(*at("log forget", "0"))
                if h:
                    pool.wait_ge(*at(f"bank{(j - 1) % 2} full", f"scores {j - 1}"))
                t8, e8 = cst[:, C_T8:C_T8 + P], cst[:, C_E8:C_E8 + P]
                G.tensor_scalar(L[:, 0, :], t8, lf[:, 0, h:h + 1], None, ALU.mult)
                G.tensor_scalar(L[:, 1, :], e8, lf[:, 0, h:h + 1], None, ALU.mult)
                done(G.tensor_scalar(L[:, 2, :], t8, lf[:, 1, h:h + 1], None, ALU.mult), "decay rows", f"{j}")

            def plus_one(buf, ready, family, step):
                pool.wait_ge(*ready)
                done(G.tensor_scalar(buf, buf, 1.0, None, ALU.add), family, step)

            pool.wait_ge(sem("consts in"), 16)
            rope("qa")
            rope("ka")
            for s in STEPS1:
                if 8 <= s < 16:
                    decay_rows(s)
                if s % 4 == 3 and s < 16:
                    n = s // 4
                    plus_one(gates[:, :, n * CN:(n + 1) * CN], at("mix exp", f"{n}"), "mix plus", f"{n}")

            plus_one(vh[:, :, :], moved("hq", 1), "silu plus", "q")
            plus_one(tok[1][:, :, :], moved("hg", 1), "silu plus", "g")
            for u in range(8):
                h, t = u // 2, u % 2
                pool.wait_ge(*at("bank1 free", f"decay {u}"))
                if u:
                    pool.wait_ge(*at("bank3 full", f"pairs {u - 1}"))
                k = hkT[:, h, t * P:(t + 1) * P]
                ins = G.tensor_tensor(kd[:, :, :], dec[:, 1 - t:8 - t, :],
                                      k.unsqueeze(1).to_broadcast([P, LEVELS, P]), ALU.mult)
                if t == 0:
                    if h:
                        pool.wait_ge(*at("bank0 full", f"cross {h - 1}"))
                    ins = G.tensor_tensor(kx[:, :], dec[:, 0, :], k, ALU.mult)
                done(ins, "k decayed", f"{u}")

    return cnt.seen


SHAPES = {
    "x": (1, S, D), "attn_norm_g": (1, D), "w_in": (1, D, 5128), "b_forget": (1, 8), "b_gate": (1, 2, D),
    "moba_q_norm_g": (1, DH), "moba_k_norm_g": (1, DH), "fox_q_norm_g": (1, DH), "fox_k_norm_g": (1, DH),
    "w_branch_moba": (1, 512, D), "w_branch_fox": (1, 512, D), "w_out": (1, D, D), "ffn_norm_g": (1, D),
    "w_ffn_up": (1, D, 2 * DFF), "ffn_conv_w": (1, 3, DFF), "ffn_conv_b": (1, DFF), "w_ffn_down": (1, DFF, D),
    "mem_2": (1, S, D), "w_in_2": (1, D, 3656), "w_out_2": (1, D, D), "w_mem_kv_2": (1, D, 512),
    "norm_mix_2": (1, D), "norm_mem_2": (1, D), "norm_ffn_2": (1, D), "hg_out_gain_2": (1, P),
    "sa_q_gain_2": (1, DH), "sa_k_gain_2": (1, DH), "mem_q_gain_2": (1, DH), "mem_k_gain_2": (1, DH),
    "w_ffn_in_2": (1, D, 2 * DFF), "w_ffn_out_2": (1, DFF, D), "consts": (P, C_END),
}


def build(nc, known):
    dram = {n: nc.dram_tensor(f"in_{n}", s, F32, kind="ExternalInput").ap() for n, s in SHAPES.items()}
    out = nc.dram_tensor("out", (1, S, D), F32, kind="ExternalOutput").ap()
    return program(nc, dram, out, known)


def kernel(**inputs):
    import concourse.bacc as bacc
    from concourse.bass_utils import run_bass_kernel_spmd

    def core():
        return bacc.Bacc("TRN2", target_bir_lowering=False, num_devices=1)

    known = build(core(), {})
    nc = core()
    assert build(nc, known) == known
    arrays = {f"in_{n}": np.ascontiguousarray(inputs[n]) for n in SHAPES if n != "consts"}
    arrays["in_consts"] = constants()
    r = run_bass_kernel_spmd(nc, [arrays], core_ids=[0])
    return r.results[0]["out"]
```

```python
import numpy as np
from contextlib import ExitStack

import concourse.bass as bass
from concourse import mybir
from concourse.alu_op_type import AluOpType as ALU

ACT = mybir.ActivationFunctionType
AX = mybir.AxisListType
F32 = mybir.dt.float32
F32R = mybir.dt.float32r

P = 128
D = 1024
S = 256
T = S // P
DH = 64
DFF = 2816
KT = D // P
FT = DFF // P
CK = 4
CN = 512
RAW, SPLIT = 2, 4
PAIRS = DFF // CN
REST = DFF - PAIRS * CN
NORMS = ("mem", "x1", "ffn1", "x2", "ffn2")
LEVELS = 7
EPS = 1e-6
BIG = 1e30
FLOOR = -3e38
TOPK = min(256, S // 4)
IDX_SCALE = float(8 ** -0.5 * 64 ** -0.5)

C_ID = 0
C_CM = C_ID + P
C_T8 = C_CM + 3 * P
C_E8 = C_T8 + P
C_OR = C_E8 + P
C_CS = C_OR + 2 * P
C_END = C_CS + T * 16
C_HC = 0
C_HM = C_HC + 9 * P
C_HEND = C_HM + 8 * P


def constants():
    c, g = np.zeros((P, C_END), np.float32), np.zeros((P, C_HEND), np.float32)
    s, t = np.arange(P)[:, None], np.arange(P)[None, :]
    c[:, C_ID:C_ID + P] = s == t
    c[:, C_CM + P:C_CM + 2 * P] = np.where(t <= s, 0, -BIG)
    c[:, C_CM + 2 * P:C_CM + 3 * P] = np.where(t <= s, 0, -BIG)
    c[:, C_T8:C_T8 + P] = 8.0 * (s <= t)
    c[:, C_E8:C_E8 + P] = 8.0
    c[:, C_OR:C_OR + P] = 1.0
    c[:, C_OR + P:C_OR + 2 * P] = s > t
    g[:, C_HC:C_HC + P] = s > t
    for n in range(LEVELS):
        half = 64 >> n
        mid = t // (2 * half) * (2 * half) + half - 1
        late = t > mid
        g[:, C_HC + (n + 1) * P:C_HC + (n + 2) * P] = np.where(late, (s > mid) & (s <= t), (s > t) & (s <= mid))
        same = s // (2 * half) == t // (2 * half)
        g[:, C_HM + n * P:C_HM + (n + 1) * P] = same & late & (s <= mid)
    g[:, C_HC + 8 * P:C_HC + 9 * P] = s <= t
    g[:, C_HM + 7 * P:C_HM + 8 * P] = s == t
    freq = (500000.0 ** (-np.arange(8) * 2.0 / 16)).astype(np.float32)
    angle = (np.arange(S, dtype=np.float32)[:, None] * freq[None, :]).astype(np.float64)
    for i in range(T):
        c[:, C_CS + 16 * i:C_CS + 16 * i + 8] = np.cos(angle[i * P:(i + 1) * P])
        c[:, C_CS + 16 * i + 8:C_CS + 16 * i + 16] = np.sin(angle[i * P:(i + 1) * P])
    return c, g


def plan():
    groups, chunks = {}, []

    def add(name, w, col, n, kt, lhs, k0=0):
        groups[name] = dict(name=name, w=w, col=col, n=n, kt=kt, lhs=lhs, k0=k0, idx=len(groups))
        stream(name)

    def stream(*names):
        for name in names:
            if "at" in groups[name]:
                for _ in groups[name].pop("at"):
                    chunks.pop()
        for a in range(0, groups[names[0]]["kt"], CK):
            for name in names:
                g = groups[name]
                g.setdefault("at", []).append(len(chunks))
                chunks.append(dict(w=g["w"], row=a * P, nk=min(CK, g["kt"] - a), col=g["col"], n=g["n"]))
        for name in names:
            g = groups[name]
            g["first"], g["last"] = g["at"][0], g["at"][-1]

    add("mkv", "w_mem_kv_2", 0, CN, KT, "o")
    for n, c in (("qa", 0), ("ka", 512), ("va", 1024), ("qb", 1536), ("kb", 2048)):
        add(n, "w_in", c, CN, KT, "h")
    add("f", "w_in", 3072, 8, KT, "h")
    add("vb", "w_in", 2560, CN, KT, "h")
    for n in range(4):
        add(f"gate{n}", "w_in", 3080 + CN * n, CN, KT, "h")
    for c in range(2):
        add(f"bra{c}", "w_branch_moba", CN * c, CN, 4, "o")
        add(f"brb{c}", "w_branch_fox", CN * c, CN, 4, "o", 4)
    for c in range(2):
        add(f"wo1_{c}", "w_out", CN * c, CN, KT, "h")

    def ffn(m, up, down, gcol, ucol):
        lhs = "o" if m == 1 else "h"
        add(f"g{m}s", up, gcol + PAIRS * CN, REST, KT, lhs)
        add(f"u{m}s", up, ucol + PAIRS * CN, REST, KT, lhs)
        stream(f"g{m}s", f"u{m}s")
        for j in range(PAIRS):
            add(f"g{m}_{j}", up, gcol + CN * j, CN, KT, lhs)
            add(f"u{m}_{j}", up, ucol + CN * j, CN, KT, lhs)
        for c in range(2):
            add(f"d{m}_{c}", down, CN * c, CN, FT, "act")

    ffn(1, "w_ffn_up", "w_ffn_down", DFF, 0)
    for n, c, w in (("iqb", 3072, 328), ("sviq", 2560, 512), ("hf", 512, 512), ("hq", 0, 512), ("sqk", 2048, 512),
                    ("mq", 3400, 256), ("hi", 1024, 512), ("hg", 1536, 512)):
        add(n, "w_in_2", c, w, KT, "h")
        if n == "sviq":
            stream("iqb", "sviq")
    for c in range(2):
        add(f"wo2_{c}", "w_out_2", CN * c, CN, KT, "o")
    ffn(2, "w_ffn_in_2", "w_ffn_out_2", 0, DFF)
    return groups, chunks


class Count:

    def __init__(self, known, sem):
        self.known, self.now, self.seen, self.sem, self.loop = known, {}, {}, sem, None

    def mark(self, ins, family, step, i=0):
        ins.then_inc(self.sem(family), 1)
        if family.endswith("free"):
            return
        n = self.now[family] = self.now.get(family, 0) + 1
        if (family, step) not in self.seen:
            self.seen[family, step] = [n, 0]
            if self.loop:
                self.loop[1].append((family, step))
        else:
            base, per = self.seen[family, step]
            assert isinstance(i, int) and n == base + per * i, (family, step, n, base, per, i)

    def value(self, family, step, i=0):
        family = family.replace("free", "full")
        if self.known and (family, step) not in self.known:
            raise KeyError((family, step))
        base, per = self.known.get((family, step), (1, 0))
        return base + i * per if per else base

    def at(self, family, step, i=0):
        return self.sem(family), self.value(family, step, i)

    def enter(self):
        self.loop = (dict(self.now), [])

    def leave(self, times):
        was, steps = self.loop
        per = {f: n - was.get(f, 0) for f, n in self.now.items()}
        for f, s in steps:
            self.seen[f, s][1] = per[f]
        for f in self.now:
            self.now[f] = was.get(f, 0) + per[f] * times
        self.loop = None


def program(nc, dram, out, known):
    groups, chunks = plan()
    ctx = ExitStack()
    sems = {}

    def sem(name):
        if name not in sems:
            sems[name] = ctx.enter_context(nc.semaphore("s_" + name.replace(" ", "_")))
        return sems[name]

    cnt = Count(known, sem)
    done, at = cnt.mark, cnt.at

    with ctx:
        def sb(name, shape, dt=F32, where=ctx):
            return where.enter_context(nc.sbuf_tensor("b_" + name, shape, dt))

        raw = sb("raw", [P, RAW, CK, CN])
        whi = sb("whi", [P, SPLIT, CK, CN], F32R)
        wlo = sb("wlo", [P, SPLIT, CK, CN], F32R)
        x = sb("x", [P, T, D])
        hhi = sb("hhi", [P, KT, S], F32R)
        hlo = sb("hlo", [P, KT, S], F32R)
        ohi = sb("ohi", [P, KT, S], F32R)
        olo = sb("olo", [P, KT, S], F32R)
        cst = sb("cst", [P, C_END])
        gain = sb("gain", [P, D])
        xn = sb("xn", [P, T, D])
        mkT = sb("mkT", [P, 2, S])
        mv = sb("mv", [P, T, 256])
        hgain = sb("hgain", [P, 8, DH])
        vec = sb("vec", [4 * FT, P])
        vT = sb("vT", [P, 4 * FT])
        bf = sb("bf", [P, 8])
        ss = sb("ss", [P, 16 + 2 * len(NORMS)])
        ms = sb("ms", [P, 16 + 2 * len(NORMS)])
        rs = sb("rs", [P, 16 + 2 * len(NORMS)])
        nt = sb("nt", [P, 16 + 2 * len(NORMS)])
        mx = sb("mx", [P, 24, T])
        nm = sb("nm", [P, 24, T])
        sm = sb("sm", [P, 24, T])
        rc = sb("rc", [P, 24, T])
        lf = sb("lf", [P, T, 8])
        lt = sb("lt", [P, 2, T, 8])
        rp = sb("rp", [P, 4, T, 8, 8])
        og = sb("og", [P, P])

        a1 = ExitStack()
        qT = [sb(f"qT{n}", [P, 4, S], where=a1) for n in range(2)]
        kT = [sb(f"kT{n}", [P, 4, S], where=a1) for n in range(2)]
        va = [sb(f"v{n}", [P, T, 512], where=a1) for n in range(2)]
        gates = sb("gates", [P, T, 2 * D], where=a1)
        qraw = sb("qraw", [P, T, 512], where=a1)
        sq = sb("sq", [P, T, 512], where=a1)
        L = sb("L", [P, 3, P], where=a1)
        Sm = [sb(f"Sm{n}", [P, 384], where=a1) for n in range(2)]
        PT = sq[:, 0, :]
        memx = gates[:, :, 0:D]
        memg = gates[:, 0, D:2 * D]
        a1.close()

        a2 = ExitStack()
        ahi = sb("ahi", [P, FT, S], F32R, where=a2)
        alo = sb("alo", [P, FT, S], F32R, where=a2)
        y = sb("y", [P, 4, S], where=a2)
        e = sb("e", [P, 4, S], where=a2)
        lg = sb("lg", [P, 4, S], where=a2)
        gtok, utok = xn[:, :, 0:CN], xn[:, :, CN:2 * CN]
        a2.close()

        a3 = ExitStack()
        logf = sb("logf", [P, T, 512], where=a3)
        vh = sb("vh", [P, T, 512], where=a3)
        hqT = sb("hqT", [P, 4, S], where=a3)
        hkT = sb("hkT", [P, 4, S], where=a3)
        big = sb("big", [P, 3 * 1024], where=a3)
        dec = big[:, 0:1024].rearrange("p (l t) -> p l t", t=P)
        qd = big[:, 1024:1920].rearrange("p (l t) -> p l t", t=P)
        kd = big[:, 2048:2944].rearrange("p (l t) -> p l t", t=P)
        iqT = big[:, 0:1024].rearrange("p (l t) -> p l t", t=S)
        sco, work = big[:, 1024:1408], big[:, 1408:1792]
        rel = [big[:, 2048:2432], big[:, 2432:2816]]
        kx, qx = sb("kx", [P, P], where=a3), sb("qx", [P, P], where=a3)
        AT = sb("AT", [P, 3, P], where=a3)
        ikT = sb("ikT", [P, S], where=a3)
        sqkT = sb("sqkT", [P, 4, S], where=a3)
        sv = sb("sv", [P, T, 256], where=a3)
        mqT = sb("mqT", [P, 2, S], where=a3)
        madd = sb("madd", [P, 384], where=a3)
        iw = sb("iw", [P, T, 8], where=a3)
        mx8 = sb("mx8", [P, T, 8], where=a3)
        ikk = sb("ikk", [P, T, P], where=a3)
        tok = [sb("tokA", [P, T, 512], where=a3), sb("tokB", [P, T, 512], where=a3)]
        hgc = sb("hgc", [P, C_HEND], where=a3)
        Sn, PTn = [big[:, 1024:1536], big[:, 1536:2048]], big[:, 0:512]
        a3.close()

        acc = [[ctx.enter_context(nc.psum_tensor(f"acc{p}{t}", [P, 512], F32)) for t in range(T)] for p in range(2)]
        XX = ctx.enter_context(nc.psum_tensor("banks", [P, 4, 512], F32))
        X = [XX[:, n, :] for n in range(4)]
        ident = cst[:, C_ID:C_ID + P]
        lhs_of = {"h": (hhi, hlo), "o": (ohi, olo), "act": (ahi, alo)}

        def rstd(k, t=None):
            c = 16 + 2 * NORMS.index(k)
            return slice(c, c + 2) if t is None else slice(c + t, c + t + 1)

        def head(j):
            r = slice(64 * (j % 2), 64 * (j % 2) + 64)
            if j < 16:
                n, h = j // 8, j % 8
                return qT[n][r, h // 2, :], kT[n][r, h // 2, :], va[n][:, :, h * DH:h * DH + DH], j * DH, False
            h = (j - 16) % 4
            if j < 20:
                return sqkT[r, h // 2, :], sqkT[r, 2 + h // 2, :], sv[:, :, h * DH:h * DH + DH], 512 + h * DH, False
            return mqT[r, h // 2, :], mkT[r, h // 2, :], mv[:, :, h * DH:h * DH + DH], 768 + h * DH, True

        def probs(j):
            return (Sm if j < 16 else Sn)[j % 2]

        def probsT(j):
            return PT if j < 16 else PTn

        T_BANKS = {"mk": [0], "qa": [2, 3], "ka": [0, 1], "qb": [2, 3], "kb": [0, 1], "sqk": [2, 3], "mq": [0]}
        FIRST_GROUPS = (("qa", "mk"), ("ka", "qa"), ("va", "ka"), ("qb", None), ("kb", "qb"), ("f", "kb"), ("vb", None))

        def unit_with(j):
            return j - 3 if 3 <= j < 16 else None

        def moved(name, t, i=0):
            return sem(f"acc{groups[name]['idx'] % 2}{t} free"), groups[name]["idx"] // 2 + 1 + i

        def leave(ins, name, t, i=0):
            done(ins, f"acc{groups[name]['idx'] % 2}{t} free", name, i)

        def sums(eng, name, t, i=0):
            g = groups[name]
            if t == 0:
                eng.wait_ge(sem("tile 0 summed"), g["idx"] + 1 + 2 * i)
            else:
                eng.wait_ge(sem("chunk used"), g["last"] + 1 + 4 * i)
            return acc[g["idx"] % 2][t]

        STEPS1 = range(20)
        STEPS2 = range(16, 26)

        block = ctx.enter_context(nc.Block())

        @block.tensor
        def _(pe):
            def claim(bank, step, i=0):
                v = cnt.value(f"bank{bank} full", step, i) - 1
                if not isinstance(v, int) or v > 0:
                    pe.wait_ge(sem(f"bank{bank} free"), v)

            def full(ins, bank, step, i=0):
                done(ins, f"bank{bank} full", step, i)

            def gemm(name, c=None, i=0, norm=None):
                g = groups[name]
                hi, lo = lhs_of[g["lhs"]]
                p, turn, cols = g["idx"] % 2, g["idx"] // 2, g["n"]
                lastc = (g["kt"] - 1) // CK
                for c in range(lastc + 1) if c is None else [c]:
                    n = g["at"][c]
                    nk = min(CK, g["kt"] - c * CK)
                    pe.wait_ge(sem("lo ready"), n + 1 + 4 * i)
                    for t in range(T):
                        if c == 0 and turn > 0:
                            pe.wait_ge(sem(f"acc{p}{t} free"), turn + i)
                        if norm:
                            pe.wait_ge(*at(f"bank{2 * t + c} free", f"{norm}T"))
                        for k in range(nk):
                            kk = g["k0"] + c * CK + k
                            a, b = hi[:, kk, t * P:(t + 1) * P], lo[:, kk, t * P:(t + 1) * P]
                            wh, wl = whi[:, n % SPLIT, k, 0:cols], wlo[:, n % SPLIT, k, 0:cols]
                            o = acc[p][t][:, 0:cols]
                            first, last = c == 0 and k == 0, c == lastc and k == nk - 1
                            nc.tensor.matmul(o, a, wh, start=first, stop=False)
                            nc.tensor.matmul(o, b, wh, start=False, stop=False)
                            mm = nc.tensor.matmul(o, a, wl, start=False, stop=last)
                        if t == T - 1:
                            mm.then_inc(sem("chunk used"), 1)
                        elif c == lastc:
                            mm.then_inc(sem("tile 0 summed"), 1)

            def norm_T(k, b, tiles=range(T)):
                for t in tiles:
                    pe.wait_ge(*at("tokens scaled", f"{k} {t} {b}"))
                    claim(2 * t + b, f"{k}T")
                    for c in range(4):
                        mm = nc.tensor.transpose(X[2 * t + b][:, c * P:(c + 1) * P],
                                                 xn[:, t, (4 * b + c) * P:(4 * b + c + 1) * P], ident)
                    full(mm, 2 * t + b, f"{k}T")

            def before_norm(k, name):
                gemm(name, 0)
                norm_T(k, 0)
                for c in range(1, len(groups[name]["at"])):
                    gemm(name, c)

            def after_norm(k, one, two):
                gemm(one, 0, norm=k)
                norm_T(k, 1, [0])
                gemm(two, 0, norm=k)
                norm_T(k, 1, [1])
                gemm(one, 1, norm=k)
                gemm(two, 1, norm=k)

            def tok_T(src, step, ready, banks, blocks=4, first=0):
                pe.wait_ge(*ready)
                for b in range(0, blocks, 2):
                    bank = banks[b // 2]
                    claim(bank, step)
                    for c in range(2):
                        for t in range(T):
                            cols = slice((first + b + c) * P, (first + b + c + 1) * P)
                            mm = nc.tensor.transpose(X[bank][:, c * S + t * P:c * S + (t + 1) * P], src[:, t, cols],
                                                     ident)
                    full(mm, bank, step)

            def attn_scores(j):
                q, k, _, _, whole = head(j)
                b = j % 2
                claim(b, f"scores {j}")
                for start, steps in ((0, ("qa", "ka")), (8, ("qb", "kb")), (16, ("sqk",)), (20, ("mq", "mk"))):
                    if j == start:
                        for step in steps:
                            pe.wait_ge(*at(f"bank{T_BANKS[step][-1]} free", f"{step}T"))
                fox = 8 <= j < 16
                mm = nc.tensor.matmul(X[b][:, 0:S], q[:, P:S], k, start=True, stop=not fox)
                if fox:
                    pe.wait_ge(*at("decay rows", f"{j}"))
                    nc.tensor.matmul(X[b][:, 0:P], L[:, 1, :], cst[:, C_OR + P:C_OR + 2 * P], start=False, stop=False)
                    nc.tensor.matmul(X[b][:, 0:S], L[:, 2, :], cst[:, C_OR:C_OR + 2 * P], start=False, stop=True)
                n = S if whole else P
                mm = nc.tensor.matmul(X[b][:, S:S + n], q[:, 0:P], k[:, 0:n], start=True, stop=not fox)
                if fox:
                    mm = nc.tensor.matmul(X[b][:, S:S + P], L[:, 0, :], cst[:, C_OR + P:C_OR + 2 * P],
                                          start=False, stop=True)
                full(mm, b, f"scores {j}")

            def attn_T(j, unit=None):
                step = f"probs {j} {unit}"
                claim(2, step)
                if j is not None:
                    pe.wait_ge(*(at(f"bank{j % 2} free", f"scores {j}") if head(j)[4] else at("probs ready", f"{j}")))
                    for c in range(4 if head(j)[4] else 3):
                        mm = nc.tensor.transpose(X[2][:, c * P:(c + 1) * P], probs(j)[:, c * P:(c + 1) * P], ident)
                if unit is not None:
                    blk, t = unit // 2, unit % 2
                    pe.wait_ge(*at("bank3 free", f"pv {2 * blk + 1}"))
                    mm = nc.tensor.transpose(X[2][:, 3 * P:4 * P], xn[:, t, blk * P:(blk + 1) * P], ident)
                full(mm, 2, step)

            def attn_pv(j):
                _, _, v, _, whole = head(j)
                pe.wait_ge(*at("bank2 free", f"probs {j} {unit_with(j)}"))
                for start, step in ((0, "va"), (8, "vb"), (16, "sviq"), (20, "mkv")):
                    if j == start:
                        pe.wait_ge(*moved(step, 1))
                claim(3, f"pv {j}")
                pt = probsT(j)
                nc.tensor.matmul(X[3][:, DH:2 * DH], pt[:, 0:P], v[:, 0, :], start=True, stop=False)
                nc.tensor.matmul(X[3][:, DH:2 * DH], pt[:, P:2 * P], v[:, 1, :], start=False, stop=True)
                mm = nc.tensor.matmul(X[3][:, 0:DH], pt[:, 2 * P:3 * P], v[:, 0, :], start=True, stop=not whole)
                if whole:
                    mm = nc.tensor.matmul(X[3][:, 0:DH], pt[:, 3 * P:4 * P], v[:, 1, :], start=False, stop=True)
                full(mm, 3, f"pv {j}")

            def ffn_T(m, which, i=0, short=""):
                src, base = (gtok, 0) if which == "g" else (utok, 2)
                for t in range(T):
                    pe.wait_ge(*moved(f"{which}{m}{short or '_0'}", t, i))
                for b in range(1 if short else 2):
                    step = f"{which}{m}{short}T"
                    claim(base + b, step, i)
                    for c in range(2):
                        for t in range(T):
                            mm = nc.tensor.transpose(X[base + b][:, c * S + t * P:c * S + (t + 1) * P],
                                                     src[:, t, (2 * b + c) * P:(2 * b + c + 1) * P], ident)
                    full(mm, base + b, step, i)

            def ffn(m):
                after_norm(f"ffn{m}", f"g{m}s", f"u{m}s")
                ffn_T(m, "g", short="s")
                gemm(f"g{m}_0", 0)
                ffn_T(m, "u", short="s")
                gemm(f"g{m}_0", 1)

                def pair(i, last):
                    gemm(f"u{m}_0", 0, i)
                    ffn_T(m, "g", i)
                    gemm(f"u{m}_0", 1, i)
                    if not last:
                        gemm(f"g{m}_0", 0, i + 1)
                    else:
                        pe.wait_ge(*at("act split", f"{m}", 0))
                        gemm(f"d{m}_0", 0)
                    ffn_T(m, "u", i)
                    if not last:
                        gemm(f"g{m}_0", 1, i + 1)

                with pe.Fori(0, PAIRS - 1) as i:
                    cnt.enter()
                    pair(i, False)
                cnt.leave(PAIRS - 1)
                pair(PAIRS - 1, True)
                for c in range(1, (FT + CK - 1) // CK):
                    if c < PAIRS:
                        pe.wait_ge(*at("act split", f"{m}", c))
                    gemm(f"d{m}_0", c)
                if m == 1:
                    before_norm("x2", "d1_1")
                else:
                    gemm("d2_1")

            pe.wait_ge(sem("consts in"), 16)
            pe.wait_ge(sem("vec in"), 32)
            full(nc.tensor.transpose(X[0][:, 0:4 * FT], vec[:, :], ident[0:4 * FT, 0:4 * FT]), 0, "vecT")

            norm_T("mem", 0)
            norm_T("mem", 1)
            gemm("mkv", 0, norm="mem")
            norm_T("x1", 0)
            gemm("mkv", 1, norm="mem")
            norm_T("x1", 1)
            for name, last in FIRST_GROUPS:
                gemm(name, norm="x1" if name == "qa" else None)
                if last:
                    tok_T(qraw, f"{last}T", at("heads roped" if last in ("qa", "ka") else "heads ready", last), T_BANKS[last], 2 if last == "mk" else 4)

            for s in STEPS1:
                if s < 16:
                    attn_scores(s)
                if s % 2 == 0 and s < 16:
                    gemm(f"gate{s // 4}", s // 2 % 2)
                if s >= 1:
                    attn_T(s - 1 if s <= 16 else None, s - 4 if s >= 4 else None)
                if 2 <= s <= 17:
                    attn_pv(s - 2)
            pe.wait_ge(*at("out split", "15"))
            for c in range(2):
                gemm(f"bra{c}")
                gemm(f"brb{c}")
            for c in range(2):
                for t in range(T):
                    bank = 2 * c + t
                    pe.wait_ge(*at("merged", f"{c} {t}"))
                    claim(bank, "mergedT")
                    for b in range(4):
                        mm = nc.tensor.transpose(X[bank][:, b * P:(b + 1) * P],
                                                 xn[:, t, c * CN + b * P:c * CN + (b + 1) * P], ident)
                    full(mm, bank, "mergedT")
            pe.wait_ge(*at("bank3 free", "mergedT"))
            gemm("wo1_0")
            before_norm("ffn1", "wo1_1")
            ffn(1)

            after_norm("x2", "iqb", "sviq")
            gemm("hf")
            tok_T(tok[0], "iqT", moved("sviq", 1), [0, 1])
            claim(2, "ikT")
            for t in range(T):
                mm = nc.tensor.transpose(X[2][:, t * P:(t + 1) * P], ikk[:, t, :], ident)
            full(mm, 2, "ikT")
            pe.wait_ge(*at("bank2 free", "ikT"))
            for h in range(8):
                r = slice(64 * (h % 2), 64 * (h % 2) + 64)
                claim(h % 2, f"index {h}")
                q = iqT[r, h // 2, :]
                nc.tensor.matmul(X[h % 2][:, 0:S], q[:, P:S], ikT[r, :], start=True, stop=True)
                mm = nc.tensor.matmul(X[h % 2][:, S:S + P], q[:, 0:P], ikT[r, 0:P], start=True, stop=True)
                full(mm, h % 2, f"index {h}")
            gemm("hq")
            tok_T(tok[1], "hkT", at("hgrn k", "0"), [2, 3])
            gemm("sqk")
            tok_T(tok[0], "hqT", at("hgrn q", "0"), [0, 1])
            gemm("mq")
            tok_T(tok[0], "sqkT", at("heads ready", "sqk"), T_BANKS["sqk"])
            gemm("hi")
            tok_T(tok[0], "mqT", at("heads ready", "mq"), T_BANKS["mq"], 2)

            def hgrn_decay(u):
                h, t = u // 2, u % 2
                pe.wait_ge(*at("log f", "0"))
                if u == 0:
                    pe.wait_ge(sem("hgrn table in"), 16)
                for b in range(2):
                    claim(b, f"decay {u}")
                    c = C_HC + t * P + b * 512
                    full(nc.tensor.matmul(X[b][:, :], logf[:, t, h * P:(h + 1) * P], hgc[:, c:c + 512],
                                          start=True, stop=True), b, f"decay {u}")

            def hgrn_pairs(u):
                h, t = u // 2, u % 2
                pe.wait_ge(*at("q decayed", f"{u}"))
                pe.wait_ge(*at("k decayed", f"{u}"))
                for b in range(2):
                    claim(2 + b, f"pairs {u}")
                    for c in range(4):
                        n, ts = 4 * b + c, slice(t * P, (t + 1) * P)
                        k, q = (kd[:, n, :], qd[:, n, :]) if n < LEVELS else (hkT[:, h, ts], hqT[:, h, ts])
                        mm = nc.tensor.matmul(X[2 + b][:, c * P:(c + 1) * P], k, q, start=True, stop=True)
                    full(mm, 2 + b, f"pairs {u}")
                if t == 1:
                    claim(0, f"cross {h}")
                    full(nc.tensor.matmul(X[0][:, 0:P], kx[:, :], qx[:, :], start=True, stop=True), 0, f"cross {h}")

            def hgrn_out(h):
                pe.wait_ge(*moved("hi", 1))
                pe.wait_ge(*at("weights summed", f"{2 * h + 1}"))
                pe.wait_ge(*at("bank0 free", f"cross {h}"))
                claim(1, f"hout {h}")
                v = vh[:, :, h * P:(h + 1) * P]
                nc.tensor.matmul(X[1][:, 0:P], AT[:, 0, :], v[:, 0, :], start=True, stop=True)
                nc.tensor.matmul(X[1][:, P:2 * P], AT[:, 1, :], v[:, 1, :], start=True, stop=False)
                full(nc.tensor.matmul(X[1][:, P:2 * P], AT[:, 2, :], v[:, 0, :], start=False, stop=True), 1, f"hout {h}")

            for s in STEPS2:
                if s < 24:
                    attn_scores(s)
                if s in (17, 20):
                    gemm("hg", (s - 17) // 3)
                if 17 <= s <= 24:
                    attn_T(s - 1)
                if 18 <= s:
                    attn_pv(s - 2)
            hgrn_decay(0)
            for u in range(8):
                hgrn_pairs(u)
                if u < 7:
                    hgrn_decay(u + 1)
                if u % 2 == 1:
                    hgrn_out(u // 2)
            for b, blk in enumerate((4, 6, 0, 2)):
                ready = at("bank3 free", "pv 23") if b < 2 else at("hgrn normed", "0")
                tok_T(xn, f"out {blk}T", ready, [b], 2, blk)
            pe.wait_ge(*at("bank3 free", "out 2T"))
            gemm("wo2_0")
            before_norm("ffn2", "wo2_1")
            ffn(2)

        @block.sync
        def _(sp):
            for t in range(T):
                sp.dma_start(memx[:, t, :], dram["mem_2"][0, t * P:(t + 1) * P, :]).then_inc(sem(f"mem {t} in"), 16)
            for t in range(T):
                sp.dma_start(x[:, t, :], dram["x"][0, t * P:(t + 1) * P, :]).then_inc(sem(f"x {t} in"), 16)

            for n, c in enumerate(chunks):
                if n >= RAW:
                    sp.wait_ge(sem("lo ready"), n - RAW + 1)
                src = dram[c["w"]][0, c["row"]:c["row"] + c["nk"] * P, c["col"]:c["col"] + c["n"]]
                sp.dma_start(raw[:, n % RAW, 0:c["nk"], 0:c["n"]], src.rearrange("(k p) n -> p k n", p=P))\
                  .then_inc(sem(f"raw {n % RAW} in"), 16)
            for c in range(2):
                for t in range(T):
                    sp.wait_ge(*moved(f"d2_{c}", t))
                    sp.dma_start(out[0, t * P:(t + 1) * P, c * CN:(c + 1) * CN], x[:, t, c * CN:(c + 1) * CN])\
                      .then_inc(sem("out written"), 16)
            sp.wait_ge(sem("out written"), 16 * 2 * T)

        @block.scalar
        def _(act):
            A = nc.scalar.activation
            nc.scalar.preload_act_table_set("natural_log_exp_and_others")

            def row(dst, name, family):
                act.dma_start(dst, dram[name][0, :].partition_broadcast(P)).then_inc(sem(family), 16)

            act.dma_start(cst[:, :], dram["consts"]).then_inc(sem("consts in"), 16)
            row(memg, "norm_mem_2", "memory gain in")
            row(gain[:, :], "attn_norm_g", "gain in")
            act.dma_start(vec[0:3 * FT, :], dram["ffn_conv_w"][0].rearrange("a (b p) -> (a b) p", p=P))\
               .then_inc(sem("vec in"), 16)
            act.dma_start(vec[3 * FT:4 * FT, :], dram["ffn_conv_b"][0].rearrange("(b p) -> b p", p=P))\
               .then_inc(sem("vec in"), 16)
            row(bf[:, :], "b_forget", "small in")
            row(og[:, :], "hg_out_gain_2", "small in")
            for n, name in enumerate(("moba_q_norm_g", "moba_k_norm_g", "fox_q_norm_g", "fox_k_norm_g",
                                      "sa_q_gain_2", "sa_k_gain_2", "mem_q_gain_2", "mem_k_gain_2")):
                row(hgain[:, n, :], name, "small in")

            nxt = [0]

            def hi_one(n, i=0):
                c = chunks[n]
                act.wait_ge(sem(f"raw {n % RAW} in"), 16 * (n // RAW + 1) + 16 * (4 // RAW) * i)
                if n >= SPLIT:
                    act.wait_ge(sem("chunk used"), n - SPLIT + 1 + 4 * i)
                A(whi[:, n % SPLIT, 0:c["nk"], 0:c["n"]], raw[:, n % RAW, 0:c["nk"], 0:c["n"]], ACT.Copy)\
                    .then_inc(sem("hi ready"), 1)

            def hi_to(n):
                while nxt[0] <= min(n, len(chunks) - 1):
                    hi_one(nxt[0])
                    nxt[0] += 1

            def guess(step, cols):
                act.wait_ge(*at("mean square", step))
                done(A(rs[:, cols], ms[:, cols], ACT.Ln), "log", step)
                act.wait_ge(*at("log", step))
                done(A(rs[:, cols], rs[:, cols], ACT.Exp, scale=-0.5), "guess", step)

            def norm_squares(k, src, ready, junk):
                for t in range(T):
                    act.wait_ge(*ready(t))
                    if t:
                        act.wait_ge(*at("squares", f"{k} 0"))
                    done(A(junk, src[:, t, :], ACT.Square, accum_out=ss[:, rstd(k, t)]), "squares", f"{k} {t}")

            def norm_hi(k, hi, b):
                for t in range(T):
                    act.wait_ge(*at(f"bank{2 * t + b} full", f"{k}T"))
                    done(A(hi[:, 4 * b:4 * b + 4, t * P:(t + 1) * P],
                           X[2 * t + b].rearrange("p (c t) -> p c t", t=P), ACT.Copy),
                         "feature hi", f"{k} {2 * t + b}")

            def scaled(dst, a, func, k, t):
                return A(dst, a, func, scale=rs[:, rstd(k, t)])

            def root_in(k):
                act.wait_ge(*at("newton", f"{k} c"))

            def norm(k, last, hi, name, gain_name):
                norm_hi(k, hi, 0)
                hi_to(groups[last]["last"] + 4)
                norm_squares(k, x, lambda t: moved(last, t), y.rearrange("p c t -> p (c t)"))
                norm_hi(k, hi, 1)
                guess(k, rstd(k))
                if gain_name:
                    next_gain(k, gain_name)
                root_in(k)

            def next_gain(k, name):
                act.wait_ge(*at("tokens scaled", f"{k} 1 1"))
                row(gain[:, :], name, "gain in")

            def heads_in(name, src, sqs, k, n=512):
                for t in range(T):
                    a = sums(act, name, t)
                    scaled(src[:, t, 0:n], a[:, 0:n], ACT.Copy, k, t)
                    if name == "mkv":
                        scaled(mv[:, t, :], a[:, 256:512], ACT.Copy, k, t)
                    leave(scaled(sqs[:, t, 0:n], a[:, 0:n], ACT.Square, k, t), name, t)

            def turned(dst, step, banks):
                for n, b in enumerate(banks):
                    act.wait_ge(*at(f"bank{b} full", f"{step}T"))
                    done(A(dst[:, 2 * n:2 * n + 2, :], X[b].rearrange("p (c t) -> p c t", t=S), ACT.Copy),
                         f"bank{b} free", f"{step}T")

            def exps(j):
                act.wait_ge(*at("max ready", f"{j}"))
                whole, pr, b = head(j)[4], probs(j), j % 2
                if whole and j >= 18:
                    act.wait_ge(*at("bank2 full", f"probs {j - 2} None"))
                for t, c0, n in ((1, 0, S), (0, S, S if whole else P)):
                    src = X[b][:, c0:c0 + n] if whole else pr[:, c0:c0 + n]
                    ins = A(pr[:, c0:c0 + n], src, ACT.Exp, bias=nm[:, j, t:t + 1], scale=DH ** -0.5,
                            accum_out=sm[:, j, t:t + 1])
                if whole:
                    done(ins, f"bank{b} free", f"scores {j}")
                else:
                    done(ins, "probs ready", f"{j}")

            def probs_out(j, unit):
                step = f"probs {j} {unit}"
                act.wait_ge(*at("bank2 full", step))
                c0 = 0 if j is not None else 3 * P
                c1 = 4 * P if unit is not None or head(j)[4] else 3 * P
                pt = probsT(j or 0)
                if j is not None and j not in (0, 16):
                    act.wait_ge(*at("bank3 full", f"pv {j - 1}"))
                if unit:
                    act.wait_ge(*at("out split", f"{unit - 1}"))
                done(A(pt[:, c0:c1], X[2][:, c0:c1], ACT.Copy), "bank2 free", step)
                if unit is not None:
                    act.wait_ge(*at("bank2 free", step))
                    blk, t = unit // 2, unit % 2
                    done(A(ohi[:, blk, t * P:(t + 1) * P], pt[:, 3 * P:4 * P], ACT.Copy), "out hi", f"{unit}")

            def ffn(m):
                first = groups[f"g{m}_0"]["first"]

                def move(which, i=0, short=""):
                    name, n = f"{which}{m}{short or '_0'}", REST if short else CN
                    dst, base = (gtok, 0) if which == "g" else (utok, 2)
                    for t in range(T):
                        a = sums(act, name, t, i)
                        if not short and t == 0:
                            for b in range(base, base + 2):
                                act.wait_ge(sem(f"bank{b} full"), cnt.value(f"bank{b} full", f"{which}{m}T", i) - 1
                                            if (f"bank{b} full", f"{which}{m}T") in known else 1)
                        leave(scaled(dst[:, t, 0:n], a[:, 0:n], ACT.Copy, f"ffn{m}", t), name, t, i)

                def gate_in(i=0, short=""):
                    v = cnt.value("act split", f"{m}{short}", i) - 1
                    if not isinstance(v, int) or v > 0:
                        act.wait_ge(sem("act split"), v)
                    for b in range(1 if short else 2):
                        act.wait_ge(*at(f"bank{b} full", f"g{m}{short}T", i))
                        blk = FT - 2 if short else 4 * i + 2 * b
                        if m == 1:
                            for c in range(2):
                                ins = A(y[:, 2 * b + c, :], X[b][:, c * S:(c + 1) * S], ACT.Identity,
                                        bias=vT[:, bass.ds(blk + c + 3 * FT, 1)],
                                        scale=vT[:, bass.ds(blk + c + 2 * FT, 1)])
                            done(ins, "gate in", f"{m}{short} {b}", i)
                        else:
                            done(A(y[:, 2 * b:2 * b + 2, :], X[b].rearrange("p (c t) -> p c t", t=S), ACT.Copy),
                                 f"bank{b} free", f"g{m}{short}T", i)

                def finish(i=0, short=""):
                    n = 2 if short else 4
                    act.wait_ge(*at(f"bank{0 if short else 1} free", f"g{m}{short}T", i))
                    done(A(lg[:, 0:n, :], y[:, 0:n, :], ACT.Abs), "gate abs", f"{m}{short}", i)
                    act.wait_ge(*at("gate abs", f"{m}{short}", i))
                    done(A(lg[:, 0:n, :], lg[:, 0:n, :], ACT.Exp, scale=-1.0), "gate exp", f"{m}{short}", i)
                    act.wait_ge(*at("gate exp", f"{m}{short}", i))
                    done(A(lg[:, 0:n, :], lg[:, 0:n, :], ACT.Ln, bias=1.0), "gate ln", f"{m}{short}", i)
                    act.wait_ge(*at("gate log", f"{m}{short}", i))
                    done(A(e[:, 0:n, :], e[:, 0:n, :], ACT.Exp), "gate sigmoid", f"{m}{short}", i)
                    act.wait_ge(*at("act ready", f"{m}{short}", i))
                    dst = ahi[:, FT - 2:FT, :] if short else ahi[:, bass.ds(4 * i, 4), :]
                    done(A(dst, y[:, 0:n, :], ACT.Copy), "act hi", f"{m}{short}", i)

                hi_to(first)
                move("g", short="s")
                hi_to(first + 1)
                gate_in(short="s")
                hi_to(first + 3)
                move("u", short="s")
                finish(short="s")
                with act.Fori(0, PAIRS) as i:
                    cnt.enter()
                    move("g", i)
                    hi_one(first + 4, i)
                    hi_one(first + 5, i)
                    gate_in(i)
                    hi_one(first + 6, i)
                    hi_one(first + 7, i)
                    move("u", i)
                    finish(i)
                cnt.leave(PAIRS)
                nxt[0] = first + 4 + 4 * PAIRS
                hi_to(groups[f"d{m}_0"]["last"] + 2)
                if m == 1:
                    norm("x2", "d1_1", hhi, None, "norm_ffn_2")
                else:
                    hi_to(groups["d2_1"]["last"])

            def log_sigmoid(step, z, buf, name):
                act.wait_ge(*moved(name, 1))
                done(A(buf[:, :, :], buf[:, :, :], ACT.Exp, scale=-1.0), "silu exp", step)
                act.wait_ge(*at("silu exp", step))
                done(A(buf[:, :, :], buf[:, :, :], ACT.Ln, bias=1.0), "silu ln", step)
                act.wait_ge(*at("silu log", step))
                done(A(buf[:, :, :], buf[:, :, :], ACT.Exp), "sigmoid", step)

            act.wait_ge(*at("bank0 full", "vecT"))
            done(A(vT[:, :], X[0][:, 0:4 * FT], ACT.Copy), "bank0 free", "vecT")
            norm_squares("mem", memx, lambda t: (sem(f"mem {t} in"), 16), sq.rearrange("p t n -> p (t n)"))
            norm_hi("mem", ohi, 0)
            norm_hi("mem", ohi, 1)
            hi_to(1)
            guess("mem", rstd("mem"))
            for t in range(T):
                act.wait_ge(*at("tokens scaled", "mem 1 1"))
                act.dma_start(gates[:, t, :], dram["b_gate"][0].rearrange("a d -> (a d)").partition_broadcast(P))\
                   .then_inc(sem("gate bias in"), 16)
            norm_hi("x1", hhi, 0)
            hi_to(groups["mkv"]["last"] + 2)
            norm_hi("x1", hhi, 1)
            act.wait_ge(*at("squares", "mem 1"))
            norm_squares("x1", x, lambda t: (sem(f"x {t} in"), 16), sq.rearrange("p t n -> p (t n)"))
            guess("x1", rstd("x1"))
            next_gain("x1", "ffn_norm_g")
            root_in("mem")
            act.wait_ge(*at("squares", "x1 1"))
            heads_in("mkv", qraw, sq, "mem", 256)
            guess("mk", slice(0, T * 4))
            root_in("x1")
            where = {"mk": mkT, "qa": qT[0], "ka": kT[0], "qb": qT[1], "kb": kT[1]}
            for name, last in FIRST_GROUPS:
                hi_to(groups[name]["last"] + 3)
                if last:
                    turned(where[last], last, T_BANKS[last])
                if name in where:
                    heads_in(name, qraw, sq, "x1")
                    guess(name, slice(0, T * 8))
                elif name != "f":
                    for t in range(T):
                        a = sums(act, name, t)
                        leave(scaled(va[name == "vb"][:, t, :], a[:, :], ACT.Copy, "x1", t), name, t)
                else:
                    act.wait_ge(*at("forget", "-|z|"))
                    done(A(lt[:, 0], lt[:, 0], ACT.Exp), "forget exp", "0")
                    act.wait_ge(*at("forget exp", "0"))
                    done(A(lt[:, 1], lt[:, 0], ACT.Ln, bias=1.0), "forget ln", "0")

            for s in STEPS1:
                if s % 2 == 0 and s < 16:
                    hi_to(groups["gate0"]["first"] + s // 2 + 3)
                if s < 16:
                    exps(s)
                if s % 4 == 3 and s < 16:
                    n = s // 4
                    act.wait_ge(*moved(f"gate{n}", 1))
                    cols = gates[:, :, n * CN:(n + 1) * CN]
                    done(A(cols, cols, ACT.Exp, scale=-1.0), "mix exp", f"{n}")
                if s >= 1:
                    probs_out(s - 1 if s <= 16 else None, s - 4 if s >= 4 else None)
            for c in range(2):
                hi_to(groups[f"brb{c}"]["last"] + 3)
            for b in range(4):
                act.wait_ge(*at(f"bank{b} full", "mergedT"))
                done(A(hhi[:, 4 * (b // 2):4 * (b // 2) + 4, b % 2 * P:(b % 2 + 1) * P],
                       X[b].rearrange("p (c t) -> p c t", t=P), ACT.Copy), "merged hi", f"{b}")
            hi_to(groups["wo1_1"]["last"])
            norm("ffn1", "wo1_1", ohi, None, "norm_mix_2")
            ffn(1)

            act.dma_start(hgc[:, :], dram["hgrn"]).then_inc(sem("hgrn table in"), 16)
            for t in range(T):
                a = sums(act, "iqb", t)
                scaled(tok[0][:, t, 256:512], a[:, 0:256], ACT.Copy, "x2", t)
                scaled(ikk[:, t, 0:DH], a[:, 256:320], ACT.Copy, "x2", t)
                scaled(ikk[:, t, DH:P], a[:, 256:320], ACT.Copy, "x2", t)
                leave(scaled(iw[:, t, :], a[:, 320:328], ACT.Copy, "x2", t), "iqb", t)
            hi_to(groups["sviq"]["last"] + 3)
            for t in range(T):
                a = sums(act, "sviq", t)
                scaled(sv[:, t, :], a[:, 0:256], ACT.Copy, "x2", t)
                leave(scaled(tok[0][:, t, 0:256], a[:, 256:512], ACT.Copy, "x2", t), "sviq", t)
            hi_to(groups["hf"]["last"] + 3)
            for t in range(T):
                a = sums(act, "hf", t)
                scaled(tok[1][:, t, :], a[:, :], ACT.Copy, "x2", t)
                leave(scaled(vh[:, t, :], a[:, :], ACT.Abs, "x2", t), "hf", t)
            act.wait_ge(*moved("hf", 1))
            done(A(vh[:, :, :], vh[:, :, :], ACT.Exp, scale=-1.0), "hgrn exp", "f")
            act.wait_ge(*at("hgrn exp", "f"))
            done(A(vh[:, :, :], vh[:, :, :], ACT.Ln, bias=1.0), "hgrn ln", "f")
            turned(iqT, "iq", [0, 1])
            act.wait_ge(*at("bank2 full", "ikT"))
            done(A(ikT[:, :], X[2][:, 0:S], ACT.Copy), "bank2 free", "ikT")
            act.wait_ge(*at("hgrn k arg", "0"))
            done(A(tok[1][:, :, :], tok[1][:, :, :], ACT.Exp), "hgrn k", "0")
            for h in range(8):
                act.wait_ge(*at(f"bank{h % 2} full", f"index {h}"))
                if h >= 2:
                    act.wait_ge(*at("index summed", f"{h - 2}"))
                done(A(rel[h % 2], X[h % 2][:, 0:384], ACT.Relu, scale=IDX_SCALE), f"bank{h % 2} free", f"index {h}")
            hi_to(groups["hq"]["last"] + 3)
            act.wait_ge(*at("log f", "0"))
            for t in range(T):
                a = sums(act, "hq", t)
                scaled(tok[0][:, t, :], a[:, :], ACT.Copy, "x2", t)
                leave(scaled(vh[:, t, :], a[:, :], ACT.Abs, "x2", t), "hq", t)
            log_sigmoid("q", tok[0], vh, "hq")
            hi_to(groups["sqk"]["last"] + 3)
            turned(hkT, "hk", [2, 3])
            turned(hqT, "hq", [0, 1])
            heads_in("sqk", tok[0], tok[1], "x2")
            guess("sqk", slice(0, T * 8))
            hi_to(groups["mq"]["last"] + 3)
            turned(sqkT, "sqk", T_BANKS["sqk"])
            heads_in("mq", tok[0], tok[1], "x2", 256)
            guess("mq", slice(0, T * 4))
            hi_to(groups["hi"]["last"] + 3)
            turned(mqT, "mq", T_BANKS["mq"])
            act.wait_ge(*at("hgrn q", "0"))
            for t in range(T):
                a = sums(act, "hi", t)
                leave(scaled(vh[:, t, :], a[:, :], ACT.Copy, "x2", t), "hi", t)
            for s in STEPS2:
                if s in (17, 20):
                    hi_to(groups["hg"]["first"] + (s - 17) // 3 + 3)
                if s < 24:
                    exps(s)
                if s == 21:
                    for t in range(T):
                        a = sums(act, "hg", t)
                        scaled(tok[0][:, t, :], a[:, :], ACT.Copy, "x2", t)
                        leave(scaled(tok[1][:, t, :], a[:, :], ACT.Abs, "x2", t), "hg", t)
                if 17 <= s <= 24:
                    probs_out(s - 1, None)
            log_sigmoid("g", tok[0], tok[1], "hg")

            def decays(u):
                if u > 0:
                    act.wait_ge(*at("q decayed", f"{u - 1}"))
                    act.wait_ge(*at("k decayed", f"{u - 1}"))
                for b in range(2):
                    act.wait_ge(*at(f"bank{b} full", f"decay {u}"))
                    done(A(dec[:, 4 * b:4 * b + 4, :], X[b].rearrange("p (c t) -> p c t", t=P), ACT.Exp),
                         f"bank{b} free", f"decay {u}")

            decays(0)
            for u in range(8):
                if u % 2 == 1:
                    h = u // 2
                    act.wait_ge(*at("bank0 full", f"cross {h}"))
                    if h:
                        act.wait_ge(*at("bank1 full", f"hout {h - 1}"))
                    done(A(AT[:, 2, :], X[0][:, 0:P], ACT.Copy), "bank0 free", f"cross {h}")
                if u < 7:
                    decays(u + 1)
            act.wait_ge(*at("bank1 free", "hout 3"))
            act.wait_ge(*at("weights summed", "7"))
            act.wait_ge(*at("hgrn gate", "0"))
            done(A(tok[1][:, :, :], xn[:, :, 0:512], ACT.Square), "hgrn squares", "0")
            guess("hgrn", slice(0, T * 4))
            for b, blk in enumerate((4, 6, 0, 2)):
                act.wait_ge(*at(f"bank{b} full", f"out {blk}T"))
                done(A(ohi[:, blk:blk + 2, :], X[b].rearrange("p (c t) -> p c t", t=S), ACT.Copy), "out2 hi", f"{b}")
            hi_to(groups["wo2_1"]["last"])
            norm("ffn2", "wo2_1", hhi, None, None)
            ffn(2)

        @block.vector
        def _(dve):
            V = nc.vector
            nxt = [0]

            def lo_one(n, i=0):
                c = chunks[n]
                dve.wait_ge(sem("hi ready"), n + 1 + 4 * i)
                V.tensor_tensor(wlo[:, n % SPLIT, 0:c["nk"], 0:c["n"]], raw[:, n % RAW, 0:c["nk"], 0:c["n"]],
                                whi[:, n % SPLIT, 0:c["nk"], 0:c["n"]].bitcast(F32), ALU.subtract)\
                    .then_inc(sem("lo ready"), 1)

            def lo_to(n):
                while nxt[0] <= min(n, len(chunks) - 1):
                    lo_one(nxt[0])
                    nxt[0] += 1

            def root(step, cols):
                dve.wait_ge(*at("guess", step))
                done(V.tensor_tensor(nt[:, cols], rs[:, cols], rs[:, cols], ALU.mult), "newton", f"{step} a")
                dve.wait_ge(*at("newton", f"{step} a"))
                done(V.scalar_tensor_tensor(nt[:, cols], nt[:, cols], -0.5, ms[:, cols], ALU.mult, ALU.mult),
                     "newton", f"{step} b")
                dve.wait_ge(*at("newton", f"{step} b"))
                done(V.scalar_tensor_tensor(rs[:, cols], nt[:, cols], 1.5, rs[:, cols], ALU.add, ALU.mult),
                     "newton", f"{step} c")
                dve.wait_ge(*at("newton", f"{step} c"))

            def norm_gain(k, src, g, b, t, ready):
                for r in ready:
                    dve.wait_ge(*r)
                h = slice(b * CN, (b + 1) * CN)
                done(V.tensor_tensor(xn[:, t, h], src[:, t, h], g[:, h], ALU.mult), "tokens scaled", f"{k} {t} {b}")

            def norm_lo(k, hi, lo, b):
                for t in range(T):
                    n = 2 * t + b
                    dve.wait_ge(*at("feature hi", f"{k} {n}"))
                    h = (slice(None), slice(4 * b, 4 * b + 4), slice(t * P, (t + 1) * P))
                    done(V.tensor_tensor(lo[h], X[n].rearrange("p (c t) -> p c t", t=P), hi[h].bitcast(F32),
                                         ALU.subtract), f"bank{n} free", f"{k}T")

            def norm_root(k):
                for t in range(T):
                    dve.wait_ge(*at("squares", f"{k} {t}"))
                done(V.tensor_scalar(ms[:, rstd(k)], ss[:, rstd(k)], 1.0 / D, EPS, ALU.mult, ALU.add),
                     "mean square", k)
                root(k, rstd(k))

            def residual(name, k=None, gain_in=None):
                c = int(name[-1])
                for t in range(T):
                    a = sums(dve, name, t)
                    cols = x[:, t, c * CN:(c + 1) * CN]
                    leave(V.tensor_tensor(cols, a[:, :], cols, ALU.add), name, t)
                    if k:
                        norm_gain(k, x, gain, c, t, [gain_in, moved(name, t)])

            def norm(k, first, last, hi, lo, gain_in):
                lo_to(groups[first]["last"] + 2)
                residual(first, k, gain_in)
                norm_lo(k, hi, lo, 0)
                lo_to(groups[last]["last"] + 3)
                residual(last, k, gain_in)
                lo_to(groups[last]["last"] + 4)
                norm_lo(k, hi, lo, 1)
                norm_root(k)

            def head_norm(step, src, sqs, heads, gains, width=DH, rope=False, name=None):
                dve.wait_ge(*moved(name or step, 1))
                n = T * heads
                shape = [P, T, heads, width]
                view = src[:, :, 0:heads * width].rearrange("p t (h d) -> p t h d", d=width)
                done(V.tensor_reduce(ss[:, 0:n].rearrange("p (t h) -> p t h", t=T),
                                     sqs[:, :, 0:heads * width].rearrange("p t (h d) -> p t h d", d=width),
                                     AX.X, ALU.add), "head squares", step)
                dve.wait_ge(*at("head squares", step))
                done(V.tensor_scalar(ms[:, 0:n], ss[:, 0:n], 1.0 / width, EPS, ALU.mult, ALU.add), "mean square", step)
                root(step, slice(0, n))
                r = rs[:, 0:n].rearrange("p (t h) -> p t h", t=T).unsqueeze(3).to_broadcast(shape)
                done(V.tensor_tensor(view, view, r, ALU.mult), "heads scaled", step)
                dve.wait_ge(*at("heads scaled", step))
                if step == "mk":
                    dve.wait_ge(sem("small in"), 16 * 10)
                for n, (h0, h1, g) in enumerate(gains):
                    part = view[:, :, h0:h1, :]
                    b = g.unsqueeze(1).unsqueeze(1).to_broadcast([P, T, h1 - h0, width])
                    ins = V.tensor_tensor(part, part, b, ALU.mult)
                done(ins, "heads gained" if rope else "heads ready", step)

            def attn_max(j):
                whole, pr, b = head(j)[4], probs(j), j % 2
                dve.wait_ge(*at(f"bank{b} full", f"scores {j}"))
                if whole:
                    for t, c0 in ((1, 0), (0, S)):
                        ins = V.tensor_reduce(mx[:, j, t:t + 1], X[b][:, c0:c0 + S], AX.X, ALU.max)
                    done(ins, "row max", f"{j}")
                    dve.wait_ge(*at("row max", f"{j}"))
                else:
                    if j >= 2 and j not in (16, 17):
                        dve.wait_ge(*at("bank2 full", f"probs {j - 2} {unit_with(j - 2)}"))
                    mask = cst[:, C_CM:C_CM + 3 * P] if j < 16 else madd[:, :]
                    for t, c0, n in ((1, 0, S), (0, S, P)):
                        ins = V.tensor_tensor_reduce(out=pr[:, c0:c0 + n], in0=X[b][:, c0:c0 + n],
                                                     in1=mask[:, c0:c0 + n], scale=1.0, scalar=FLOOR, op0=ALU.add,
                                                     op1=ALU.max, accum_out=mx[:, j, t:t + 1])
                    done(ins, f"bank{b} free", f"scores {j}")
                    dve.wait_ge(*at(f"bank{b} free", f"scores {j}"))
                done(V.tensor_scalar(nm[:, j, :], mx[:, j, :], -DH ** -0.5, None, ALU.mult), "max ready", f"{j}")

            def attn_out(j):
                done(V.reciprocal(rc[:, j, :], sm[:, j, :]), "sum inverted", f"{j}")
                dve.wait_ge(*at("sum inverted", f"{j}"))
                dve.wait_ge(*at("bank3 full", f"pv {j}"))
                c = head(j)[3]
                done(V.tensor_tensor(xn[:, :, c:c + DH], X[3][:, 0:2 * DH].rearrange("p (t d) -> p t d", d=DH),
                                     rc[:, j, :].unsqueeze(2).to_broadcast([P, T, DH]), ALU.mult),
                     "bank3 free", f"pv {j}")

            def ffn(m):
                first = groups[f"g{m}_0"]["first"]

                def conv(i=0, short=""):
                    for b in range(1 if short else 2):
                        dve.wait_ge(*at("gate in", f"{m}{short} {b}", i))
                        blk = FT - 2 if short else 4 * i + 2 * b
                        for lag in (1, 2):
                            for c in range(2):
                                step = f"{m}{short} {b} {c}"
                                if lag == 2:
                                    dve.wait_ge(*at("tap added", step, i))
                                ins = V.scalar_tensor_tensor(
                                    y[:, 2 * b + c, lag:S], X[b][:, c * S:(c + 1) * S - lag],
                                    vT[:, bass.ds(blk + c + (2 - lag) * FT, 1)], y[:, 2 * b + c, lag:S],
                                    ALU.mult, ALU.add)
                                if lag == 1:
                                    done(ins, "tap added", step, i)
                        done(ins, f"bank{b} free", f"g{m}{short}T", i)

                def finish(i=0, short=""):
                    n = 2 if short else 4
                    step = f"{m}{short}"
                    dve.wait_ge(*at("gate ln", step, i))
                    done(V.scalar_tensor_tensor(e[:, 0:n, :], y[:, 0:n, :], 0.0, lg[:, 0:n, :], ALU.min,
                                                ALU.subtract), "gate log", step, i)
                    dve.wait_ge(*at("gate log", step, i))
                    for b in range(n // 2):
                        dve.wait_ge(*at(f"bank{2 + b} full", f"u{m}{short}T", i))
                        done(V.tensor_tensor(y[:, 2 * b:2 * b + 2, :], y[:, 2 * b:2 * b + 2, :],
                                             X[2 + b].rearrange("p (c t) -> p c t", t=S), ALU.mult),
                             f"bank{2 + b} free", f"u{m}{short}T", i)
                    dve.wait_ge(*at(f"bank{1 + n // 2} free", f"u{m}{short}T", i))
                    dve.wait_ge(*at("gate sigmoid", step, i))
                    done(V.tensor_tensor(y[:, 0:n, :], y[:, 0:n, :], e[:, 0:n, :], ALU.mult), "act ready", step, i)
                    dve.wait_ge(*at("act hi", step, i))
                    blks = slice(FT - 2, FT) if short else bass.ds(4 * i, 4)
                    done(V.tensor_tensor(alo[:, blks, :], y[:, 0:n, :], ahi[:, blks, :].bitcast(F32), ALU.subtract),
                         "act split", step, i)

                lo_to(first + 1)
                if m == 1:
                    conv(short="s")
                lo_to(first + 3)
                finish(short="s")
                with dve.Fori(0, PAIRS) as i:
                    cnt.enter()
                    lo_one(first + 4, i)
                    lo_one(first + 5, i)
                    if m == 1:
                        conv(i)
                    lo_one(first + 6, i)
                    lo_one(first + 7, i)
                    finish(i)
                cnt.leave(PAIRS)
                nxt[0] = first + 4 + 4 * PAIRS
                if m == 1:
                    norm("x2", "d1_0", "d1_1", hhi, hlo, gain_at(3))
                else:
                    for c in range(2):
                        lo_to(groups[f"d2_{c}"]["last"] + 3)
                        residual(f"d2_{c}")

            def gain_at(n):
                return sem("gain in"), 16 * n

            for b in range(2):
                for t in range(T):
                    norm_gain("mem", memx, memg, b, t, [(sem("memory gain in"), 16), (sem(f"mem {t} in"), 16)])
            norm_lo("mem", ohi, olo, 0)
            norm_lo("mem", ohi, olo, 1)
            lo_to(1)
            for b in range(2):
                for t in range(T):
                    norm_gain("x1", x, gain, b, t, [gain_at(1), (sem(f"x {t} in"), 16),
                                                    at(f"bank{2 * t + b} full", "memT")])
            norm_root("mem")
            norm_lo("x1", hhi, hlo, 0)
            lo_to(groups["mkv"]["last"] + 2)
            norm_lo("x1", hhi, hlo, 1)
            norm_root("x1")
            head_norm("mk", qraw, sq, 4, [(0, 4, hgain[:, 7, :])], name="mkv")
            for name, last in FIRST_GROUPS:
                lo_to(groups[name]["last"] + 3)
                if name[0] in "qk":
                    g = hgain[:, 2 * (name[1] == "b") + (name[0] == "k"), :]
                    head_norm(name, qraw, sq, 8, [(0, 8, g)], rope=name[1] == "a")
                if name == "f":
                    for t in range(T):
                        a = sums(dve, name, t)
                        leave(V.scalar_tensor_tensor(lf[:, t, :], a[:, 0:8], rs[:, rstd("x1", t)], bf[:, :], ALU.mult,
                                                     ALU.add), name, t)
                    dve.wait_ge(*moved("f", 1))
                    done(V.tensor_scalar(lt[:, 0], lf[:, :, :], -1.0, None, ALU.mult), "forget neg", "0")
                    dve.wait_ge(*at("forget neg", "0"))
                    done(V.tensor_tensor(lt[:, 0], lt[:, 0], lf[:, :, :], ALU.min), "forget", "-|z|")
                    dve.wait_ge(*at("forget ln", "0"))
                    done(V.scalar_tensor_tensor(lf[:, :, :], lf[:, :, :], 0.0, lt[:, 1], ALU.min, ALU.subtract),
                         "log forget", "0")

            for s in STEPS1:
                if s % 2 == 0 and s < 16:
                    lo_to(groups["gate0"]["first"] + s // 2 + 3)
                if s < 16:
                    attn_max(s)
                if s % 4 == 3 and s < 16:
                    n = s // 4
                    for t in range(T):
                        a = sums(dve, f"gate{n}", t)
                        if n == 0 and t == 0:
                            dve.wait_ge(sem("gate bias in"), 32)
                        cols = gates[:, t, n * CN:(n + 1) * CN]
                        leave(V.scalar_tensor_tensor(cols, a[:, :], rs[:, rstd("x1", t)], cols, ALU.mult, ALU.add),
                              f"gate{n}", t)
                if 2 <= s <= 17:
                    attn_out(s - 2)
                if s >= 4:
                    u = s - 4
                    dve.wait_ge(*at("out hi", f"{u}"))
                    h = (slice(None), u // 2, slice(u % 2 * P, (u % 2 + 1) * P))
                    done(V.tensor_tensor(olo[h], PT[:, 3 * P:4 * P], ohi[h].bitcast(F32), ALU.subtract),
                         "out split", f"{u}")
                if s % 4 == 1 and s >= 5:
                    n = s // 4 - 1
                    cols = gates[:, :, n * CN:(n + 1) * CN]
                    dve.wait_ge(*at("mix plus", f"{n}"))
                    done(V.reciprocal(cols, cols), "mix ready", f"{n}")

            for c in range(2):
                lo_to(groups[f"bra{c}"]["last"] + 3)
                if c == 0:
                    dve.wait_ge(*at("mix ready", "3"))
                for t in range(T):
                    a = sums(dve, f"bra{c}", t)
                    leave(V.tensor_tensor(xn[:, t, c * CN:(c + 1) * CN], a[:, :], gates[:, t, c * CN:(c + 1) * CN],
                                          ALU.mult), f"bra{c}", t)
                lo_to(groups[f"brb{c}"]["last"] + 3)
                for t in range(T):
                    a = sums(dve, f"brb{c}", t)
                    g = gates[:, t, D + c * CN:D + (c + 1) * CN]
                    leave(V.tensor_tensor(g, a[:, :], g, ALU.mult), f"brb{c}", t)
                    dve.wait_ge(*moved(f"brb{c}", t))
                    cols = xn[:, t, c * CN:(c + 1) * CN]
                    done(V.tensor_tensor(cols, cols, g, ALU.add), "merged", f"{c} {t}")
            for b in range(4):
                dve.wait_ge(*at("merged hi", f"{b}"))
                h = (slice(None), slice(4 * (b // 2), 4 * (b // 2) + 4), slice(b % 2 * P, (b % 2 + 1) * P))
                done(V.tensor_tensor(hlo[h], X[b].rearrange("p (c t) -> p c t", t=P), hhi[h].bitcast(F32),
                                     ALU.subtract), f"bank{b} free", "mergedT")
            norm("ffn1", "wo1_0", "wo1_1", ohi, olo, gain_at(2))
            ffn(1)

            lo_to(groups["hf"]["last"] + 3)
            dve.wait_ge(*at("hgrn ln", "f"))
            done(V.scalar_tensor_tensor(logf[:, :, :], tok[1][:, :, :], 0.0, vh[:, :, :], ALU.min, ALU.subtract),
                 "log f", "0")
            dve.wait_ge(*at("log f", "0"))
            done(V.tensor_tensor(tok[1][:, :, :], logf[:, :, :], tok[1][:, :, :], ALU.subtract), "hgrn k arg", "0")
            halves = ((1, slice(0, S)), (0, slice(S, S + P)))
            for h in range(8):
                dve.wait_ge(*at(f"bank{h % 2} free", f"index {h}"))
                for t, c in halves:
                    if h == 0:
                        ins = V.tensor_scalar(sco[:, c], rel[0][:, c], iw[:, t, h:h + 1], None, ALU.mult)
                    else:
                        if t == 1:
                            dve.wait_ge(*at("index summed", f"{h - 1}"))
                        ins = V.scalar_tensor_tensor(sco[:, c], rel[h % 2][:, c], iw[:, t, h:h + 1], sco[:, c],
                                                     ALU.mult, ALU.add)
                done(ins, "index summed", f"{h}")
            dve.wait_ge(*at("index summed", "7"))
            done(V.tensor_tensor(sco, sco, cst[:, C_CM:C_CM + 3 * P], ALU.add), "index masked", "0")
            dve.wait_ge(*at("index masked", "0"))
            for r in range(TOPK // 8):
                for t, c in halves:
                    src = sco if r == 0 else work
                    if r:
                        dve.wait_ge(*at("struck out", f"{r - 1} {t}"))
                    done(V.max(mx8[:, t, :], src[:, c]), "eight found", f"{r} {t}")
                for t, c in halves:
                    src = sco if r == 0 else work
                    dve.wait_ge(*at("eight found", f"{r} {t}"))
                    done(V.match_replace(work[:, c], mx8[:, t, :], src[:, c], FLOOR), "struck out", f"{r} {t}")
            for t, c in halves:
                dve.wait_ge(*at("struck out", f"{TOPK // 8 - 1} {t}"))
            done(V.tensor_scalar(madd[:, :], work, -2e38, BIG, ALU.is_lt, ALU.mult), "chosen", "0")
            dve.wait_ge(*at("chosen", "0"))
            done(V.scalar_tensor_tensor(madd[:, :], madd[:, :], -BIG, cst[:, C_CM:C_CM + 3 * P], ALU.add, ALU.add),
                 "chosen", "1")
            lo_to(groups["hq"]["last"] + 3)
            dve.wait_ge(*at("silu ln", "q"))
            done(V.scalar_tensor_tensor(vh[:, :, :], tok[0][:, :, :], 0.0, vh[:, :, :], ALU.min, ALU.subtract),
                 "silu log", "q")
            dve.wait_ge(*at("sigmoid", "q"))
            done(V.tensor_tensor(tok[0][:, :, :], tok[0][:, :, :], vh[:, :, :], ALU.mult), "hgrn q", "0")
            lo_to(groups["sqk"]["last"] + 3)
            head_norm("sqk", tok[0], tok[1], 8, [(0, 4, hgain[:, 4, :]), (4, 8, hgain[:, 5, :])])
            lo_to(groups["mq"]["last"] + 3)
            head_norm("mq", tok[0], tok[1], 4, [(0, 4, hgain[:, 6, :])])
            lo_to(groups["hi"]["last"] + 3)
            dve.wait_ge(*at("chosen", "1"))
            for s in STEPS2:
                if s in (17, 20):
                    lo_to(groups["hg"]["first"] + (s - 17) // 3 + 3)
                if s < 24:
                    attn_max(s)
                if 18 <= s:
                    attn_out(s - 2)
            dve.wait_ge(*at("silu ln", "g"))
            done(V.scalar_tensor_tensor(tok[1][:, :, :], tok[0][:, :, :], 0.0, tok[1][:, :, :], ALU.min, ALU.subtract),
                 "silu log", "g")
            dve.wait_ge(*at("sigmoid", "g"))
            done(V.tensor_tensor(tok[0][:, :, :], tok[0][:, :, :], tok[1][:, :, :], ALU.mult), "hgrn gate", "0")

            def q_decayed(u):
                h, t = u // 2, u % 2
                dve.wait_ge(*at("bank1 free", f"decay {u}"))
                if u:
                    dve.wait_ge(*at("bank3 full", f"pairs {u - 1}"))
                q = hqT[:, h, t * P:(t + 1) * P]
                ins = V.tensor_tensor(qd[:, :, :], dec[:, 1 - t:8 - t, :],
                                      q.unsqueeze(1).to_broadcast([P, LEVELS, P]), ALU.mult)
                if t == 1:
                    if h:
                        dve.wait_ge(*at("bank0 full", f"cross {h - 1}"))
                    ins = V.tensor_tensor(qx[:, :], dec[:, 7, :], q, ALU.mult)
                done(ins, "q decayed", f"{u}")

            q_decayed(0)
            for u in range(8):
                h, t = u // 2, u % 2
                masked = tok[1].rearrange("p t (l s) -> p (t l) s", s=P)
                if u:
                    dve.wait_ge(*at("weights summed", f"{u - 1}"))
                else:
                    dve.wait_ge(*at("hgrn gate", "0"))
                for b in range(2):
                    dve.wait_ge(*at(f"bank{2 + b} full", f"pairs {u}"))
                    done(V.tensor_tensor(masked[:, 4 * b:4 * b + 4, :], X[2 + b].rearrange("p (l s) -> p l s", s=P),
                                         hgc[:, C_HM + b * 512:C_HM + (b + 1) * 512].rearrange("p (l s) -> p l s", s=P),
                                         ALU.mult), f"bank{2 + b} free", f"pairs {u}")
                dve.wait_ge(*at("bank3 free", f"pairs {u}"))
                if h:
                    dve.wait_ge(*at("bank1 full", f"hout {h - 1}"))
                done(V.tensor_reduce(AT[:, t, :], masked.rearrange("p l s -> p s l"), AX.X, ALU.add),
                     "weights summed", f"{u}")
                if u < 7:
                    q_decayed(u + 1)
                if t == 1:
                    dve.wait_ge(*at("bank1 full", f"hout {h}"))
                    done(V.tensor_copy(xn[:, :, h * P:(h + 1) * P], X[1][:, 0:2 * P].rearrange("p (t d) -> p t d", d=P)),
                         "bank1 free", f"hout {h}")
            dve.wait_ge(*at("hgrn squares", "0"))
            view = xn[:, :, 0:512].rearrange("p t (h d) -> p t h d", d=P)
            done(V.tensor_reduce(ss[:, 0:8].rearrange("p (t h) -> p t h", t=T),
                                 tok[1].rearrange("p t (h d) -> p t h d", d=P), AX.X, ALU.add), "head squares", "hgrn")
            dve.wait_ge(*at("head squares", "hgrn"))
            done(V.tensor_scalar(ms[:, 0:8], ss[:, 0:8], 1.0 / P, EPS, ALU.mult, ALU.add), "mean square", "hgrn")
            root("hgrn", slice(0, 8))
            r = rs[:, 0:8].rearrange("p (t h) -> p t h", t=T).unsqueeze(3).to_broadcast([P, T, 4, P])
            done(V.tensor_tensor(view, view, r, ALU.mult), "heads scaled", "hgrn")
            dve.wait_ge(*at("heads scaled", "hgrn"))
            b = og[:, :].unsqueeze(1).unsqueeze(1).to_broadcast([P, T, 4, P])
            done(V.tensor_tensor(view, view, b, ALU.mult), "heads gained", "hgrn")
            dve.wait_ge(*at("heads gained", "hgrn"))
            done(V.tensor_tensor(xn[:, :, 0:512], xn[:, :, 0:512], tok[0][:, :, :], ALU.mult), "hgrn normed", "0")
            for b, blk in enumerate((4, 6, 0, 2)):
                dve.wait_ge(*at("out2 hi", f"{b}"))
                h = (slice(None), slice(blk, blk + 2), slice(None))
                done(V.tensor_tensor(olo[h], X[b].rearrange("p (c t) -> p c t", t=S), ohi[h].bitcast(F32),
                                     ALU.subtract), f"bank{b} free", f"out {blk}T")
            norm("ffn2", "wo2_0", "wo2_1", hhi, hlo, gain_at(4))
            ffn(2)

        @block.gpsimd
        def _(pool):
            G = nc.gpsimd

            def rope(name):
                pool.wait_ge(*at("heads gained", name))
                v = qraw[:, :, :].rearrange("p t (h d) -> p t h d", d=DH)
                x1, x2 = v[:, :, :, 0:8], v[:, :, :, 8:16]
                cs = cst[:, C_CS:C_CS + 16 * T].rearrange("p (t a d) -> p t a d", t=T, a=2)
                cos = cs[:, :, 0, :].unsqueeze(2).to_broadcast([P, T, 8, 8])
                sin = cs[:, :, 1, :].unsqueeze(2).to_broadcast([P, T, 8, 8])
                for n, (a, b) in enumerate(((x1, cos), (x2, sin), (x2, cos), (x1, sin))):
                    ins = G.tensor_tensor(rp[:, n], a, b, ALU.mult)
                done(ins, "rope products", name)
                pool.wait_ge(*at("rope products", name))
                G.tensor_tensor(x1, rp[:, 0], rp[:, 1], ALU.subtract)
                done(G.tensor_tensor(x2, rp[:, 2], rp[:, 3], ALU.add), "heads roped", name)

            def decay_rows(j):
                h = j - 8
                pool.wait_ge(*at("log forget", "0"))
                if h:
                    pool.wait_ge(*at(f"bank{(j - 1) % 2} full", f"scores {j - 1}"))
                t8, e8 = cst[:, C_T8:C_T8 + P], cst[:, C_E8:C_E8 + P]
                G.tensor_scalar(L[:, 0, :], t8, lf[:, 0, h:h + 1], None, ALU.mult)
                G.tensor_scalar(L[:, 1, :], e8, lf[:, 0, h:h + 1], None, ALU.mult)
                done(G.tensor_scalar(L[:, 2, :], t8, lf[:, 1, h:h + 1], None, ALU.mult), "decay rows", f"{j}")

            def plus_one(buf, ready, family, step):
                pool.wait_ge(*ready)
                done(G.tensor_scalar(buf, buf, 1.0, None, ALU.add), family, step)

            pool.wait_ge(sem("consts in"), 16)
            rope("qa")
            rope("ka")
            for s in STEPS1:
                if 8 <= s < 16:
                    decay_rows(s)
                if s % 4 == 3 and s < 16:
                    n = s // 4
                    plus_one(gates[:, :, n * CN:(n + 1) * CN], at("mix exp", f"{n}"), "mix plus", f"{n}")

            for u in range(8):
                h, t = u // 2, u % 2
                pool.wait_ge(*at("bank1 free", f"decay {u}"))
                if u:
                    pool.wait_ge(*at("bank3 full", f"pairs {u - 1}"))
                k = hkT[:, h, t * P:(t + 1) * P]
                ins = G.tensor_tensor(kd[:, :, :], dec[:, 1 - t:8 - t, :],
                                      k.unsqueeze(1).to_broadcast([P, LEVELS, P]), ALU.mult)
                if t == 0:
                    if h:
                        pool.wait_ge(*at("bank0 full", f"cross {h - 1}"))
                    ins = G.tensor_tensor(kx[:, :], dec[:, 0, :], k, ALU.mult)
                done(ins, "k decayed", f"{u}")

    return cnt.seen


SHAPES = {
    "x": (1, S, D), "attn_norm_g": (1, D), "w_in": (1, D, 5128), "b_forget": (1, 8), "b_gate": (1, 2, D),
    "moba_q_norm_g": (1, DH), "moba_k_norm_g": (1, DH), "fox_q_norm_g": (1, DH), "fox_k_norm_g": (1, DH),
    "w_branch_moba": (1, 512, D), "w_branch_fox": (1, 512, D), "w_out": (1, D, D), "ffn_norm_g": (1, D),
    "w_ffn_up": (1, D, 2 * DFF), "ffn_conv_w": (1, 3, DFF), "ffn_conv_b": (1, DFF), "w_ffn_down": (1, DFF, D),
    "mem_2": (1, S, D), "w_in_2": (1, D, 3656), "w_out_2": (1, D, D), "w_mem_kv_2": (1, D, 512),
    "norm_mix_2": (1, D), "norm_mem_2": (1, D), "norm_ffn_2": (1, D), "hg_out_gain_2": (1, P),
    "sa_q_gain_2": (1, DH), "sa_k_gain_2": (1, DH), "mem_q_gain_2": (1, DH), "mem_k_gain_2": (1, DH),
    "w_ffn_in_2": (1, D, 2 * DFF), "w_ffn_out_2": (1, DFF, D), "consts": (P, C_END), "hgrn": (P, C_HEND),
}


def build(nc, known):
    dram = {n: nc.dram_tensor(f"in_{n}", s, F32, kind="ExternalInput").ap() for n, s in SHAPES.items()}
    out = nc.dram_tensor("out", (1, S, D), F32, kind="ExternalOutput").ap()
    return program(nc, dram, out, known)


def kernel(**inputs):
    import concourse.bacc as bacc
    from concourse.bass_utils import run_bass_kernel_spmd

    def core():
        return bacc.Bacc("TRN2", target_bir_lowering=False, num_devices=1)

    known = build(core(), {})
    nc = core()
    assert build(nc, known) == known
    arrays = {f"in_{n}": np.ascontiguousarray(inputs[n]) for n in SHAPES if n in inputs}
    arrays["in_consts"], arrays["in_hgrn"] = constants()
    r = run_bass_kernel_spmd(nc, [arrays], core_ids=[0])
    return r.results[0]["out"]
```

```python
import numpy as np
from contextlib import ExitStack

import concourse.bass as bass
from concourse import mybir
from concourse.alu_op_type import AluOpType as ALU

ACT = mybir.ActivationFunctionType
AX = mybir.AxisListType
F32 = mybir.dt.float32
F32R = mybir.dt.float32r

P = 128
D = 1024
S = 256
T = S // P
DH = 64
DFF = 2816
KT = D // P
FT = DFF // P
CK = 2
PART = 2
PER = 4 * PART
CN = 512
RAW, SPLIT = 4, 8
PAIRS = DFF // CN
REST = DFF - PAIRS * CN
NORMS = ("mem", "x1", "ffn1", "x2", "ffn2")
LEVELS = 7
EPS = 1e-6
BIG = 1e30
FLOOR = -3e38
TOPK = min(256, S // 4)
IDX_SCALE = float(8 ** -0.5 * 64 ** -0.5)

C_ID = 0
C_CM = C_ID + P
C_T8 = C_CM + 3 * P
C_E8 = C_T8 + P
C_CS = C_E8 + P
C_END = C_CS + T * 16
C_HC = 0
C_HM = C_HC + 9 * P
C_HEND = C_HM + 8 * P


def constants():
    c, g = np.zeros((P, C_END), np.float32), np.zeros((P, C_HEND), np.float32)
    s, t = np.arange(P)[:, None], np.arange(P)[None, :]
    c[:, C_ID:C_ID + P] = s == t
    c[:, C_CM + P:C_CM + 2 * P] = np.where(t <= s, 0, -BIG)
    c[:, C_CM + 2 * P:C_CM + 3 * P] = np.where(t <= s, 0, -BIG)
    c[:, C_T8:C_T8 + P] = 8.0 * (s <= t)
    c[:, C_E8:C_E8 + P] = 8.0
    g[:, C_HC:C_HC + P] = s > t
    for n in range(LEVELS):
        half = 64 >> n
        mid = t // (2 * half) * (2 * half) + half - 1
        late = t > mid
        g[:, C_HC + (n + 1) * P:C_HC + (n + 2) * P] = np.where(late, (s > mid) & (s <= t), (s > t) & (s <= mid))
        same = s // (2 * half) == t // (2 * half)
        g[:, C_HM + n * P:C_HM + (n + 1) * P] = same & late & (s <= mid)
    g[:, C_HC + 8 * P:C_HC + 9 * P] = s <= t
    g[:, C_HM + 7 * P:C_HM + 8 * P] = s == t
    freq = (500000.0 ** (-np.arange(8) * 2.0 / 16)).astype(np.float32)
    angle = (np.arange(S, dtype=np.float32)[:, None] * freq[None, :]).astype(np.float64)
    for i in range(T):
        c[:, C_CS + 16 * i:C_CS + 16 * i + 8] = np.cos(angle[i * P:(i + 1) * P])
        c[:, C_CS + 16 * i + 8:C_CS + 16 * i + 16] = np.sin(angle[i * P:(i + 1) * P])
    return c, g, np.ascontiguousarray(np.eye(8, dtype=np.float32)[:, :, None].repeat(P, 2))


def plan():
    groups, chunks = {}, []

    def add(name, w, col, n, kt, lhs, k0=0):
        groups[name] = dict(name=name, w=w, col=col, n=n, kt=kt, lhs=lhs, k0=k0, idx=len(groups))
        stream(name)

    def stream(*names, part=PART, order=None):
        for name in names:
            if "at" in groups[name]:
                for _ in groups[name].pop("at"):
                    chunks.pop()
        order = order or range(0, groups[names[0]]["kt"], CK)
        for name in names:
            groups[name].update(part=part, ks=list(order), at=[])
        for a in range(0, len(order), part):
            for name in names:
                g = groups[name]
                for k in order[a:a + part]:
                    g["at"].append(len(chunks))
                    chunks.append(dict(w=g["w"], row=k * P, nk=min(CK, g["kt"] - k), col=g["col"], n=g["n"]))
        for name in names:
            g = groups[name]
            g["first"], g["last"] = g["at"][0], g["at"][-1]

    add("mkv", "w_mem_kv_2", 0, CN, KT, "o")
    for n, c in (("qa", 0), ("ka", 512), ("va", 1024), ("qb", 1536), ("kb", 2048)):
        add(n, "w_in", c, CN, KT, "h")
    add("vb", "w_in", 2560, CN, KT, "h")
    add("f", "w_in", 3072, 8, KT, "h")
    for n in range(4):
        add(f"gate{n}", "w_in", 3080 + CN * n, CN, KT, "h")
    for c in range(2):
        add(f"bra{c}", "w_branch_moba", CN * c, CN, 4, "o")
    for c in range(2):
        add(f"brb{c}", "w_branch_fox", CN * c, CN, 4, "o", 4)
    stream("brb0", "brb1", part=1)
    for c in range(2):
        add(f"wo1_{c}", "w_out", CN * c, CN, KT, "h")

    def ffn(m, up, down, gcol, ucol):
        lhs = "o" if m == 1 else "h"
        add(f"g{m}s", up, gcol + PAIRS * CN, REST, KT, lhs)
        add(f"u{m}s", up, ucol + PAIRS * CN, REST, KT, lhs)
        stream(f"g{m}s", f"u{m}s")
        for j in range(PAIRS):
            add(f"g{m}_{j}", up, gcol + CN * j, CN, KT, lhs)
            add(f"u{m}_{j}", up, ucol + CN * j, CN, KT, lhs)
        for c in range(2):
            add(f"d{m}_{c}", down, CN * c, CN, FT, "act")

    ffn(1, "w_ffn_up", "w_ffn_down", DFF, 0)
    for n, c, w in (("hf", 512, 512), ("hq", 0, 512), ("hi", 1024, 512), ("iqb", 3072, 328), ("sviq", 2560, 512),
                    ("mq", 3400, 256), ("sqk", 2048, 512), ("hg", 1536, 512)):
        add(n, "w_in_2", c, w, KT, "h")
        if n == "hq":
            stream("hf", "hq")
    for c in range(2):
        add(f"wo2_{c}", "w_out_2", CN * c, CN, KT, "o")
    stream("wo2_0", "wo2_1", part=1, order=[6, 0, 2, 4])
    ffn(2, "w_ffn_in_2", "w_ffn_out_2", 0, DFF)
    return groups, chunks


class Count:

    def __init__(self, known, sem):
        self.known, self.now, self.seen, self.sem, self.loop = known, {}, {}, sem, None

    def mark(self, ins, family, step, i=0):
        ins.then_inc(self.sem(family), 1)
        if family.endswith("free"):
            return
        n = self.now[family] = self.now.get(family, 0) + 1
        if (family, step) not in self.seen:
            self.seen[family, step] = [n, 0]
            if self.loop:
                self.loop[1].append((family, step))
        else:
            base, per = self.seen[family, step]
            assert isinstance(i, int) and n == base + per * i, (family, step, n, base, per, i)

    def value(self, family, step, i=0):
        family = family.replace("free", "full")
        if self.known and (family, step) not in self.known:
            raise KeyError((family, step))
        base, per = self.known.get((family, step), (1, 0))
        return base + i * per if per else base

    def at(self, family, step, i=0):
        return self.sem(family), self.value(family, step, i)

    def enter(self):
        self.loop = (dict(self.now), [])

    def leave(self, times):
        was, steps = self.loop
        per = {f: n - was.get(f, 0) for f, n in self.now.items()}
        for f, s in steps:
            self.seen[f, s][1] = per[f]
        for f in self.now:
            self.now[f] = was.get(f, 0) + per[f] * times
        self.loop = None


def program(nc, dram, out, known):
    groups, chunks = plan()
    ctx = ExitStack()
    sems = {}

    def sem(name):
        if name not in sems:
            sems[name] = ctx.enter_context(nc.semaphore("s_" + name.replace(" ", "_")))
        return sems[name]

    cnt = Count(known, sem)
    done, at = cnt.mark, cnt.at

    with ctx:
        def sb(name, shape, dt=F32, where=ctx):
            return where.enter_context(nc.sbuf_tensor("b_" + name, shape, dt))

        raw = sb("raw", [P, RAW, CK, CN])
        whi = sb("whi", [P, SPLIT, CK, CN], F32R)
        wlo = sb("wlo", [P, SPLIT, CK, CN], F32R)
        x = sb("x", [P, T, D])
        hhi = sb("hhi", [P, KT, S], F32R)
        hlo = sb("hlo", [P, KT, S], F32R)
        a0 = ExitStack()
        spare0, spare1 = [sb(f"spare{n}", [P, KT * S], where=a0) for n in range(2)]
        a0.close()
        ohi = sb("ohi", [P, KT, S], F32R)
        olo = sb("olo", [P, KT, S], F32R)
        cst = sb("cst", [P, C_END])
        gain = sb("gain", [P, D])
        xn = sb("xn", [P, T, D])
        mkT = sb("mkT", [P, 2, S])
        mv = sb("mv", [P, T, 256])
        hgain = sb("hgain", [P, 8, DH])
        vec = sb("vec", [4 * FT, P])
        vT = sb("vT", [P, 4 * FT])
        bf = sb("bf", [P, 8])
        ss = sb("ss", [P, 16 + 2 * len(NORMS)])
        ms = sb("ms", [P, 16 + 2 * len(NORMS)])
        rs = sb("rs", [P, 16 + 2 * len(NORMS)])
        nt = sb("nt", [P, 16 + 2 * len(NORMS)])
        mx = sb("mx", [P, 24, T])
        nm = sb("nm", [P, 24, T])
        sm = sb("sm", [P, 24, T])
        rc = sb("rc", [P, 24, T])
        lf = sb("lf", [P, T, 8])
        lt = sb("lt", [P, 2, T, 8])
        c8 = sb("c8", [8, S])
        rp = sb("rp", [P, 4, T, 8, 8])
        og = sb("og", [P, P])

        a1 = ExitStack()
        qT = [sb(f"qT{n}", [P, 4, S], where=a1) for n in range(2)]
        kT = [sb(f"kT{n}", [P, 4, S], where=a1) for n in range(2)]
        va = [sb(f"v{n}", [P, T, 512], where=a1) for n in range(2)]
        gates = sb("gates", [P, T, 2 * D], where=a1)
        qraws = [sb(f"qraw{n}", [P, T, 512], where=a1) for n in range(2)]
        sq = sb("sq", [P, T, 512], where=a1)
        Sm = [sb(f"Sm{n}", [P, 384], where=a1) for n in range(2)]
        PT = sb("PT", [P, 384], where=a1)
        pick = sb("pick", [8, 8, P], where=a1)
        raw_of = {"mk": qraws[1], "qa": qraws[0], "ka": qraws[1], "qb": qraws[0], "kb": qraws[1]}
        memx = gates[:, :, 0:D]
        memg = gates[:, 0, D:2 * D]
        a1.close()

        a2 = ExitStack()
        ahi = sb("ahi", [P, FT, S], F32R, where=a2)
        alo = sb("alo", [P, FT, S], F32R, where=a2)
        y = sb("y", [P, 4, S], where=a2)
        e = sb("e", [P, 4, S], where=a2)
        lg = sb("lg", [P, 4, S], where=a2)
        gtok, utok = xn[:, :, 0:CN], xn[:, :, CN:2 * CN]
        a2.close()

        a3 = ExitStack()
        logf = sb("logf", [P, T, 512], where=a3)
        vh = sb("vh", [P, T, 512], where=a3)
        hqT = sb("hqT", [P, 4, S], where=a3)
        hkT = sb("hkT", [P, 4, S], where=a3)
        dec = sb("dec", [P, 8, P], where=a3)
        qd, kd = sb("qd", [P, LEVELS, P], where=a3), sb("kd", [P, LEVELS, P], where=a3)
        masked = sb("masked", [P, 8, P], where=a3)
        kx, qx = sb("kx", [P, P], where=a3), sb("qx", [P, P], where=a3)
        AT = sb("AT", [P, 3, P], where=a3)
        ikT = sb("ikT", [P, S], where=a3)
        sqkT = sb("sqkT", [P, 4, S], where=a3)
        sv = sb("sv", [P, T, 256], where=a3)
        mqT = sb("mqT", [P, 2, S], where=a3)
        madd = sb("madd", [P, 384], where=a3)
        iw = sb("iw", [P, T, 8], where=a3)
        mx8 = sb("mx8", [P, T, 8], where=a3)
        tok = [sb("tokA", [P, T, 512], where=a3), sb("tokB", [P, T, 512], where=a3)]
        hgc = sb("hgc", [P, C_HEND], where=a3)
        abs_q = masked.rearrange("p l s -> p (l s)").rearrange("p (t n) -> p t n", t=T)
        iqT = spare0[:, 0:1024].rearrange("p (l t) -> p l t", t=S)
        rel = [spare0[:, 1024:1408], spare0[:, 1408:1792]]
        sco, work = spare1[:, 0:384], spare1[:, 384:768]
        ikk = spare1[:, 768:1024].rearrange("p (t n) -> p t n", t=T)
        itok = spare1[:, 1024:2048].rearrange("p (t n) -> p t n", t=T)
        Sn, PTn = [spare0[:, 0:512], spare0[:, 512:1024]], spare1[:, 1024:1536]
        flat = dec.rearrange("p l t -> p (l t)")
        So = [flat[:, 0:384], flat[:, 512:896]]
        PTo = kd.rearrange("p l t -> p (l t)")[:, 0:384]
        a3.close()

        acc = [[ctx.enter_context(nc.psum_tensor(f"acc{p}{t}", [P, 512], F32)) for t in range(T)] for p in range(2)]
        XX = ctx.enter_context(nc.psum_tensor("banks", [P, 4, 512], F32))
        X = [XX[:, n, :] for n in range(4)]
        ident = cst[:, C_ID:C_ID + P]
        lhs_of = {"h": (hhi, hlo), "o": (ohi, olo), "act": (ahi, alo)}

        def rstd(k, t=None):
            c = 16 + 2 * NORMS.index(k)
            return slice(c, c + 2) if t is None else slice(c + t, c + t + 1)

        def head(j):
            r = slice(64 * (j % 2), 64 * (j % 2) + 64)
            if j < 16:
                n, h = j // 8, j % 8
                return qT[n][r, h // 2, :], kT[n][r, h // 2, :], va[n][:, :, h * DH:h * DH + DH], j * DH, False
            h = (j - 16) % 4
            if j < 20:
                return sqkT[r, h // 2, :], sqkT[r, 2 + h // 2, :], sv[:, :, h * DH:h * DH + DH], 512 + h * DH, False
            return mqT[r, h // 2, :], mkT[r, h // 2, :], mv[:, :, h * DH:h * DH + DH], 768 + h * DH, True

        def probs(j):
            return (Sm if j < 16 else So if j < 20 else Sn)[j % 2]

        def probsT(j):
            return PT if j < 16 else PTo if j < 20 else PTn

        def part_end(name, c):
            g = groups[name]
            return g["at"][min(g["part"] * (c + 1), len(g["at"])) - 1]

        def block_of(j):
            return j // 2 if j < 16 else 4 + (j - 16) // 2

        T_BANKS = {"mk": [0], "qa": [2, 3], "ka": [0, 1], "qb": [2, 3], "kb": [2, 3], "sqk": [2, 3], "mq": [0]}
        HEADS1 = list(range(16))
        HEADS2 = [20, 21, 22, 23, 16, 17, 18, 19]

        def before(j, n):
            order = HEADS1 if j < 16 else HEADS2
            k = order.index(j) - n
            return order[k] if k >= 0 else None

        def moved(name, t, i=0):
            return sem(f"acc{groups[name]['idx'] % 2}{t} free"), groups[name]["idx"] // 2 + 1 + i

        def leave(ins, name, t, i=0):
            done(ins, f"acc{groups[name]['idx'] % 2}{t} free", name, i)

        def sums(eng, name, t, i=0):
            g = groups[name]
            if t == 0:
                eng.wait_ge(sem("tile 0 summed"), g["idx"] + 1 + 2 * i)
            else:
                eng.wait_ge(sem("chunk used"), g["last"] + 1 + PER * i)
            return acc[g["idx"] % 2][t]

        MIX1 = [("gemm", "qa", 0), ("gemm", "qa", 1), ("sums", "qa"), ("gemm", "ka", 0), ("turn", "mk"),
                ("gemm", "ka", 1), ("sums", "ka"), ("gemm", "va", 0), ("turn", "qa"), ("gemm", "va", 1), ("sums", "va"),
                ("gemm", "qb", 0), ("turn", "ka")]
        FILL = [[("qb", 1)], [("kb", 0)], [("kb", 1)], [("vb", 0)], [("vb", 1)], [("f", 0), ("f", 1)],
                *[[(f"gate{n}", c)] for n in range(4) for c in range(2)],
                [("bra0", 0)], [("bra1", 0)], [("brb0", 0)], [("brb1", 0)]]
        BEHIND = {0: [("sums", "qb")], 2: [("turn", "qb"), ("sums", "kb")], 4: [("turn", "kb"), ("sums", "vb")],
                  5: [("sums", "f")], 6: [("decay sums", 0)], 7: [("sums", "gate0")],
                  **{7 + 2 * n: [("mix", n - 1), ("sums", f"gate{n}")] for n in range(1, 4)},
                  14: [("mix", 3), ("sums", "bra0")], 15: [("sums", "bra1")]}
        for s, fill in enumerate(FILL):
            MIX1 += [("scores", s)] if s < 16 else []
            MIX1 += [("divide", s - 1)] if 1 <= s < 17 else []
            MIX1 += BEHIND.get(s - 1, [])
            MIX1 += [("gemm", *part) for part in fill]
            MIX1 += [("probs", s - 1)] if 1 <= s < 17 else []
            MIX1 += [("pv", s - 2)] if s >= 2 else []

        MIX2 = [("gemm", "hi", 0), ("exp", "k"), ("sums", "hq"),
                ("gemm", "hi", 1), ("exp", "q"), ("turn", "hk"), ("sums", "hi"),
                ("gemm", "iqb", 0), ("turn", "hq"), ("decay", 0),
                ("gemm", "iqb", 1), ("pairs", 0), ("decay", 1), ("sums", "iqb"),
                ("gemm", "sviq", 0), ("pairs", 1), ("decay", 2),
                ("gemm", "sviq", 1), ("hout", 0), ("pairs", 2), ("decay", 3), ("sums", "sviq"),
                ("gemm", "mq", 0), ("turn", "iq"), *[("index", h) for h in range(4)], ("pairs", 3), ("decay", 4),
                ("gemm", "mq", 1), *[("index", h) for h in range(4, 8)], ("hout", 1), ("masked", 0), ("sums", "mq"),
                ("gemm", "sqk", 0), ("pairs", 4), ("decay", 5), ("turn", "mq"), ("best", 0), ("best", 1),
                ("scores", 20), ("gemm", "sqk", 1), ("divide", 20), ("pairs", 5), ("probs", 20), ("decay", 6),
                ("scores", 21), ("divide", 21), ("best", 2), ("pv", 20), ("best", 3), ("sums", "sqk"),
                ("gemm", "hg", 0), ("probs", 21), ("hout", 2), ("pairs", 6), ("pv", 21), ("decay", 7),
                ("scores", 22), ("divide", 22), ("best", 4), ("best", 5), ("turn", "sqk"), ("scores", 23), ("divide", 23),
                ("gemm", "hg", 1), ("pairs", 7), ("probs", 22), ("pv", 22), ("probs", 23), ("pv", 23), ("hout", 3),
                ("sums", "hg"), ("best", 6), ("best", 7), ("chosen", 0), ("hgrn norm", 0), ("log", "g"), ("scores", 16),
                ("exp", "g"), ("gemm", "wo2_0", 0), ("gemm", "wo2_1", 0), ("divide", 16), ("hgrn norm", 1), ("probs", 16),
                ("scores", 17), ("divide", 17), ("pv", 16), ("out", 0), ("out", 2), ("probs", 17),
                ("scores", 18), ("divide", 18), ("gemm", "wo2_0", 1), ("pv", 17), ("probs", 18), ("gemm", "wo2_1", 1),
                ("scores", 19), ("divide", 19), ("gemm", "wo2_0", 2), ("pv", 18), ("probs", 19), ("gemm", "wo2_1", 2),
                ("pv", 19)]
        MIX2_LOW = (part_end("iqb", 1) + 3 * PART + 1,
                    1 + max(part_end(n, *rest) + 3 * PART for kind, n, *rest in MIX2 if kind == "gemm"))
        OUT_BANK = {0: 0, 2: 1}
        TURN2 = {"hk": (tok[1], [2, 3], hkT), "hq": (tok[0], [0, 1], hqT), "iq": (itok, [0, 1], iqT),
                 "sqk": (tok[0], [2, 3], sqkT), "mq": (tok[0], [0], mqT)}

        block = ctx.enter_context(nc.Block())

        @block.tensor
        def _(pe):
            def claim(bank, step, i=0):
                v = cnt.value(f"bank{bank} full", step, i) - 1
                if not isinstance(v, int) or v > 0:
                    pe.wait_ge(sem(f"bank{bank} free"), v)

            def full(ins, bank, step, i=0):
                done(ins, f"bank{bank} full", step, i)

            def gemm(name, c=None, i=0, norm=None):
                g = groups[name]
                hi, lo = lhs_of[g["lhs"]]
                p, turn, cols = g["idx"] % 2, g["idx"] // 2, g["n"]
                lastc = (g["kt"] - 1) // CK
                for c in range(lastc + 1) if c is None else range(g["part"] * c, min(g["part"] * (c + 1), lastc + 1)):
                    n = g["at"][c]
                    nk = min(CK, g["kt"] - g["ks"][c])
                    pe.wait_ge(sem("lo ready"), n + 1 + PER * i)
                    for t in range(T):
                        if c == 0 and turn > 0:
                            pe.wait_ge(sem(f"acc{p}{t} free"), turn + i)
                        if norm:
                            pe.wait_ge(*at(f"bank{2 * t + c // PART} free", f"{norm}T"))
                        for k in range(nk):
                            kk = g["k0"] + g["ks"][c] + k
                            a, b = hi[:, kk, t * P:(t + 1) * P], lo[:, kk, t * P:(t + 1) * P]
                            wh, wl = whi[:, n % SPLIT, k, 0:cols], wlo[:, n % SPLIT, k, 0:cols]
                            o = acc[p][t][:, 0:cols]
                            first, last = c == 0 and k == 0, c == lastc and k == nk - 1
                            nc.tensor.matmul(o, a, wh, start=first, stop=False)
                            nc.tensor.matmul(o, b, wh, start=False, stop=False)
                            mm = nc.tensor.matmul(o, a, wl, start=False, stop=last)
                        if t == T - 1:
                            mm.then_inc(sem("chunk used"), 1)
                        elif c == lastc:
                            mm.then_inc(sem("tile 0 summed"), 1)

            def norm_T(k, b, tiles=range(T)):
                for t in tiles:
                    pe.wait_ge(*at("tokens scaled", f"{k} {t} {b}"))
                    claim(2 * t + b, f"{k}T")
                    for c in range(4):
                        mm = nc.tensor.transpose(X[2 * t + b][:, c * P:(c + 1) * P],
                                                 xn[:, t, (4 * b + c) * P:(4 * b + c + 1) * P], ident)
                    full(mm, 2 * t + b, f"{k}T")

            def before_norm(k, name):
                gemm(name, 0)
                norm_T(k, 0)
                for c in range(1, -(-len(groups[name]["at"]) // PART)):
                    gemm(name, c)

            def after_norm(k, one, two):
                gemm(one, 0, norm=k)
                norm_T(k, 1, [0])
                gemm(two, 0, norm=k)
                norm_T(k, 1, [1])
                gemm(one, 1, norm=k)
                gemm(two, 1, norm=k)

            def tok_T(src, step, ready, banks, blocks=4, first=0):
                pe.wait_ge(*ready)
                for b in range(0, blocks, 2):
                    bank = banks[b // 2]
                    claim(bank, step)
                    for c in range(2):
                        for t in range(T):
                            cols = slice((first + b + c) * P, (first + b + c + 1) * P)
                            mm = nc.tensor.transpose(X[bank][:, c * S + t * P:c * S + (t + 1) * P], src[:, t, cols],
                                                     ident)
                    full(mm, bank, step)

            def attn_scores(j):
                q, k, _, _, whole = head(j)
                b = j % 2
                claim(b, f"scores {j}")
                for start, steps in ((0, ("qa", "ka")), (8, ("qb", "kb")), (16, ("sqk",)), (20, ("mq", "mk"))):
                    if j == start:
                        for step in steps:
                            pe.wait_ge(*at(f"bank{T_BANKS[step][-1]} free", f"{step}T"))
                fox = 8 <= j < 16
                n = S if whole else P
                if j == 8:
                    pe.wait_ge(*at("bank0 free", "decay sums"))
                    pe.wait_ge(sem("pick in"), 16)
                for t, c0, c1 in ((1, 0, S), (0, S, S + n)):
                    mm = nc.tensor.matmul(X[b][:, c0:c1], q[:, t * P:(t + 1) * P], k[:, 0:c1 - c0], start=True,
                                          stop=not fox)
                    if fox:
                        mm = nc.tensor.matmul(X[b][:, c0:c1], pick[:, j - 8, :],
                                              c8[:, 0:c1 - c0], start=False, stop=True)
                full(mm, b, f"scores {j}")

            def attn_T(j):
                claim(2, f"probs {j}")
                pe.wait_ge(*at("probs ready", f"{j}"))
                for c, to in enumerate((1, 3, 0, 2) if head(j)[4] else (1, 2, 0)):
                    mm = nc.tensor.transpose(X[2][:, to * P:(to + 1) * P], probs(j)[:, c * P:(c + 1) * P], ident)
                full(mm, 2, f"probs {j}")

            def attn_pv(j):
                _, _, v, _, whole = head(j)
                pe.wait_ge(*at("bank2 free", f"probs {j}"))
                for start, step in ((0, "va"), (8, "vb"), (16, "sviq"), (20, "mkv")):
                    if j == start:
                        pe.wait_ge(*moved(step, 1))
                claim(3, f"pv {j}")
                pt, o = probsT(j), X[3][64 * (j % 2):64 * (j % 2) + 64, :]
                nc.tensor.matmul(o[:, 0:S], v[:, 0, :], pt[:, 0:S], start=True, stop=False)
                c0 = 0 if whole else P
                mm = nc.tensor.matmul(o[:, c0:S], v[:, 1, :], pt[:, S:S + S - c0], start=False, stop=True)
                full(mm, 3, f"pv {j}")

            def ffn_T(m, which, i=0, short=""):
                src, base = (gtok, 0) if which == "g" else (utok, 2)
                for t in range(T):
                    pe.wait_ge(*moved(f"{which}{m}{short or '_0'}", t, i))
                for b in range(1 if short else 2):
                    step = f"{which}{m}{short}T"
                    claim(base + b, step, i)
                    for c in range(2):
                        for t in range(T):
                            mm = nc.tensor.transpose(X[base + b][:, c * S + t * P:c * S + (t + 1) * P],
                                                     src[:, t, (2 * b + c) * P:(2 * b + c + 1) * P], ident)
                    full(mm, base + b, step, i)

            def ffn(m):
                after_norm(f"ffn{m}", f"g{m}s", f"u{m}s")
                ffn_T(m, "g", short="s")
                gemm(f"g{m}_0", 0)
                ffn_T(m, "u", short="s")
                gemm(f"g{m}_0", 1)

                def pair(i, last):
                    gemm(f"u{m}_0", 0, i)
                    ffn_T(m, "g", i)
                    gemm(f"u{m}_0", 1, i)
                    if not last:
                        gemm(f"g{m}_0", 0, i + 1)
                    else:
                        pe.wait_ge(*at("act split", f"{m}", 0))
                        gemm(f"d{m}_0", 0)
                    ffn_T(m, "u", i)
                    if not last:
                        gemm(f"g{m}_0", 1, i + 1)

                with pe.Fori(0, PAIRS - 1) as i:
                    cnt.enter()
                    pair(i, False)
                cnt.leave(PAIRS - 1)
                pair(PAIRS - 1, True)
                for c in range(1, -(-FT // (CK * PART))):
                    if c < PAIRS:
                        pe.wait_ge(*at("act split", f"{m}", c))
                    gemm(f"d{m}_0", c)
                if m == 1:
                    before_norm("x2", "d1_1")
                else:
                    gemm("d2_1")

            pe.wait_ge(sem("identity in"), 16)

            norm_T("mem", 0)
            norm_T("mem", 1)
            gemm("mkv", 0, norm="mem")
            norm_T("x1", 0)
            gemm("mkv", 1, norm="mem")
            norm_T("x1", 1)
            pe.wait_ge(sem("vec in"), 32)
            claim(0, "vecT")
            full(nc.tensor.transpose(X[0][:, 0:4 * FT], vec[:, :], ident[0:4 * FT, 0:4 * FT]), 0, "vecT")
            pe.wait_ge(sem("consts in"), 16)
            for kind, n, *rest in MIX1:
                if kind == "gemm":
                    if n == "bra0":
                        pe.wait_ge(*at("bank3 free", "pv 7"))
                    elif n == "brb0":
                        pe.wait_ge(*at("bank3 free", "pv 11"))
                    gemm(n, *rest, norm="x1" if n == "qa" else None)
                elif kind == "turn":
                    tok_T(raw_of[n], f"{n}T", at("heads roped" if n in ("qa", "ka") else "heads ready", n), T_BANKS[n],
                          2 * len(T_BANKS[n]))
                elif kind == "decay sums":
                    pe.wait_ge(*at("log forget", "0"))
                    claim(0, "decay sums")
                    nc.tensor.matmul(X[0][0:8, 0:S], lf[:, 0, :], cst[:, C_T8:C_T8 + S], start=True, stop=False)
                    full(nc.tensor.matmul(X[0][0:8, P:S], lf[:, 1, :], cst[:, C_T8:C_T8 + P], start=False, stop=True),
                         0, "decay sums")
                elif kind == "scores":
                    attn_scores(n)
                elif kind == "probs":
                    attn_T(n)
                elif kind == "pv":
                    attn_pv(n)
            pe.wait_ge(*at("bank3 free", "pv 15"))
            gemm("brb0", 1)
            gemm("brb1", 1)
            def merged_T(c):
                for t in range(T):
                    bank = 2 * c + t
                    pe.wait_ge(*at("merged", f"{c} {t}"))
                    claim(bank, "mergedT")
                    for b in range(4):
                        mm = nc.tensor.transpose(X[bank][:, b * P:(b + 1) * P],
                                                 xn[:, t, c * CN + b * P:c * CN + (b + 1) * P], ident)
                    full(mm, bank, "mergedT")

            merged_T(0)
            pe.wait_ge(*at("bank1 free", "mergedT"))
            gemm("wo1_0", 0)
            merged_T(1)
            pe.wait_ge(*at("bank3 free", "mergedT"))
            gemm("wo1_0", 1)
            before_norm("ffn1", "wo1_1")
            ffn(1)

            def index(h):
                r = slice(64 * (h % 2), 64 * (h % 2) + 64)
                claim(h % 2, f"index {h}")
                q = iqT[r, h // 2, :]
                nc.tensor.matmul(X[h % 2][:, 0:S], q[:, P:S], ikT[r, :], start=True, stop=True)
                mm = nc.tensor.matmul(X[h % 2][:, S:S + P], q[:, 0:P], ikT[r, 0:P], start=True, stop=True)
                full(mm, h % 2, f"index {h}")

            def turn(name):
                src, banks, _ = TURN2[name]
                ready = {"hk": ("hgrn k", "0"), "hq": ("hgrn q", "0")}.get(name, ("heads ready", name))
                tok_T(src, f"{name}T", moved("sviq", 1) if name == "iq" else at(*ready), banks, 2 * len(banks))
                if name == "iq":
                    claim(2, "ikT")
                    for t in range(T):
                        mm = nc.tensor.transpose(X[2][:, t * P:(t + 1) * P], ikk[:, t, :], ident)
                    full(mm, 2, "ikT")
                    pe.wait_ge(*at("bank2 free", "ikT"))

            def hgrn_decay(u):
                h, t = u // 2, u % 2
                pe.wait_ge(*at("log f", "0"))
                if u == 0:
                    pe.wait_ge(sem("hgrn table in"), 16)
                for b in range(2):
                    claim(b, f"decay {u}")
                    c = C_HC + t * P + b * 512
                    full(nc.tensor.matmul(X[b][:, :], logf[:, t, h * P:(h + 1) * P], hgc[:, c:c + 512],
                                          start=True, stop=True), b, f"decay {u}")

            def hgrn_pairs(u):
                h, t = u // 2, u % 2
                pe.wait_ge(*at("q decayed", f"{u}"))
                pe.wait_ge(*at("k decayed", f"{u}"))
                for b in range(2):
                    claim(2 + b, f"pairs {u}")
                    for c in range(4):
                        n, ts = 4 * b + c, slice(t * P, (t + 1) * P)
                        k, q = (kd[:, n, :], qd[:, n, :]) if n < LEVELS else (hkT[:, h, ts], hqT[:, h, ts])
                        mm = nc.tensor.matmul(X[2 + b][:, c * P:(c + 1) * P], k, q, start=True, stop=True)
                    full(mm, 2 + b, f"pairs {u}")
                if t == 1:
                    claim(0, f"cross {h}")
                    full(nc.tensor.matmul(X[0][:, 0:P], kx[:, :], qx[:, :], start=True, stop=True), 0, f"cross {h}")

            def hgrn_out(h):
                pe.wait_ge(*moved("hi", 1))
                pe.wait_ge(*at("weights summed", f"{2 * h + 1}"))
                pe.wait_ge(*at("bank0 free", f"cross {h}"))
                claim(1, f"hout {h}")
                v = vh[:, :, h * P:(h + 1) * P]
                nc.tensor.matmul(X[1][:, 0:P], AT[:, 0, :], v[:, 0, :], start=True, stop=True)
                nc.tensor.matmul(X[1][:, P:2 * P], AT[:, 1, :], v[:, 1, :], start=True, stop=False)
                full(nc.tensor.matmul(X[1][:, P:2 * P], AT[:, 2, :], v[:, 0, :], start=False, stop=True), 1, f"hout {h}")

            after_norm("x2", "hf", "hq")
            for kind, n, *rest in MIX2:
                if kind == "gemm":
                    if (n, rest[0]) == ("wo2_0", 0):
                        pe.wait_ge(*at("bank3 free", "pv 23"))
                    if (n, rest[0]) == ("wo2_0", 1):
                        for blk, bank in OUT_BANK.items():
                            pe.wait_ge(*at(f"bank{bank} free", f"out {blk}T"))
                    gemm(n, *rest)
                elif kind == "turn":
                    turn(n)
                elif kind == "index":
                    index(n)
                elif kind == "decay":
                    hgrn_decay(n)
                elif kind == "pairs":
                    hgrn_pairs(n)
                elif kind == "hout":
                    hgrn_out(n)
                elif kind == "scores":
                    attn_scores(n)
                elif kind == "probs":
                    attn_T(n)
                elif kind == "pv":
                    attn_pv(n)
                elif kind == "out":
                    tok_T(xn, f"out {n}T", at("hgrn normed", "0"), [OUT_BANK[n]], 2, n)
            pe.wait_ge(*at("bank3 free", "pv 19"))
            gemm("wo2_0", 3)
            gemm("wo2_1", 3)
            norm_T("ffn2", 0)
            ffn(2)

        @block.sync
        def _(sp):
            sp.dma_start(ident, dram["consts"][:, C_ID:C_ID + P]).then_inc(sem("identity in"), 16)
            sp.dma_start(memg, dram["norm_mem_2"][0, :].partition_broadcast(P)).then_inc(sem("memory gain in"), 16)
            for t in range(T):
                sp.dma_start(memx[:, t, :], dram["mem_2"][0, t * P:(t + 1) * P, :]).then_inc(sem(f"mem {t} in"), 16)
            def small(dst, name, family):
                sp.dma_start(dst, dram[name][0, :].partition_broadcast(P)).then_inc(sem(family), 16)

            for n, c in enumerate(chunks):
                if n == PART:
                    sp.dma_start(gain[:, :], dram["attn_norm_g"][0, :].partition_broadcast(P))\
                      .then_inc(sem("gain in"), 16)
                    for t in range(T):
                        sp.dma_start(x[:, t, :], dram["x"][0, t * P:(t + 1) * P, :]).then_inc(sem(f"x {t} in"), 16)
                if n == RAW:
                    sp.dma_start(cst[:, P:], dram["consts"][:, P:]).then_inc(sem("consts in"), 16)
                    sp.dma_start(vec[0:3 * FT, :], dram["ffn_conv_w"][0].rearrange("a (b p) -> (a b) p", p=P))\
                       .then_inc(sem("vec in"), 16)
                    sp.dma_start(vec[3 * FT:4 * FT, :], dram["ffn_conv_b"][0].rearrange("(b p) -> b p", p=P))\
                       .then_inc(sem("vec in"), 16)
                    small(bf[:, :], "b_forget", "small in")
                    small(og[:, :], "hg_out_gain_2", "small in")
                    for head, name in enumerate(("moba_q_norm_g", "moba_k_norm_g", "fox_q_norm_g", "fox_k_norm_g",
                                              "sa_q_gain_2", "sa_k_gain_2", "mem_q_gain_2", "mem_k_gain_2")):
                        small(hgain[:, head, :], name, "small in")
                    sp.dma_start(pick[:, :, :], dram["pick"]).then_inc(sem("pick in"), 16)
                if n >= RAW:
                    sp.wait_ge(sem("lo ready"), n - RAW + 1)
                src = dram[c["w"]][0, c["row"]:c["row"] + c["nk"] * P, c["col"]:c["col"] + c["n"]]
                sp.dma_start(raw[:, n % RAW, 0:c["nk"], 0:c["n"]], src.rearrange("(k p) n -> p k n", p=P))\
                  .then_inc(sem(f"raw {n % RAW} in"), 16)
            for c in range(2):
                for t in range(T):
                    sp.wait_ge(*moved(f"d2_{c}", t))
                    sp.dma_start(out[0, t * P:(t + 1) * P, c * CN:(c + 1) * CN], x[:, t, c * CN:(c + 1) * CN])\
                      .then_inc(sem("out written"), 16)
            sp.wait_ge(sem("out written"), 16 * 2 * T)

        @block.scalar
        def _(act):
            A = nc.scalar.activation
            nc.scalar.preload_act_table_set("natural_log_exp_and_others")

            def row(dst, name, family):
                act.dma_start(dst, dram[name][0, :].partition_broadcast(P)).then_inc(sem(family), 16)

            nxt = [0]

            def hi_one(n, i=0):
                c = chunks[n]
                act.wait_ge(sem(f"raw {n % RAW} in"), 16 * (n // RAW + 1) + 16 * (PER // RAW) * i)
                if n >= SPLIT:
                    act.wait_ge(sem("chunk used"), n - SPLIT + 1 + PER * i)
                A(whi[:, n % SPLIT, 0:c["nk"], 0:c["n"]], raw[:, n % RAW, 0:c["nk"], 0:c["n"]], ACT.Copy)\
                    .then_inc(sem("hi ready"), 1)

            def hi_to(n):
                while nxt[0] <= min(n, len(chunks) - 1):
                    hi_one(nxt[0])
                    nxt[0] += 1

            def guess(step, cols):
                act.wait_ge(*at("mean square", step))
                done(A(rs[:, cols], ms[:, cols], ACT.Ln), "log", step)
                act.wait_ge(*at("log", step))
                done(A(rs[:, cols], rs[:, cols], ACT.Exp, scale=-0.5), "guess", step)

            def norm_squares(k, src, ready, junk):
                for t in range(T):
                    act.wait_ge(*ready(t))
                    if t:
                        act.wait_ge(*at("squares", f"{k} 0"))
                    done(A(junk, src[:, t, :], ACT.Square, accum_out=ss[:, rstd(k, t)]), "squares", f"{k} {t}")

            def norm_hi(k, hi, b):
                for t in range(T):
                    act.wait_ge(*at(f"bank{2 * t + b} full", f"{k}T"))
                    done(A(hi[:, 4 * b:4 * b + 4, t * P:(t + 1) * P],
                           X[2 * t + b].rearrange("p (c t) -> p c t", t=P), ACT.Copy),
                         "feature hi", f"{k} {2 * t + b}")

            def scaled(dst, a, func, k, t):
                return A(dst, a, func, scale=rs[:, rstd(k, t)])

            def root_in(k):
                act.wait_ge(*at("newton", f"{k} c"))

            def norm(k, last, hi, name, gain_name):
                norm_hi(k, hi, 0)
                hi_to(groups[last]["last"] + 4 * PART)
                norm_squares(k, x, lambda t: moved(last, t), y.rearrange("p c t -> p (c t)"))
                norm_hi(k, hi, 1)
                guess(k, rstd(k))
                if gain_name:
                    next_gain(k, gain_name)
                root_in(k)

            def next_gain(k, name):
                act.wait_ge(*at("tokens scaled", f"{k} 1 1"))
                row(gain[:, :], name, "gain in")

            def heads_in(name, src, sqs, k, n=512):
                last = {"qa": "mk", "ka": "qa", "qb": "ka", "kb": "qb", "mq": None, "sqk": "mq"}.get(name)
                if last:
                    act.wait_ge(*at("head squares", last))
                for t in range(T):
                    a = sums(act, name, t)
                    scaled(src[:, t, 0:n], a[:, 0:n], ACT.Copy, k, t)
                    if name == "mkv":
                        scaled(mv[:, t, :], a[:, 256:512], ACT.Copy, k, t)
                    leave(scaled(sqs[:, t, 0:n], a[:, 0:n], ACT.Square, k, t), name, t)

            def turned(dst, step, banks):
                for n, b in enumerate(banks):
                    act.wait_ge(*at(f"bank{b} full", f"{step}T"))
                    done(A(dst[:, 2 * n:2 * n + 2, :], X[b].rearrange("p (c t) -> p c t", t=S), ACT.Copy),
                         f"bank{b} free", f"{step}T")

            def exps(j):
                act.wait_ge(*at("max ready", f"{j}"))
                whole, pr, b = head(j)[4], probs(j), j % 2
                if whole and before(j, 2):
                    act.wait_ge(*at("bank2 full", f"probs {before(j, 2)}"))
                for t, c0, n in ((1, 0, S), (0, S, S if whole else P)):
                    src = X[b][:, c0:c0 + n] if whole else pr[:, c0:c0 + n]
                    ins = A(pr[:, c0:c0 + n], src, ACT.Exp, bias=nm[:, j, t:t + 1], scale=DH ** -0.5,
                            accum_out=sm[:, j, t:t + 1])
                if whole:
                    done(ins, f"bank{b} free", f"scores {j}")
                else:
                    done(ins, "exps ready", f"{j}")

            def probs_out(j):
                act.wait_ge(*at("bank2 full", f"probs {j}"))
                last = before(j, 1)
                if last is not None:
                    act.wait_ge(*at("bank3 full", f"pv {last}"))
                n = 4 * P if head(j)[4] else 3 * P
                done(A(probsT(j)[:, 0:n], X[2][:, 0:n], ACT.Copy), "bank2 free", f"probs {j}")

            def pv_out(j):
                o, blk = slice(64 * (j % 2), 64 * (j % 2) + 64), block_of(j)
                act.wait_ge(*at("bank3 full", f"pv {j}"))
                done(A(ohi[o, blk, :], X[3][o, 0:S], ACT.Copy), "out hi", f"{j}")

            def ffn(m):
                first = groups[f"g{m}_0"]["first"]

                def move(which, i=0, short=""):
                    name, n = f"{which}{m}{short or '_0'}", REST if short else CN
                    dst, base = (gtok, 0) if which == "g" else (utok, 2)
                    for t in range(T):
                        a = sums(act, name, t, i)
                        if not short and t == 0:
                            for b in range(base, base + 2):
                                v = cnt.value(f"bank{b} full", f"{which}{m}T", i) - 1
                                act.wait_ge(sem(f"bank{b} full"), v if known else 1)
                        leave(scaled(dst[:, t, 0:n], a[:, 0:n], ACT.Copy, f"ffn{m}", t), name, t, i)

                def gate_in(i=0, short=""):
                    v = cnt.value("act split", f"{m}{short}", i) - 1
                    if not isinstance(v, int) or v > 0:
                        act.wait_ge(sem("act split"), v)
                    for b in range(1 if short else 2):
                        act.wait_ge(*at(f"bank{b} full", f"g{m}{short}T", i))
                        blk = FT - 2 if short else 4 * i + 2 * b
                        if m == 1:
                            for c in range(2):
                                ins = A(y[:, 2 * b + c, :], X[b][:, c * S:(c + 1) * S], ACT.Identity,
                                        bias=vT[:, bass.ds(blk + c + 3 * FT, 1)],
                                        scale=vT[:, bass.ds(blk + c + 2 * FT, 1)])
                            done(ins, "gate in", f"{m}{short} {b}", i)
                        else:
                            done(A(y[:, 2 * b:2 * b + 2, :], X[b].rearrange("p (c t) -> p c t", t=S), ACT.Copy),
                                 f"bank{b} free", f"g{m}{short}T", i)

                def finish(i=0, short=""):
                    n = 2 if short else 4
                    act.wait_ge(*at(f"bank{0 if short else 1} free", f"g{m}{short}T", i))
                    done(A(lg[:, 0:n, :], y[:, 0:n, :], ACT.Abs), "gate abs", f"{m}{short}", i)
                    act.wait_ge(*at("gate abs", f"{m}{short}", i))
                    done(A(lg[:, 0:n, :], lg[:, 0:n, :], ACT.Exp, scale=-1.0), "gate exp", f"{m}{short}", i)
                    act.wait_ge(*at("gate exp", f"{m}{short}", i))
                    done(A(lg[:, 0:n, :], lg[:, 0:n, :], ACT.Ln, bias=1.0), "gate ln", f"{m}{short}", i)
                    act.wait_ge(*at("gate log", f"{m}{short}", i))
                    done(A(e[:, 0:n, :], e[:, 0:n, :], ACT.Exp), "gate sigmoid", f"{m}{short}", i)
                    act.wait_ge(*at("act ready", f"{m}{short}", i))
                    dst = ahi[:, FT - 2:FT, :] if short else ahi[:, bass.ds(4 * i, 4), :]
                    done(A(dst, y[:, 0:n, :], ACT.Copy), "act hi", f"{m}{short}", i)

                hi_to(first + PART - 1)
                move("g", short="s")
                move("u", short="s")
                hi_to(first + 2 * PART - 1)
                gate_in(short="s")
                hi_to(first + 4 * PART - 1)
                finish(short="s")
                with act.Fori(0, PAIRS) as i:
                    cnt.enter()
                    move("g", i)
                    for n in range(PER, PER + 2 * PART):
                        hi_one(first + n, i)
                    gate_in(i)
                    for n in range(PER + 2 * PART, 2 * PER):
                        hi_one(first + n, i)
                    move("u", i)
                    finish(i)
                cnt.leave(PAIRS)
                nxt[0] = first + PER + PER * PAIRS
                hi_to(groups[f"d{m}_0"]["last"] + 2 * PART)
                if m == 1:
                    norm("x2", "d1_1", hhi, None, "norm_ffn_2")
                else:
                    hi_to(groups["d2_1"]["last"])

            def log_one_plus(name, buf):
                act.wait_ge(*moved(name, 1))
                done(A(buf[:, :, :], buf[:, :, :], ACT.Exp, scale=-1.0), "one plus exp", name)
                act.wait_ge(*at("one plus exp", name))
                done(A(buf[:, :, :], buf[:, :, :], ACT.Ln, bias=1.0), "one plus ln", name)

            norm_hi("mem", ohi, 0)
            norm_hi("mem", ohi, 1)
            hi_to(2 * PART - 1)
            norm_squares("mem", memx, lambda t: (sem(f"mem {t} in"), 16), sq.rearrange("p t n -> p (t n)"))
            guess("mem", rstd("mem"))
            for t in range(T):
                act.wait_ge(*at("tokens scaled", "mem 1 1"))
                act.dma_start(gates[:, t, :], dram["b_gate"][0].rearrange("a d -> (a d)").partition_broadcast(P))\
                   .then_inc(sem("gate bias in"), 16)
            norm_hi("x1", hhi, 0)
            hi_to(groups["mkv"]["last"] + 2 * PART)
            norm_hi("x1", hhi, 1)
            act.wait_ge(*at("squares", "mem 1"))
            norm_squares("x1", x, lambda t: (sem(f"x {t} in"), 16), sq.rearrange("p t n -> p (t n)"))
            guess("x1", rstd("x1"))
            next_gain("x1", "ffn_norm_g")
            root_in("mem")
            act.wait_ge(*at("squares", "x1 1"))
            heads_in("mkv", raw_of["mk"], sq, "mem", 256)
            guess("mk", slice(0, T * 4))
            act.wait_ge(*at("bank0 full", "vecT"))
            done(A(vT[:, :], X[0][:, 0:4 * FT], ACT.Copy), "bank0 free", "vecT")
            root_in("x1")
            where = {"mk": mkT, "qa": qT[0], "ka": kT[0], "qb": qT[1], "kb": kT[1]}
            for kind, n, *rest in MIX1:
                if kind == "gemm":
                    hi_to(part_end(n, *rest) + 3 * PART)
                elif kind == "turn":
                    turned(where[n], n, T_BANKS[n])
                elif kind == "decay sums":
                    act.wait_ge(*at("bank0 full", "decay sums"))
                    done(A(c8[:, :], X[0][0:8, 0:S], ACT.Copy, scale=-1.0), "bank0 free", "decay sums")
                elif kind == "sums" and n in where:
                    heads_in(n, raw_of[n], sq, "x1")
                    guess(n, slice(0, T * 8))
                elif kind == "sums" and n in ("va", "vb"):
                    for t in range(T):
                        a = sums(act, n, t)
                        leave(scaled(va[n == "vb"][:, t, :], a[:, :], ACT.Copy, "x1", t), n, t)
                elif kind == "sums" and n == "f":
                    act.wait_ge(*at("forget", "-|z|"))
                    done(A(lt[:, 0], lt[:, 0], ACT.Exp), "forget exp", "0")
                    act.wait_ge(*at("forget exp", "0"))
                    done(A(lt[:, 1], lt[:, 0], ACT.Ln, bias=1.0), "forget ln", "0")
                elif kind == "sums" and n[:4] == "gate":
                    g = int(n[4:])
                    act.wait_ge(*moved(n, 1))
                    act.wait_ge(*(at("mix log", f"{g - 1}") if g else at("head squares", "kb")))
                    done(A(sq[:, :, :], gates[:, :, g * CN:(g + 1) * CN], ACT.Abs), "mix abs", f"{g}")
                    act.wait_ge(*at("mix abs", f"{g}"))
                    done(A(sq[:, :, :], sq[:, :, :], ACT.Exp, scale=-1.0), "mix exp", f"{g}")
                    act.wait_ge(*at("mix exp", f"{g}"))
                    done(A(sq[:, :, :], sq[:, :, :], ACT.Ln, bias=1.0), "mix ln", f"{g}")
                elif kind == "mix":
                    cols = gates[:, :, n * CN:(n + 1) * CN]
                    act.wait_ge(*at("mix log", f"{n}"))
                    done(A(cols, cols, ACT.Exp), "mix ready", f"{n}")
                elif kind == "scores":
                    exps(n)
                elif kind == "probs":
                    probs_out(n)
                elif kind == "pv":
                    pv_out(n)
            hi_to(groups["wo1_0"]["last"] + 1 * PART)
            for b in range(4):
                act.wait_ge(*at(f"bank{b} full", "mergedT"))
                done(A(hhi[:, 4 * (b // 2):4 * (b // 2) + 4, b % 2 * P:(b % 2 + 1) * P],
                       X[b].rearrange("p (c t) -> p c t", t=P), ACT.Copy), "merged hi", f"{b}")
            hi_to(groups["wo1_1"]["last"])
            norm("ffn1", "wo1_1", ohi, None, "norm_mix_2")
            ffn(1)

            act.dma_start(hgc[:, :], dram["hgrn"]).then_inc(sem("hgrn table in"), 16)
            def group_in(name):
                if name in ("sqk", "mq"):
                    heads_in(name, tok[0], tok[1], "x2", groups[name]["n"])
                    guess(name, slice(0, T * groups[name]["n"] // DH))
                    return
                for t in range(T):
                    a = sums(act, name, t)
                    if name == "hf":
                        scaled(tok[1][:, t, :], a[:, :], ACT.Copy, "x2", t)
                        ins = scaled(vh[:, t, :], a[:, :], ACT.Abs, "x2", t)
                    elif name == "hq":
                        scaled(tok[0][:, t, :], a[:, :], ACT.Copy, "x2", t)
                        ins = scaled(abs_q[:, t, :], a[:, :], ACT.Abs, "x2", t)
                    elif name == "hg":
                        scaled(tok[0][:, t, :], a[:, :], ACT.Copy, "x2", t)
                        ins = scaled(tok[1][:, t, :], a[:, :], ACT.Abs, "x2", t)
                    elif name == "iqb":
                        scaled(itok[:, t, 256:512], a[:, 0:256], ACT.Copy, "x2", t)
                        scaled(ikk[:, t, 0:DH], a[:, 256:320], ACT.Copy, "x2", t)
                        scaled(ikk[:, t, DH:P], a[:, 256:320], ACT.Copy, "x2", t)
                        ins = scaled(iw[:, t, :], a[:, 320:328], ACT.Copy, "x2", t)
                    elif name == "sviq":
                        scaled(sv[:, t, :], a[:, 0:256], ACT.Copy, "x2", t)
                        ins = scaled(itok[:, t, 0:256], a[:, 256:512], ACT.Copy, "x2", t)
                    else:
                        if t == 0:
                            act.wait_ge(*at("log f", "0"))
                        ins = scaled(vh[:, t, :], a[:, :], ACT.Copy, "x2", t)
                    leave(ins, name, t)
                if name in ("hf", "hq", "hg"):
                    log_one_plus(name, {"hf": vh, "hq": abs_q, "hg": tok[1]}[name])

            def exp_in(n):
                buf = {"k": tok[1], "q": abs_q, "g": tok[1]}[n]
                act.wait_ge(*at("hgrn arg", n))
                done(A(buf[:, :, :], buf[:, :, :], ACT.Exp), "hgrn k" if n == "k" else "sigmoid", "0" if n == "k" else n)

            def decays(u):
                if u > 0:
                    act.wait_ge(*at("q decayed", f"{u - 1}"))
                    act.wait_ge(*at("k decayed", f"{u - 1}"))
                for b in range(2):
                    act.wait_ge(*at(f"bank{b} full", f"decay {u}"))
                    done(A(dec[:, 4 * b:4 * b + 4, :], X[b].rearrange("p (c t) -> p c t", t=P), ACT.Exp),
                         f"bank{b} free", f"decay {u}")

            group_in("hf")
            for kind, n, *rest in MIX2:
                if kind == "gemm":
                    hi_to(part_end(n, *rest) + 3 * PART)
                elif kind == "sums":
                    group_in(n)
                elif kind == "exp":
                    exp_in(n)
                elif kind == "turn":
                    turned(TURN2[n][2], n, TURN2[n][1])
                    if n == "iq":
                        act.wait_ge(*at("bank2 full", "ikT"))
                        done(A(ikT[:, :], X[2][:, 0:S], ACT.Copy), "bank2 free", "ikT")
                elif kind == "index":
                    act.wait_ge(*at(f"bank{n % 2} full", f"index {n}"))
                    if n >= 2:
                        act.wait_ge(*at("index summed", f"{n - 2}"))
                    done(A(rel[n % 2], X[n % 2][:, 0:384], ACT.Relu, scale=IDX_SCALE), f"bank{n % 2} free", f"index {n}")
                elif kind == "decay":
                    decays(n)
                elif kind == "pairs" and n % 2 == 1:
                    h = n // 2
                    act.wait_ge(*at("bank0 full", f"cross {h}"))
                    if h:
                        act.wait_ge(*at("bank1 full", f"hout {h - 1}"))
                    done(A(AT[:, 2, :], X[0][:, 0:P], ACT.Copy), "bank0 free", f"cross {h}")
                elif kind == "scores":
                    exps(n)
                elif kind == "probs":
                    probs_out(n)
                elif kind == "pv":
                    pv_out(n)
                elif kind == "hgrn norm" and n == 0:
                    act.wait_ge(*at("bank1 free", "hout 3"))
                    act.wait_ge(*at("weights summed", "7"))
                    done(A(abs_q[:, :, :], xn[:, :, 0:512], ACT.Square), "hgrn squares", "0")
                    guess("hgrn", slice(0, T * 4))
                elif kind == "out":
                    b = OUT_BANK[n]
                    act.wait_ge(*at(f"bank{b} full", f"out {n}T"))
                    done(A(ohi[:, n:n + 2, :], X[b].rearrange("p (c t) -> p c t", t=S), ACT.Copy), "out2 hi", f"{n}")
            hi_to(groups["wo2_1"]["last"] + 2 * PART - 1)
            norm("ffn2", "wo2_1", hhi, None, None)
            ffn(2)

        @block.vector
        def _(dve):
            V = nc.vector
            nxt = [0]

            def lo_one(n, i=0):
                c = chunks[n]
                dve.wait_ge(sem("hi ready"), n + 1 + PER * i)
                V.tensor_tensor(wlo[:, n % SPLIT, 0:c["nk"], 0:c["n"]], raw[:, n % RAW, 0:c["nk"], 0:c["n"]],
                                whi[:, n % SPLIT, 0:c["nk"], 0:c["n"]].bitcast(F32), ALU.subtract)\
                    .then_inc(sem("lo ready"), 1)

            def lo_to(n):
                while nxt[0] <= min(n, len(chunks) - 1):
                    lo_one(nxt[0])
                    nxt[0] += 1

            def root(step, cols):
                dve.wait_ge(*at("guess", step))
                done(V.tensor_tensor(nt[:, cols], rs[:, cols], rs[:, cols], ALU.mult), "newton", f"{step} a")
                dve.wait_ge(*at("newton", f"{step} a"))
                done(V.scalar_tensor_tensor(nt[:, cols], nt[:, cols], -0.5, ms[:, cols], ALU.mult, ALU.mult),
                     "newton", f"{step} b")
                dve.wait_ge(*at("newton", f"{step} b"))
                done(V.scalar_tensor_tensor(rs[:, cols], nt[:, cols], 1.5, rs[:, cols], ALU.add, ALU.mult),
                     "newton", f"{step} c")
                dve.wait_ge(*at("newton", f"{step} c"))

            def norm_gain(k, src, g, b, t, ready):
                for r in ready:
                    dve.wait_ge(*r)
                h = slice(b * CN, (b + 1) * CN)
                done(V.tensor_tensor(xn[:, t, h], src[:, t, h], g[:, h], ALU.mult), "tokens scaled", f"{k} {t} {b}")

            def norm_lo(k, hi, lo, b):
                for t in range(T):
                    n = 2 * t + b
                    dve.wait_ge(*at("feature hi", f"{k} {n}"))
                    h = (slice(None), slice(4 * b, 4 * b + 4), slice(t * P, (t + 1) * P))
                    done(V.tensor_tensor(lo[h], X[n].rearrange("p (c t) -> p c t", t=P), hi[h].bitcast(F32),
                                         ALU.subtract), f"bank{n} free", f"{k}T")

            def norm_root(k):
                for t in range(T):
                    dve.wait_ge(*at("squares", f"{k} {t}"))
                done(V.tensor_scalar(ms[:, rstd(k)], ss[:, rstd(k)], 1.0 / D, EPS, ALU.mult, ALU.add),
                     "mean square", k)
                root(k, rstd(k))

            def residual(name, k=None, gain_in=None):
                c = int(name[-1])
                for t in range(T):
                    a = sums(dve, name, t)
                    cols = x[:, t, c * CN:(c + 1) * CN]
                    leave(V.tensor_tensor(cols, a[:, :], cols, ALU.add), name, t)
                    if k:
                        norm_gain(k, x, gain, c, t, [gain_in, moved(name, t)])

            def norm(k, first, last, hi, lo, gain_in):
                lo_to(groups[first]["last"] + 2 * PART)
                residual(first, k, gain_in)
                norm_lo(k, hi, lo, 0)
                lo_to(groups[last]["last"] + 3 * PART)
                residual(last, k, gain_in)
                lo_to(groups[last]["last"] + 4 * PART)
                norm_lo(k, hi, lo, 1)
                norm_root(k)

            def head_norm(step, src, sqs, heads, gains, width=DH, rope=False, name=None):
                dve.wait_ge(*moved(name or step, 1))
                n = T * heads
                shape = [P, T, heads, width]
                view = src[:, :, 0:heads * width].rearrange("p t (h d) -> p t h d", d=width)
                done(V.tensor_reduce(ss[:, 0:n].rearrange("p (t h) -> p t h", t=T),
                                     sqs[:, :, 0:heads * width].rearrange("p t (h d) -> p t h d", d=width),
                                     AX.X, ALU.add), "head squares", step)
                dve.wait_ge(*at("head squares", step))
                done(V.tensor_scalar(ms[:, 0:n], ss[:, 0:n], 1.0 / width, EPS, ALU.mult, ALU.add), "mean square", step)
                root(step, slice(0, n))
                r = rs[:, 0:n].rearrange("p (t h) -> p t h", t=T).unsqueeze(3).to_broadcast(shape)
                done(V.tensor_tensor(view, view, r, ALU.mult), "heads scaled", step)
                dve.wait_ge(*at("heads scaled", step))
                if step == "mk":
                    dve.wait_ge(sem("small in"), 16 * 10)
                for n, (h0, h1, g) in enumerate(gains):
                    part = view[:, :, h0:h1, :]
                    b = g.unsqueeze(1).unsqueeze(1).to_broadcast([P, T, h1 - h0, width])
                    ins = V.tensor_tensor(part, part, b, ALU.mult)
                done(ins, "heads gained" if rope else "heads ready", step)

            def attn_max(j):
                whole, pr, b = head(j)[4], probs(j), j % 2
                dve.wait_ge(*at(f"bank{b} full", f"scores {j}"))
                if whole:
                    for t, c0 in ((1, 0), (0, S)):
                        ins = V.tensor_reduce(mx[:, j, t:t + 1], X[b][:, c0:c0 + S], AX.X, ALU.max)
                    done(ins, "row max", f"{j}")
                    dve.wait_ge(*at("row max", f"{j}"))
                else:
                    last = before(j, 2)
                    if last is not None and last >= 0:
                        dve.wait_ge(*at("bank2 full", f"probs {last}"))
                    mask = cst[:, C_CM:C_CM + 3 * P] if j < 16 else madd[:, :]
                    for t, c0, n in ((1, 0, S), (0, S, P)):
                        ins = V.tensor_tensor_reduce(out=pr[:, c0:c0 + n], in0=X[b][:, c0:c0 + n],
                                                     in1=mask[:, c0:c0 + n], scale=1.0, scalar=FLOOR, op0=ALU.add,
                                                     op1=ALU.max, accum_out=mx[:, j, t:t + 1])
                    done(ins, f"bank{b} free", f"scores {j}")
                    dve.wait_ge(*at(f"bank{b} free", f"scores {j}"))
                done(V.tensor_scalar(nm[:, j, :], mx[:, j, :], -DH ** -0.5, None, ALU.mult), "max ready", f"{j}")

            def divide(j):
                whole, pr = head(j)[4], probs(j)
                dve.wait_ge(*(at(f"bank{j % 2} free", f"scores {j}") if whole else at("exps ready", f"{j}")))
                done(V.reciprocal(rc[:, j, :], sm[:, j, :]), "sum inverted", f"{j}")
                dve.wait_ge(*at("sum inverted", f"{j}"))
                for t, c0, n in ((1, 0, S), (0, S, S if whole else P)):
                    ins = V.tensor_scalar(pr[:, c0:c0 + n], pr[:, c0:c0 + n], rc[:, j, t:t + 1], None, ALU.mult)
                done(ins, "probs ready", f"{j}")

            def pv_low(j):
                o, blk = slice(64 * (j % 2), 64 * (j % 2) + 64), block_of(j)
                dve.wait_ge(*at("out hi", f"{j}"))
                done(V.tensor_tensor(olo[o, blk, :], X[3][o, 0:S], ohi[o, blk, :].bitcast(F32), ALU.subtract),
                     "bank3 free", f"pv {j}")

            def ffn(m):
                first = groups[f"g{m}_0"]["first"]

                def conv(i=0, short=""):
                    for b in range(1 if short else 2):
                        dve.wait_ge(*at("gate in", f"{m}{short} {b}", i))
                        blk = FT - 2 if short else 4 * i + 2 * b
                        for lag in (1, 2):
                            for c in range(2):
                                step = f"{m}{short} {b} {c}"
                                if lag == 2:
                                    dve.wait_ge(*at("tap added", step, i))
                                ins = V.scalar_tensor_tensor(
                                    y[:, 2 * b + c, lag:S], X[b][:, c * S:(c + 1) * S - lag],
                                    vT[:, bass.ds(blk + c + (2 - lag) * FT, 1)], y[:, 2 * b + c, lag:S],
                                    ALU.mult, ALU.add)
                                if lag == 1:
                                    done(ins, "tap added", step, i)
                        done(ins, f"bank{b} free", f"g{m}{short}T", i)

                def finish(i=0, short=""):
                    n = 2 if short else 4
                    step = f"{m}{short}"
                    dve.wait_ge(*at("gate ln", step, i))
                    done(V.scalar_tensor_tensor(e[:, 0:n, :], y[:, 0:n, :], 0.0, lg[:, 0:n, :], ALU.min,
                                                ALU.subtract), "gate log", step, i)
                    dve.wait_ge(*at("gate log", step, i))
                    for b in range(n // 2):
                        dve.wait_ge(*at(f"bank{2 + b} full", f"u{m}{short}T", i))
                        done(V.tensor_tensor(y[:, 2 * b:2 * b + 2, :], y[:, 2 * b:2 * b + 2, :],
                                             X[2 + b].rearrange("p (c t) -> p c t", t=S), ALU.mult),
                             f"bank{2 + b} free", f"u{m}{short}T", i)
                    dve.wait_ge(*at(f"bank{1 + n // 2} free", f"u{m}{short}T", i))
                    dve.wait_ge(*at("gate sigmoid", step, i))
                    done(V.tensor_tensor(y[:, 0:n, :], y[:, 0:n, :], e[:, 0:n, :], ALU.mult), "act ready", step, i)
                    dve.wait_ge(*at("act hi", step, i))
                    blks = slice(FT - 2, FT) if short else bass.ds(4 * i, 4)
                    done(V.tensor_tensor(alo[:, blks, :], y[:, 0:n, :], ahi[:, blks, :].bitcast(F32), ALU.subtract),
                         "act split", step, i)

                lo_to(first + 2 * PART - 1)
                if m == 1:
                    conv(short="s")
                lo_to(first + 4 * PART - 1)
                finish(short="s")
                with dve.Fori(0, PAIRS) as i:
                    cnt.enter()
                    for n in range(PER, PER + 2 * PART):
                        lo_one(first + n, i)
                    if m == 1:
                        conv(i)
                    for n in range(PER + 2 * PART, 2 * PER):
                        lo_one(first + n, i)
                    finish(i)
                cnt.leave(PAIRS)
                nxt[0] = first + PER + PER * PAIRS
                if m == 1:
                    norm("x2", "d1_0", "d1_1", hhi, hlo, gain_at(3))
                else:
                    for c in range(2):
                        lo_to(groups[f"d2_{c}"]["last"] + 3 * PART)
                        residual(f"d2_{c}")

            def gain_at(n):
                return sem("gain in"), 16 * n

            for b in range(2):
                for t in range(T):
                    norm_gain("mem", memx, memg, b, t, [(sem("memory gain in"), 16), (sem(f"mem {t} in"), 16)])
            norm_lo("mem", ohi, olo, 0)
            norm_lo("mem", ohi, olo, 1)
            lo_to(2 * PART - 1)
            for b in range(2):
                for t in range(T):
                    norm_gain("x1", x, gain, b, t, [gain_at(1), (sem(f"x {t} in"), 16),
                                                    at(f"bank{2 * t + b} full", "memT")])
            norm_root("mem")
            norm_lo("x1", hhi, hlo, 0)
            lo_to(groups["mkv"]["last"] + 2 * PART)
            norm_lo("x1", hhi, hlo, 1)
            norm_root("x1")
            head_norm("mk", raw_of["mk"], sq, 4, [(0, 4, hgain[:, 7, :])], name="mkv")
            for kind, n, *rest in MIX1:
                if kind == "gemm":
                    lo_to(part_end(n, *rest) + 3 * PART)
                elif kind == "sums" and n in ("qa", "ka", "qb", "kb"):
                    g = hgain[:, 2 * (n[1] == "b") + (n[0] == "k"), :]
                    head_norm(n, raw_of[n], sq, 8, [(0, 8, g)], rope=n[1] == "a")
                elif kind == "sums" and n == "f":
                    for t in range(T):
                        a = sums(dve, n, t)
                        leave(V.scalar_tensor_tensor(lf[:, t, :], a[:, 0:8], rs[:, rstd("x1", t)], bf[:, :], ALU.mult,
                                                     ALU.add), n, t)
                    dve.wait_ge(*moved("f", 1))
                    done(V.tensor_scalar(lt[:, 0], lf[:, :, :], -1.0, None, ALU.mult), "forget neg", "0")
                    dve.wait_ge(*at("forget neg", "0"))
                    done(V.tensor_tensor(lt[:, 0], lt[:, 0], lf[:, :, :], ALU.min), "forget", "-|z|")
                    dve.wait_ge(*at("forget ln", "0"))
                    done(V.scalar_tensor_tensor(lf[:, :, :], lf[:, :, :], 0.0, lt[:, 1], ALU.min, ALU.subtract),
                         "log forget", "0")
                elif kind == "sums" and n[:4] == "gate":
                    g = int(n[4:])
                    for t in range(T):
                        a = sums(dve, n, t)
                        if g == 0 and t == 0:
                            dve.wait_ge(sem("gate bias in"), 32)
                        cols = gates[:, t, g * CN:(g + 1) * CN]
                        leave(V.scalar_tensor_tensor(cols, a[:, :], rs[:, rstd("x1", t)], cols, ALU.mult, ALU.add),
                              n, t)
                elif kind == "mix":
                    cols = gates[:, :, n * CN:(n + 1) * CN]
                    dve.wait_ge(*at("mix ln", f"{n}"))
                    done(V.scalar_tensor_tensor(cols, cols, 0.0, sq[:, :, :], ALU.min, ALU.subtract), "mix log", f"{n}")
                elif kind == "sums" and n[:3] == "bra":
                    c = int(n[3:])
                    dve.wait_ge(*at("mix ready", f"{c}"))
                    for t in range(T):
                        a = sums(dve, n, t)
                        leave(V.tensor_tensor(xn[:, t, c * CN:(c + 1) * CN], a[:, :], gates[:, t, c * CN:(c + 1) * CN],
                                              ALU.mult), n, t)
                elif kind == "scores":
                    attn_max(n)
                elif kind == "divide":
                    divide(n)
                elif kind == "pv":
                    pv_low(n)
            for c in range(2):
                lo_to(groups[f"brb{c}"]["last"] + 3 * PART)
                dve.wait_ge(*at("mix ready", f"{2 + c}"))
                for t in range(T):
                    a = sums(dve, f"brb{c}", t)
                    g = gates[:, t, D + c * CN:D + (c + 1) * CN]
                    leave(V.tensor_tensor(g, a[:, :], g, ALU.mult), f"brb{c}", t)
                    dve.wait_ge(*moved(f"brb{c}", t))
                    if c == 0 and t == 0:
                        dve.wait_ge(*moved("bra1", 1))
                    cols = xn[:, t, c * CN:(c + 1) * CN]
                    done(V.tensor_tensor(cols, cols, g, ALU.add), "merged", f"{c} {t}")
            for b in range(4):
                dve.wait_ge(*at("merged hi", f"{b}"))
                h = (slice(None), slice(4 * (b // 2), 4 * (b // 2) + 4), slice(b % 2 * P, (b % 2 + 1) * P))
                done(V.tensor_tensor(hlo[h], X[b].rearrange("p (c t) -> p c t", t=P), hhi[h].bitcast(F32),
                                     ALU.subtract), f"bank{b} free", "mergedT")
            norm("ffn1", "wo1_0", "wo1_1", ohi, olo, gain_at(2))
            ffn(1)

            halves = ((1, slice(0, S)), (0, slice(S, S + P)))

            def log_sigmoid(name):
                z, buf, dst, step = {"hf": (tok[1], vh, logf, ("log f", "0")), "hq": (tok[0], abs_q, abs_q, ("hgrn arg", "q")),
                                     "hg": (tok[0], tok[1], tok[1], ("hgrn arg", "g"))}[name]
                dve.wait_ge(*at("one plus ln", name))
                done(V.scalar_tensor_tensor(dst[:, :, :], z[:, :, :], 0.0, buf[:, :, :], ALU.min, ALU.subtract), *step)
                if name == "hf":
                    dve.wait_ge(*at("log f", "0"))
                    done(V.tensor_tensor(tok[1][:, :, :], logf[:, :, :], tok[1][:, :, :], ALU.subtract), "hgrn arg", "k")

            def index(h):
                dve.wait_ge(*at(f"bank{h % 2} free", f"index {h}"))
                for t, c in halves:
                    if h == 0:
                        ins = V.tensor_scalar(sco[:, c], rel[0][:, c], iw[:, t, h:h + 1], None, ALU.mult)
                    else:
                        if t == 1:
                            dve.wait_ge(*at("index summed", f"{h - 1}"))
                        ins = V.scalar_tensor_tensor(sco[:, c], rel[h % 2][:, c], iw[:, t, h:h + 1], sco[:, c],
                                                     ALU.mult, ALU.add)
                done(ins, "index summed", f"{h}")

            def best(r):
                for t, c in halves:
                    src = sco if r == 0 else work
                    if r:
                        dve.wait_ge(*at("struck out", f"{r - 1} {t}"))
                    done(V.max(mx8[:, t, :], src[:, c]), "eight found", f"{r} {t}")
                for t, c in halves:
                    src = sco if r == 0 else work
                    dve.wait_ge(*at("eight found", f"{r} {t}"))
                    done(V.match_replace(work[:, c], mx8[:, t, :], src[:, c], FLOOR), "struck out", f"{r} {t}")

            def chosen():
                for t, c in halves:
                    dve.wait_ge(*at("struck out", f"{TOPK // 8 - 1} {t}"))
                done(V.tensor_scalar(madd[:, :], work, -2e38, BIG, ALU.is_lt, ALU.mult), "chosen", "0")
                dve.wait_ge(*at("chosen", "0"))
                done(V.scalar_tensor_tensor(madd[:, :], madd[:, :], -BIG, cst[:, C_CM:C_CM + 3 * P], ALU.add,
                                            ALU.add), "chosen", "1")
                dve.wait_ge(*at("chosen", "1"))

            def q_decayed(u):
                h, t = u // 2, u % 2
                dve.wait_ge(*at("bank1 free", f"decay {u}"))
                if u:
                    dve.wait_ge(*at("bank3 full", f"pairs {u - 1}"))
                q = hqT[:, h, t * P:(t + 1) * P]
                ins = V.tensor_tensor(qd[:, :, :], dec[:, 1 - t:8 - t, :],
                                      q.unsqueeze(1).to_broadcast([P, LEVELS, P]), ALU.mult)
                if t == 1:
                    if h:
                        dve.wait_ge(*at("bank0 full", f"cross {h - 1}"))
                    ins = V.tensor_tensor(qx[:, :], dec[:, 7, :], q, ALU.mult)
                done(ins, "q decayed", f"{u}")

            def weights(u):
                h, t = u // 2, u % 2
                dve.wait_ge(*(at("weights summed", f"{u - 1}") if u else at("hgrn q", "0")))
                for b in range(2):
                    dve.wait_ge(*at(f"bank{2 + b} full", f"pairs {u}"))
                    done(V.tensor_tensor(masked[:, 4 * b:4 * b + 4, :], X[2 + b].rearrange("p (l s) -> p l s", s=P),
                                         hgc[:, C_HM + b * 512:C_HM + (b + 1) * 512].rearrange("p (l s) -> p l s", s=P),
                                         ALU.mult), f"bank{2 + b} free", f"pairs {u}")
                dve.wait_ge(*at("bank3 free", f"pairs {u}"))
                if h:
                    dve.wait_ge(*at("bank1 full", f"hout {h - 1}"))
                done(V.tensor_reduce(AT[:, t, :], masked.rearrange("p l s -> p s l"), AX.X, ALU.add),
                     "weights summed", f"{u}")

            def hgrn_norm(n):
                view = xn[:, :, 0:512].rearrange("p t (h d) -> p t h d", d=P)
                if n == 0:
                    dve.wait_ge(*at("hgrn squares", "0"))
                    done(V.tensor_reduce(ss[:, 0:8].rearrange("p (t h) -> p t h", t=T),
                                         abs_q.rearrange("p t (h d) -> p t h d", d=P), AX.X, ALU.add),
                         "head squares", "hgrn")
                    dve.wait_ge(*at("head squares", "hgrn"))
                    done(V.tensor_scalar(ms[:, 0:8], ss[:, 0:8], 1.0 / P, EPS, ALU.mult, ALU.add), "mean square", "hgrn")
                else:
                    root("hgrn", slice(0, 8))
                    r = rs[:, 0:8].rearrange("p (t h) -> p t h", t=T).unsqueeze(3).to_broadcast([P, T, 4, P])
                    done(V.tensor_tensor(view, view, r, ALU.mult), "heads scaled", "hgrn")
                    dve.wait_ge(*at("heads scaled", "hgrn"))
                    done(V.tensor_tensor(xn[:, :, 0:512], xn[:, :, 0:512], tok[0][:, :, :], ALU.mult),
                         "hgrn normed", "0")

            log_sigmoid("hf")
            for kind, n, *rest in MIX2:
                if kind == "gemm":
                    lo_to(min(part_end(n, *rest) + 3 * PART, MIX2_LOW[0] - 1))
                elif kind == "log":
                    log_sigmoid("hg")
                elif kind == "sums":
                    if n == "hq":
                        log_sigmoid(n)
                    elif n == "sqk":
                        head_norm("sqk", tok[0], tok[1], 8, [(0, 4, hgain[:, 4, :]), (4, 8, hgain[:, 5, :])])
                    elif n == "mq":
                        head_norm("mq", tok[0], tok[1], 4, [(0, 4, hgain[:, 6, :])])
                elif kind == "exp" and n == "q":
                    dve.wait_ge(*at("sigmoid", "q"))
                    done(V.tensor_tensor(tok[0][:, :, :], tok[0][:, :, :], abs_q[:, :, :], ALU.mult), "hgrn q", "0")
                elif kind == "exp" and n == "g":
                    dve.wait_ge(*at("sigmoid", "g"))
                    done(V.tensor_tensor(tok[0][:, :, :], tok[0][:, :, :], tok[1][:, :, :], ALU.mult), "hgrn gate", "0")
                    dve.wait_ge(*at("hgrn gate", "0"))
                    view = tok[0].rearrange("p t (h d) -> p t h d", d=P)
                    done(V.tensor_tensor(view, view, og[:, :].unsqueeze(1).unsqueeze(1).to_broadcast([P, T, 4, P]),
                                         ALU.mult), "hgrn gate", "1")
                    dve.wait_ge(*at("hgrn gate", "1"))
                elif kind == "index":
                    index(n)
                elif kind == "masked":
                    dve.wait_ge(*at("index summed", "7"))
                    done(V.tensor_tensor(sco, sco, cst[:, C_CM:C_CM + 3 * P], ALU.add), "index masked", "0")
                    dve.wait_ge(*at("index masked", "0"))
                elif kind == "best":
                    best(n)
                elif kind == "chosen":
                    chosen()
                elif kind == "decay":
                    q_decayed(n)
                elif kind == "pairs":
                    weights(n)
                elif kind == "hout":
                    dve.wait_ge(*at("bank1 full", f"hout {n}"))
                    done(V.tensor_copy(xn[:, :, n * P:(n + 1) * P], X[1][:, 0:2 * P].rearrange("p (t d) -> p t d", d=P)),
                         "bank1 free", f"hout {n}")
                elif kind == "scores":
                    attn_max(n)
                elif kind == "divide":
                    divide(n)
                elif kind == "pv":
                    pv_low(n)
                elif kind == "hgrn norm":
                    hgrn_norm(n)
                elif kind == "out":
                    dve.wait_ge(*at("out2 hi", f"{n}"))
                    h = (slice(None), slice(n, n + 2), slice(None))
                    b = OUT_BANK[n]
                    done(V.tensor_tensor(olo[h], X[b].rearrange("p (c t) -> p c t", t=S), ohi[h].bitcast(F32),
                                         ALU.subtract), f"bank{b} free", f"out {n}T")
            nxt[0] = MIX2_LOW[1]
            dve.wait_ge(sem("lo ready"), nxt[0])
            norm("ffn2", "wo2_0", "wo2_1", hhi, hlo, gain_at(4))
            ffn(2)

        @block.gpsimd
        def _(pool):
            G = nc.gpsimd

            def rope(name):
                pool.wait_ge(*at("heads gained", name))
                if name == "ka":
                    pool.wait_ge(*at("heads roped", "qa"))
                v = raw_of[name].rearrange("p t (h d) -> p t h d", d=DH)
                x1, x2 = v[:, :, :, 0:8], v[:, :, :, 8:16]
                cs = cst[:, C_CS:C_CS + 16 * T].rearrange("p (t a d) -> p t a d", t=T, a=2)
                cos = cs[:, :, 0, :].unsqueeze(2).to_broadcast([P, T, 8, 8])
                sin = cs[:, :, 1, :].unsqueeze(2).to_broadcast([P, T, 8, 8])
                for n, (a, b) in enumerate(((x1, cos), (x2, sin), (x2, cos), (x1, sin))):
                    ins = G.tensor_tensor(rp[:, n], a, b, ALU.mult)
                done(ins, "rope products", name)
                pool.wait_ge(*at("rope products", name))
                G.tensor_tensor(x1, rp[:, 0], rp[:, 1], ALU.subtract)
                done(G.tensor_tensor(x2, rp[:, 2], rp[:, 3], ALU.add), "heads roped", name)

            pool.wait_ge(sem("consts in"), 16)
            rope("qa")
            rope("ka")
            low = MIX2_LOW[0]
            for kind, n, *rest in MIX2:
                if kind == "gemm" and part_end(n, *rest) + 3 * PART >= low:
                    for low in range(low, part_end(n, *rest) + 3 * PART + 1):
                        c = chunks[low]
                        if low == MIX2_LOW[0]:
                            pool.wait_ge(sem("lo ready"), low)
                        pool.wait_ge(sem("hi ready"), low + 1)
                        G.tensor_tensor(wlo[:, low % SPLIT, 0:c["nk"], 0:c["n"]], raw[:, low % RAW, 0:c["nk"], 0:c["n"]],
                                        whi[:, low % SPLIT, 0:c["nk"], 0:c["n"]].bitcast(F32), ALU.subtract)\
                            .then_inc(sem("lo ready"), 1)
                    low = part_end(n, *rest) + 3 * PART + 1
                elif kind == "decay":
                    u = n
                    h, t = u // 2, u % 2
                    pool.wait_ge(*at("bank1 free", f"decay {u}"))
                    if u:
                        pool.wait_ge(*at("bank3 full", f"pairs {u - 1}"))
                    k = hkT[:, h, t * P:(t + 1) * P]
                    ins = G.tensor_tensor(kd[:, :, :], dec[:, 1 - t:8 - t, :],
                                          k.unsqueeze(1).to_broadcast([P, LEVELS, P]), ALU.mult)
                    if t == 0:
                        if h:
                            pool.wait_ge(*at("bank0 full", f"cross {h - 1}"))
                        ins = G.tensor_tensor(kx[:, :], dec[:, 0, :], k, ALU.mult)
                    done(ins, "k decayed", f"{u}")

    return cnt.seen


SHAPES = {
    "x": (1, S, D), "attn_norm_g": (1, D), "w_in": (1, D, 5128), "b_forget": (1, 8), "b_gate": (1, 2, D),
    "moba_q_norm_g": (1, DH), "moba_k_norm_g": (1, DH), "fox_q_norm_g": (1, DH), "fox_k_norm_g": (1, DH),
    "w_branch_moba": (1, 512, D), "w_branch_fox": (1, 512, D), "w_out": (1, D, D), "ffn_norm_g": (1, D),
    "w_ffn_up": (1, D, 2 * DFF), "ffn_conv_w": (1, 3, DFF), "ffn_conv_b": (1, DFF), "w_ffn_down": (1, DFF, D),
    "mem_2": (1, S, D), "w_in_2": (1, D, 3656), "w_out_2": (1, D, D), "w_mem_kv_2": (1, D, 512),
    "norm_mix_2": (1, D), "norm_mem_2": (1, D), "norm_ffn_2": (1, D), "hg_out_gain_2": (1, P),
    "sa_q_gain_2": (1, DH), "sa_k_gain_2": (1, DH), "mem_q_gain_2": (1, DH), "mem_k_gain_2": (1, DH),
    "w_ffn_in_2": (1, D, 2 * DFF), "w_ffn_out_2": (1, DFF, D), "consts": (P, C_END), "hgrn": (P, C_HEND), "pick": (8, 8, P),
}


def build(nc, known):
    dram = {n: nc.dram_tensor(f"in_{n}", s, F32, kind="ExternalInput").ap() for n, s in SHAPES.items()}
    out = nc.dram_tensor("out", (1, S, D), F32, kind="ExternalOutput").ap()
    return program(nc, dram, out, known)


def kernel(**inputs):
    import concourse.bacc as bacc
    from concourse.bass_utils import run_bass_kernel_spmd

    def core():
        return bacc.Bacc("TRN2", target_bir_lowering=False, num_devices=1)

    known = build(core(), {})
    nc = core()
    assert build(nc, known) == known
    arrays = {f"in_{n}": np.ascontiguousarray(inputs[n]) for n in SHAPES if n in inputs}
    arrays["in_consts"], arrays["in_hgrn"], arrays["in_pick"] = constants()
    r = run_bass_kernel_spmd(nc, [arrays], core_ids=[0])
    return r.results[0]["out"]
```
